# Optimizing a Trainium2 kernel written in Bass

```python
import math
import jax, jax.numpy as jnp
from jax import lax
import numpy as np

D_MODEL = 1024
BATCH = 1
SEQ = 256
DEPTH = 2

CHUNK = 64
N_MEM = 256
N_A_LAYERS = DEPTH // 2
N_B_LAYERS = DEPTH - N_A_LAYERS
EPS = 1e-6
NEG_INF = -1e30

GLA_HEADS = 4
GLA_DK = D_MODEL // 2 // GLA_HEADS
GLA_DV = D_MODEL // GLA_HEADS
GLA_GATE_RANK = 16
GLA_GATE_TAU = 16.0
GLA_KEY_WIDTH = GLA_HEADS * GLA_DK
GLA_VAL_WIDTH = GLA_HEADS * GLA_DV

SWA_Q_HEADS = 16
SWA_KV_HEADS = 2
SWA_HEAD_DIM = 64
SWA_Q_WIDTH = SWA_Q_HEADS * SWA_HEAD_DIM
KV_WIDTH = 2 * SWA_KV_HEADS * SWA_HEAD_DIM
WINDOW = 128
WINDOW_CHUNKS = WINDOW // CHUNK
ROPE_THETA = 10000.0

MEM_HEADS = 4
MEM_HEAD_DIM = 128
MEM_WIDTH = MEM_HEADS * MEM_HEAD_DIM

D_FF = 2816
FFN_RES_WEIGHT = 0.5

A_SPLITS = (GLA_KEY_WIDTH, 2 * GLA_KEY_WIDTH, 2 * GLA_KEY_WIDTH + GLA_VAL_WIDTH, 2 * GLA_KEY_WIDTH + 2 * GLA_VAL_WIDTH, 2 * GLA_KEY_WIDTH + 2 * GLA_VAL_WIDTH + GLA_GATE_RANK)
A_IN_WIDTH = A_SPLITS[-1] + MEM_WIDTH
A_OUT_WIDTH = GLA_VAL_WIDTH + MEM_WIDTH
B_IN_WIDTH = SWA_Q_WIDTH + MEM_WIDTH
B_OUT_WIDTH = SWA_Q_WIDTH + MEM_WIDTH
MAX_STREAM_OFFSET_CHUNKS = 64

kernel_name = 'hybrid_yoco_gla_swa_sink_macaron'

def rms_norm(x, g):
    xf = x.astype(jnp.float32)
    y = xf * lax.rsqrt(jnp.mean(xf * xf, axis=-1, keepdims=True) + EPS)
    return (y * g.astype(jnp.float32)).astype(x.dtype)

def swiglu_ffn(h, w_in, w_out):
    a, u = jnp.split(h @ w_in, 2, axis=-1)
    return (jax.nn.silu(a) * u) @ w_out

def apply_rope(t, positions):
    dh = t.shape[-1]
    half = dh // 2
    inv_freq = jnp.power(ROPE_THETA, -jnp.arange(half, dtype=jnp.float32) * (2.0 / dh))
    ang = positions.astype(jnp.float32)[..., None] * inv_freq
    cos = jnp.cos(ang)[:, :, None, :]
    sin = jnp.sin(ang)[:, :, None, :]
    tf = t.astype(jnp.float32)
    t1, t2 = tf[..., :half], tf[..., half:]
    out = jnp.concatenate([t1 * cos - t2 * sin, t2 * cos + t1 * sin], axis=-1)
    return out.astype(t.dtype)

def memory_attention(q_mem, mem_k, mem_v):
    s = jnp.einsum('bshd,bmhd->bhsm', q_mem, mem_k, preferred_element_type=jnp.float32) * (MEM_HEAD_DIM ** -0.5)
    p = jax.nn.softmax(s, axis=-1).astype(mem_v.dtype)
    o = jnp.einsum('bhsm,bmhd->bshd', p, mem_v)
    return o.reshape(o.shape[0], o.shape[1], MEM_WIDTH)

def gla_chunked(q, k, v, log_g):
    b, s, h, dk = q.shape
    dv = v.shape[-1]
    n = s // CHUNK

    def to_chunks(t):
        return t.astype(jnp.float32).reshape(b, n, CHUNK, h, t.shape[-1]).transpose(0, 3, 1, 2, 4)

    qc = to_chunks(q) * (dk ** -0.5)
    kc = to_chunks(k)
    vc = to_chunks(v)
    cum = jnp.cumsum(to_chunks(log_g), axis=-2)
    total = cum[..., -1:, :]
    mid = 0.5 * total
    up = jnp.exp(cum - mid)
    down = jnp.exp(mid - cum)
    a_past = jnp.einsum('bhnid,bhnjd->bhnij', qc * up, kc * down)
    a_fut = jnp.einsum('bhnid,bhnjd->bhnij', qc * down, kc * up)
    idx = jnp.arange(CHUNK)
    a = jnp.where(idx[:, None] >= idx[None, :], a_past, a_fut)
    o_intra = jnp.einsum('bhnij,bhnjv->bhniv', a, vc)

    q_inter = qc * jnp.exp(cum)
    k_state = kc * jnp.exp(total - cum)
    chunk_kv = jnp.einsum('bhnjd,bhnjv->bhndv', k_state, vc)
    chunk_decay = jnp.exp(total[..., 0, :])

    def step(state, inp):
        decay, kv = inp
        return decay[..., None] * state + kv, state

    init = jnp.zeros((b, h, dk, dv), jnp.float32)
    _, prior = lax.scan(step, init, (jnp.moveaxis(chunk_decay, 2, 0), jnp.moveaxis(chunk_kv, 2, 0)))
    prior = jnp.moveaxis(prior, 0, 2)
    o = o_intra + jnp.einsum('bhnid,bhndv->bhniv', q_inter, prior)
    return o.transpose(0, 2, 3, 1, 4).reshape(b, s, h, dv).astype(v.dtype)

def swa_sink_attention(q, k, v, sinks):
    b, s, hq, dh = q.shape
    n = s // CHUNK
    grp = hq // SWA_KV_HEADS
    qb = q.reshape(b, n, CHUNK, SWA_KV_HEADS, grp, dh)
    kb = k.reshape(b, n, CHUNK, SWA_KV_HEADS, dh)
    vb = v.reshape(b, n, CHUNK, SWA_KV_HEADS, dh)

    def band(t):
        parts = [jnp.pad(t, ((0, 0), (w, 0), (0, 0), (0, 0), (0, 0)))[:, :n] for w in range(WINDOW_CHUNKS - 1, -1, -1)]
        return jnp.concatenate(parts, axis=2)

    kband = band(kb)
    vband = band(vb)
    key_lag = jnp.repeat(jnp.arange(WINDOW_CHUNKS - 1, -1, -1), CHUNK)
    valid = jnp.arange(n)[:, None] >= key_lag[None, :]
    scores = jnp.einsum('bnqhgd,bnkhd->bhgnqk', qb, kband, preferred_element_type=jnp.float32) * (dh ** -0.5)
    scores = jnp.where(valid[:, None, :], scores, NEG_INF)
    sink = sinks.astype(jnp.float32).reshape(SWA_KV_HEADS, grp)[None, :, :, None, None, None]
    m = jnp.maximum(jnp.max(scores, axis=-1, keepdims=True), sink)
    p = jnp.exp(scores - m)
    probs = p / (jnp.sum(p, axis=-1, keepdims=True) + jnp.exp(sink - m))
    o = jnp.einsum('bhgnqk,bnkhd->bnqhgd', probs.astype(v.dtype), vband)
    return o.reshape(b, s, hq * dh)

def gla_layer(h, mem_k, mem_v, w_in, w_gate_up, b_gate, norm_g, w_out):
    b, s, _ = h.shape
    q, k, v, r, g_lr, q_mem = jnp.split(h @ w_in, A_SPLITS, axis=-1)
    log_gate = jax.nn.log_sigmoid((g_lr @ w_gate_up + b_gate).astype(jnp.float32)) / GLA_GATE_TAU
    o = gla_chunked(q.reshape(b, s, GLA_HEADS, GLA_DK), k.reshape(b, s, GLA_HEADS, GLA_DK),
                    v.reshape(b, s, GLA_HEADS, GLA_DV), log_gate.reshape(b, s, GLA_HEADS, GLA_DK))
    o = rms_norm(o, norm_g).reshape(b, s, GLA_VAL_WIDTH) * jax.nn.silu(r)
    mo = memory_attention(q_mem.reshape(b, s, MEM_HEADS, MEM_HEAD_DIM), mem_k, mem_v)
    return jnp.concatenate([o, mo], axis=-1) @ w_out

def swa_layer(h, positions, shared_k, shared_v, mem_k, mem_v, w_in, sinks, w_out):
    b, s, _ = h.shape
    q, q_mem = jnp.split(h @ w_in, [SWA_Q_WIDTH], axis=-1)
    q = apply_rope(q.reshape(b, s, SWA_Q_HEADS, SWA_HEAD_DIM), positions)
    o = swa_sink_attention(q, shared_k, shared_v, sinks)
    mo = memory_attention(q_mem.reshape(b, s, MEM_HEADS, MEM_HEAD_DIM), mem_k, mem_v)
    return jnp.concatenate([o, mo], axis=-1) @ w_out

def setup_inputs(seed: int = 0) -> dict:
    key = jax.random.key(seed)
    ks = jax.random.split(key, 18)

    def normal(k, shape, scale):
        return jax.random.normal(k, shape, jnp.float32) * scale

    x = normal(ks[0], (BATCH, SEQ, D_MODEL), 1.0)
    mem = normal(ks[1], (BATCH, N_MEM, D_MODEL), 1.0)
    offsets = jax.random.randint(ks[2], (BATCH, 1), 0, MAX_STREAM_OFFSET_CHUNKS, dtype=jnp.int32) * CHUNK
    positions = (offsets + jnp.arange(SEQ, dtype=jnp.int32)[None, :]).astype(jnp.int32)
    norm_g = 1.0 + normal(ks[3], (DEPTH, 6, D_MODEL), 0.05)
    w_ffn_in = normal(ks[4], (DEPTH, 2, D_MODEL, 2 * D_FF), D_MODEL ** -0.5)
    w_ffn_out = normal(ks[5], (DEPTH, 2, D_FF, D_MODEL), D_FF ** -0.5)
    mem_norm_g = 1.0 + normal(ks[6], (DEPTH, D_MODEL), 0.05)
    w_mem_kv = normal(ks[7], (DEPTH, D_MODEL, 2 * MEM_WIDTH), D_MODEL ** -0.5)
    w_in_a = normal(ks[8], (N_A_LAYERS, D_MODEL, A_IN_WIDTH), D_MODEL ** -0.5)
    w_gate_up = normal(ks[9], (N_A_LAYERS, GLA_GATE_RANK, GLA_KEY_WIDTH), GLA_GATE_RANK ** -0.5)
    b_gate = normal(ks[10], (N_A_LAYERS, GLA_KEY_WIDTH), 0.02)
    gla_norm_g = 1.0 + normal(ks[11], (N_A_LAYERS, GLA_DV), 0.05)
    w_out_a = normal(ks[12], (N_A_LAYERS, A_OUT_WIDTH, D_MODEL), A_OUT_WIDTH ** -0.5)
    kv_norm_g = 1.0 + normal(ks[13], (D_MODEL,), 0.05)
    w_kv = normal(ks[14], (D_MODEL, KV_WIDTH), D_MODEL ** -0.5)
    w_in_b = normal(ks[15], (N_B_LAYERS, D_MODEL, B_IN_WIDTH), D_MODEL ** -0.5)
    sinks = normal(ks[16], (N_B_LAYERS, SWA_Q_HEADS), 0.5)
    w_out_b = normal(ks[17], (N_B_LAYERS, B_OUT_WIDTH, D_MODEL), B_OUT_WIDTH ** -0.5)
    return {'x': x, 'mem': mem, 'positions': positions, 'norm_g': norm_g,
            'w_ffn_in': w_ffn_in, 'w_ffn_out': w_ffn_out, 'mem_norm_g': mem_norm_g, 'w_mem_kv': w_mem_kv,
            'w_in_a': w_in_a, 'w_gate_up': w_gate_up, 'b_gate': b_gate, 'gla_norm_g': gla_norm_g, 'w_out_a': w_out_a,
            'kv_norm_g': kv_norm_g, 'w_kv': w_kv, 'w_in_b': w_in_b, 'sinks': sinks, 'w_out_b': w_out_b}

def reference(x, mem, positions, norm_g, w_ffn_in, w_ffn_out, mem_norm_g, w_mem_kv,
              w_in_a, w_gate_up, b_gate, gla_norm_g, w_out_a,
              kv_norm_g, w_kv, w_in_b, sinks, w_out_b):
    b, s, _ = x.shape
    n_mem = mem.shape[1]
    shared_k = None
    shared_v = None
    for layer in range(DEPTH):
        g = norm_g[layer]
        hf = swiglu_ffn(rms_norm(x, g[0]), w_ffn_in[layer, 0], w_ffn_out[layer, 0])
        x = x + FFN_RES_WEIGHT * rms_norm(hf, g[1])
        h = rms_norm(x, g[2])
        mem_k, mem_v = jnp.split(rms_norm(mem, mem_norm_g[layer]) @ w_mem_kv[layer], 2, axis=-1)
        mem_k = mem_k.reshape(b, n_mem, MEM_HEADS, MEM_HEAD_DIM)
        mem_v = mem_v.reshape(b, n_mem, MEM_HEADS, MEM_HEAD_DIM)
        if layer < N_A_LAYERS:
            mix = gla_layer(h, mem_k, mem_v, w_in_a[layer], w_gate_up[layer], b_gate[layer],
                            gla_norm_g[layer], w_out_a[layer])
        else:
            j = layer - N_A_LAYERS
            mix = swa_layer(h, positions, shared_k, shared_v, mem_k, mem_v, w_in_b[j], sinks[j], w_out_b[j])
        x = x + rms_norm(mix, g[3])
        hf = swiglu_ffn(rms_norm(x, g[4]), w_ffn_in[layer, 1], w_ffn_out[layer, 1])
        x = x + FFN_RES_WEIGHT * rms_norm(hf, g[5])
        if layer == N_A_LAYERS - 1:
            k_s, v_s = jnp.split(rms_norm(x, kv_norm_g) @ w_kv, 2, axis=-1)
            shared_k = apply_rope(k_s.reshape(b, s, SWA_KV_HEADS, SWA_HEAD_DIM), positions)
            shared_v = v_s.reshape(b, s, SWA_KV_HEADS, SWA_HEAD_DIM)
    return x


_drawn_inputs = setup_inputs


def setup_inputs(seed=0):
    import zlib

    import numpy as np

    out = dict(_drawn_inputs(seed))
    spreads = {}
    factors = {'mem_norm_g': 2.808, 'b_gate': 7.893, 'sinks': 64.0, 'kv_norm_g': 7.831}
    for name, (base, spread) in spreads.items():
        noise = np.random.default_rng([zlib.crc32(name.encode()), seed]).standard_normal(out[name].shape)
        drawn = base * np.exp(spread * noise) if base else spread * noise
        out[name] = __import__('jax').numpy.asarray(drawn.astype(out[name].dtype))
    for name, factor in factors.items():
        out[name] = (out[name] * factor).astype(out[name].dtype)
    return out
```

```python
from contextlib import ExitStack

import numpy as np

import concourse.bass as bass
from concourse import mybir

F32 = mybir.dt.float32
F32R = mybir.dt.float32r
I32 = mybir.dt.int32
ALU = mybir.AluOpType
ACT = mybir.ActivationFunctionType
AX = mybir.AxisListType

P = 128
EPS = 1e-6
NEG_INF = -1e30
ROPE_THETA = 10000.0
TAU = 16.0
CHUNK = 64
RSQRT_MAGIC = 0x5F3759DF
TWO_PI = 2.0 * np.pi
PI_BELOW = 3.1415925


def parts_of(value, bits, count):
    parts = []
    for _ in range(count):
        exponent = int(np.floor(np.log2(abs(value))))
        step = 2.0 ** (exponent - bits + 1)
        part = float(np.floor(value / step) * step)
        parts.append(part)
        value -= part
    return parts


def hybrid_kernel(nc, x, mem, positions, norm_g, w_ffn_in, w_ffn_out, mem_norm_g, w_mem_kv,
                  w_in_a, w_gate_up, b_gate, gla_norm_g, w_out_a, kv_norm_g, w_kv, w_in_b, sinks, w_out_b, out):
    _, S, D = x.shape
    F = w_ffn_out.shape[2]
    T = S // P
    K = D // P
    FC = 256
    NCH = F // FC
    GH, DK, DV = 4, D // 8, D // 4
    KW, VW = GH * DK, GH * DV
    RANK = w_gate_up.shape[1]
    MH_, MD = 4, 128
    MW = MH_ * MD
    HQ, HD = 16, 64
    COL_K, COL_V, COL_R = KW, 2 * KW, 2 * KW + VW
    COL_G = COL_R + VW
    COL_QM = COL_G + RANK
    UNIT = 2048
    inv_freq = np.power(np.float32(ROPE_THETA),
                        -np.arange(HD // 2, dtype=np.float32) * np.float32(2.0 / HD)).astype(np.float32)
    assert T == 2 and K == 8 and F % FC == 0 and x.shape[0] == 1

    def cols(w, k0, nk, c0, n):
        return w.rearrange("(k p) n -> p k n", p=P)[:, k0:k0 + nk, c0:c0 + n]

    def halves(name, w, c0):
        return [((name, i), cols(w, 4 * i, 4, c0, 512)) for i in range(2)]

    def rows(name, w, tiles):
        return [((name, k), cols(w, k, 2, 0, D)) for k in tiles]

    wa, woa, wb, wob = w_in_a[0], w_out_a[0], w_in_b[0], w_out_b[0]
    OT_A, OT_B = VW // P, HQ * HD // P
    SEG_A = (halves("mk0", w_mem_kv[0], 0) + halves("mv0", w_mem_kv[0], MW)
             + [(("ga", 0), cols(wa, 0, K, COL_G, P))]
             + halves("ka", wa, COL_K) + halves("qa", wa, 0) + halves("qma", wa, COL_QM)
             + halves("va0", wa, COL_V) + halves("va1", wa, COL_V + 512)
             + halves("ra0", wa, COL_R) + halves("ra1", wa, COL_R + 512)
             + rows("oa", woa, range(OT_A, OT_A + 4, 2)) + rows("oa", woa, range(0, OT_A, 2)))
    SEG_KV = [(("kv", 0), cols(w_kv, 0, K, 0, 256))]
    SEG_B = (halves("mk1", w_mem_kv[1], 0) + halves("mv1", w_mem_kv[1], MW)
             + halves("qb0", wb, 0) + halves("qb1", wb, 512) + halves("qmb", wb, HQ * HD)
             + rows("ob", wob, range(OT_B, OT_B + 4, 2)) + rows("ob", wob, range(0, OT_B, 2)))
    unit = {}
    ffn_base = []
    uses = [0, 0, 0]
    for seg in (0, SEG_A, 0, SEG_KV, 0, SEG_B, 0):
        if seg == 0:
            ffn_base.append(tuple(uses))
            uses = [u + NCH for u in uses]
        else:
            for n, (name, _) in enumerate(seg):
                unit[name] = (n % 3, uses[n % 3])
                uses[n % 3] += 1

    GAINS = [("mem0", mem_norm_g[0:1, :]), ("pre0", norm_g[0, 0:1, :]),
             ("post1", norm_g[0, 1:2, :]), ("pre1", norm_g[0, 2:3, :]),
             ("post2", norm_g[0, 3:4, :]), ("pre2", norm_g[0, 4:5, :]),
             ("post3", norm_g[0, 5:6, :]), ("kv", kv_norm_g.rearrange("(a d) -> a d", a=1)), ("pre3", norm_g[1, 0:1, :]),
             ("mem1", mem_norm_g[1:2, :]),
             ("post4", norm_g[1, 1:2, :]), ("pre4", norm_g[1, 2:3, :]),
             ("post5", norm_g[1, 3:4, :]), ("pre5", norm_g[1, 4:5, :]),
             ("post6", norm_g[1, 5:6, :])]
    NG = 3
    gain_at = {name: i for i, (name, _) in enumerate(GAINS)}
    TURNS = ["mem0", "x0", "x1", "x2", "kv", "x3", "mem1", "x4", "x5"]
    turn_at = {name: i for i, name in enumerate(TURNS)}

    with ExitStack() as ctx:
        def sb(name, shape, dt=F32):
            return ctx.enter_context(nc.sbuf_tensor(name, shape, dt))

        def sem(name):
            return ctx.enter_context(nc.semaphore(name))

        ps = ctx.enter_context(nc.psum_tensor("ps", [P, 8, 512], F32))

        raw = sb("raw", [P, 3, UNIT])
        w_hi = sb("w_hi", [P, 3, UNIT], F32R)
        w_lo = sb("w_lo", [P, 3, UNIT], F32R)
        res = sb("res", [P, T, D])
        xg = sb("xg", [P, T, D])
        xh = sb("xh", [P, K, S], F32R)
        xl = sb("xl", [P, K, S], F32R)
        mh = sb("mh", [P, K, S], F32R)
        ml = sb("ml", [P, K, S], F32R)
        hh = sb("hh", [P, 2, S], F32R)
        hl = sb("hl", [P, 2, S], F32R)
        kmem = sb("kmem", [P, MH_, S])
        vmem = sb("vmem", [P, T, MW])
        qmem = sb("qmem", [P, MH_, S])
        gains = sb("gains", [P, NG, D])
        sc = sb("sc", [P, 10, 1024])
        gs = sb("gs", [P, T, D])
        kt = sb("kt", [P, 2, S])
        vs = sb("vs", [P, T, 2 * HD])
        vsh = sb("vsh", [64, 2 * HD])
        ident = sb("ident", [P, P])
        past = sb("past", [P, P])
        fut = sb("fut", [P, P])
        band0 = sb("band0", [P, 128])
        band1 = sb("band1", [P, 192])
        wgu = sb("wgu", [RANK, KW])
        bg = sb("bg", [P, GH])
        sink = sb("sink", [P, HQ])
        cosw = sb("cosw", [P, T, HD // 2])
        sinw = sb("sinw", [P, T, 2, HD // 2])
        posi = sb("posi", [P, T], I32)
        posf = sb("posf", [P, T])
        invf = sb("invf", [P, HD // 2])
        ang = sb("ang", [P, 4, T, HD // 2])
        glag = sb("glag", [P, DV])
        ssq = sb("ssq", [P, 4, 2])
        rr = sb("rr", [P, 4, 2])
        nw = sb("nw", [P, 4, 8])
        smx = sb("smx", [P, 8, 8])
        dec = sb("dec", [P, GH, 4])
        ssg = sb("ssg", [P, T * GH])
        rsg = sb("rsg", [P, T * GH])
        RM, RX, RY = 0, 1, 2

        kst, qdn, qup, am, kdn, kup = (sc[:, i, :] for i in range(6))
        state = [None, sc[:, 1, :], sc[:, 2, :], sc[:, 0, :]]
        qe = [sc[:, 6, :], sc[:, 7, :]]
        ksk = sc[:, 8, :]
        cmask = sc[:, 8, :]
        glr = sc[0:RANK, 6, 0:S]
        sil = sc[:, 9, 0:512].rearrange("p (t f) -> p t f", t=T)
        hid = sc[:, 9, 512:1024].rearrange("p (t f) -> p t f", t=T)
        junk = [sc[:, 4, :], sc[:, 5, :]]
        mx = sc[:, 6:8, :]
        pm = [sc[:, 4, :], sc[:, 5, :]]
        qt = sc[:, 1:3, :].rearrange("p a n -> p (a n)")
        wsc = [sc[:, 3, 0:512], sc[:, 6, 0:768]]
        wpt0, wpt1a, wpt1b = sc[:, 7, 0:512], sc[0:CHUNK, 7, 512:1024], sc[:, 0, 0:512]
        of = gs[:].rearrange("p t d -> p (t d)").rearrange("p (k s) -> p k s", k=K)
        pmt = sc[:, 8:10, :]

        landed = [sem(f"landed{i}") for i in range(3)]
        hi_ready = [sem(f"hi_ready{i}") for i in range(3)]
        lo_ready = [sem(f"lo_ready{i}") for i in range(3)]
        w_used = [sem(f"w_used{i}") for i in range(3)]
        gain_in = [sem(f"gain_in{i}") for i in range(NG)]
        res_in = [sem(f"res_in{t}") for t in range(T)]
        mem_in = sem("mem_in")
        small_in = sem("small_in")
        const_ready = sem("const_ready")
        pool_step = sem("pool_step")
        dve_step = sem("dve_step")
        act_step = sem("act_step")
        xg_ready = sem("xg_ready")
        turned = sem("turned")
        rx_ready = sem("rx_ready")
        th_ready = sem("th_ready")
        tl_ready = sem("tl_ready")
        ssq_ready = sem("ssq_ready")
        res_ready = sem("res_ready")
        up_done = sem("up_done")
        sil_ready = sem("sil_ready")
        gated = sem("gated")
        h_turned = sem("h_turned")
        hh_ready = sem("hh_ready")
        hl_ready = sem("hl_ready")
        y_done = sem("y_done")
        out_done = sem("out_done")
        ang_ready = sem("ang_ready")
        sin_ready = sem("sin_ready")
        kmem_ready = sem("kmem_ready")
        vmem_ready = sem("vmem_ready")
        qmem_ready = sem("qmem_ready")
        ms_done = sem("ms_done")
        ms_max = sem("ms_max")
        mp_raw = sem("mp_raw")
        mp_ready = sem("mp_ready")
        mp_turned = sem("mp_turned")
        mpt_ready = sem("mpt_ready")
        mo_done = sem("mo_done")
        mo_hi = sem("mo_hi")
        mo_lo = sem("mo_lo")
        glr_ready = sem("glr_ready")
        z_done = sem("z_done")
        zb_ready = sem("zb_ready")
        ln_ready = sem("ln_ready")
        cum_ready = sem("cum_ready")
        decay_ready = sem("decay_ready")
        k_taken = sem("k_taken")
        q_taken = sem("q_taken")
        v_ready = sem("v_ready")
        a_done = sem("a_done")
        a_taken = sem("a_taken")
        kst_turned = sem("kst_turned")
        ksk_ready = sem("ksk_ready")
        kv_done = sem("kv_done")
        s_ready = sem("s_ready")
        silr_ready = sem("silr_ready")
        o_done = sem("o_done")
        osq_ready = sem("osq_ready")
        on_ready = sem("on_ready")
        o_turned = sem("o_turned")
        oh_ready = sem("oh_ready")
        ol_ready = sem("ol_ready")
        kr_ready = sem("kr_ready")
        k_turned = sem("k_turned")
        kt_ready = sem("kt_ready")
        vs_ready = sem("vs_ready")
        qr_ready = sem("qr_ready")
        q_turned = sem("q_turned")
        qt_ready = sem("qt_ready")
        sw_done = sem("sw_done")
        sw_taken = sem("sw_taken")
        sw_max = sem("sw_max")
        wp_raw = sem("wp_raw")
        wp_ready = sem("wp_ready")
        wp_turned = sem("wp_turned")
        wpt_ready = sem("wpt_ready")
        pv_done = sem("pv_done")
        of_ready = sem("of_ready")

        block = ctx.enter_context(nc.Block())

        def gain_free(i):
            name = GAINS[i][0]
            if name[:4] == "post":
                return res_ready, 2 * int(name[4:])
            turn_name = {"pre": "x" + name[3:], "mem": name, "kv": "kv"}[name[:3] if name != "kv" else "kv"]
            return xg_ready, 2 * (turn_at[turn_name] + 1)

        def landings(slot, n):
            two = sum(min(max(n - b[slot], 0), NCH) for b in ffn_base) if slot < 2 else 0
            return 16 * (n + two)

        SIZE = {name: src.shape[1] * src.shape[2] for seg in (SEG_A, SEG_KV, SEG_B) for name, src in seg}
        NAMES = [name for seg in (SEG_A, SEG_KV, SEG_B) for name, _ in seg]

        def used(eng, name):
            slot, n = unit[name]
            eng.wait_ge(w_used[slot], n + 1)

        GROUPS = [(g, r, t) for g in range(2) for r in range(2) for t in range(T)]
        KEYS = [128, 192]
        HG = 4

        @block.sync
        def _(sp):
            def load(name, src):
                slot, n = unit[name]
                if n:
                    sp.wait_ge(lo_ready[slot], n)
                nk, w = src.shape[1], src.shape[2]
                dst = raw[:, slot, 0:nk * w].rearrange("p (k n) -> p k n", k=nk)
                sp.dma_start(dst, src).then_inc(landed[slot], 16)

            def ffn_loads(f):
                w_in = w_ffn_in[f // 2, f % 2].rearrange("(k p) (s n) -> p k s n", p=P, s=2)
                w_out = w_ffn_out[f // 2, f % 2].rearrange("(c p) n -> p c n", p=P)
                base = ffn_base[f]

                def up(c, h, first=False):
                    if not first:
                        sp.wait_ge(lo_ready[h], c + base[h])
                    dst = raw[:, h, :].rearrange("p (k s n) -> p k s n", k=4, s=2)
                    for s in range(2):
                        sp.dma_start(dst[:, :, s, :], w_in[:, 4 * h:4 * h + 4, s, bass.ds(c * FC, FC)])\
                          .then_inc(landed[h], 16)

                def down(c, first=False):
                    if not first:
                        sp.wait_ge(lo_ready[2], c + base[2])
                    sp.dma_start(raw[:, 2, :].rearrange("p (k n) -> p k n", k=2),
                                 w_out[:, bass.ds(c * 2, 2), :]).then_inc(landed[2], 16)

                up(0, 0, first=f == 0)
                up(0, 1, first=f == 0)
                up(1, 0)
                down(0, first=f == 0)
                up(1, 1)
                with sp.Fori(2, NCH) as c:
                    up(c, 0)
                    down(c - 1)
                    up(c, 1)
                down(NCH - 1)

            xv = x[0].rearrange("(t p) d -> p t d", p=P)
            for t in range(T):
                sp.dma_start(res[:, t, :], xv[:, t, :]).then_inc(res_in[t], 16)
            sp.dma_start(mx, mem[0].rearrange("(t p) d -> p t d", p=P)).then_inc(mem_in, 16)
            ffn_loads(0)
            for name, src in SEG_A:
                load(name, src)
            ffn_loads(1)
            for name, src in SEG_KV:
                load(name, src)
            sp.wait_ge(y_done, 2)
            sp.dma_start(mx, mem[0].rearrange("(t p) d -> p t d", p=P)).then_inc(mem_in, 16)
            ffn_loads(2)
            for name, src in SEG_B:
                load(name, src)
            ffn_loads(3)
            ov = out[0].rearrange("(t p) d -> p t d", p=P)
            for t in range(T):
                sp.wait_ge(res_ready, 2 * 5 + t + 1)
                sp.dma_start(ov[:, t, :], res[:, t, :]).then_inc(out_done, 16)
            sp.wait_ge(out_done, 16 * T)

        @block.gpsimd
        def _(pool):
            count = [0]

            def link(ins):
                count[0] += 1
                ins.then_inc(pool_step, 1)
                pool.wait_ge(pool_step, count[0])

            link(pool.memset(ident[:], 0.0))
            pool.affine_select(out=ident[:], in_=ident[:], compare_op=ALU.not_equal, fill=1.0, base=0,
                               pattern=[[-1, P]], channel_multiplier=1).then_inc(const_ready, 1)
            link(pool.memset(past[:], 1.0))
            link(pool.affine_select(out=past[:], in_=past[:], compare_op=ALU.is_ge, fill=0.0, base=0,
                                    pattern=[[1, P]], channel_multiplier=-1))
            link(pool.memset(past[0:64, 64:128], 0.0))
            link(pool.memset(fut[:], 1.0))
            link(pool.affine_select(out=fut[:], in_=fut[:], compare_op=ALU.is_gt, fill=0.0, base=0,
                                    pattern=[[-1, P]], channel_multiplier=1))
            link(pool.memset(fut[64:128, 0:64], 0.0))
            link(pool.memset(band0[:], 0.0))
            link(pool.memset(band0[0:64, 64:128], NEG_INF))
            link(pool.memset(band1[:], 0.0))
            link(pool.memset(band1[0:64, 128:192], NEG_INF))
            link(pool.memset(band1[64:128, 0:64], NEG_INF))
            for i in range(HD // 2):
                pool.memset(invf[:, i:i + 1], float(inv_freq[i]))
            link(pool.memset(cmask, 1.0))
            pool.memset(cmask.rearrange("p (c j) -> p c j", j=CHUNK)[:, :, 0:1], 0.0).then_inc(const_ready, 1)

            def lo(slot, n, size=UNIT):
                pool.wait_ge(hi_ready[slot], n + 1)
                pool.tensor_tensor(w_lo[:, slot, 0:size], raw[:, slot, 0:size], w_hi[:, slot, 0:size].bitcast(F32),
                                   ALU.subtract).then_inc(lo_ready[slot], 1)

            def seg(units):
                for name, src in units:
                    lo(*unit[name], size=SIZE[name])

            def ffn(f):
                with pool.Fori(0, NCH) as c:
                    for h in range(2):
                        lo(h, c + ffn_base[f][h])

            ffn(0)
            seg(SEG_A)
            ffn(1)
            seg(SEG_KV)
            ffn(2)
            seg(SEG_B)
            ffn(3)

        @block.tensor
        def _(pe):
            mm = nc.tensor.matmul
            x_act, m_act = (xh, xl), (mh, ml)

            def take(slot, n):
                pe.wait_ge(lo_ready[slot], n + 1)

            def three(dst, a, b, at_a, at_b, start, stop, group=False):
                mm(dst, a[0][at_a], b[0][at_b], start=start, stop=False, skip_group_check=group)
                mm(dst, a[0][at_a], b[1][at_b], start=False, stop=False, skip_group_check=group)
                return mm(dst, a[1][at_a], b[0][at_b], start=False, stop=stop, skip_group_check=group)

            def parts(slot, k, n=UNIT):
                return tuple(w[:, slot, 0:n].rearrange("p (k n) -> p k n", k=k) for w in (w_hi, w_lo))

            def turn(name, src):
                n = turn_at[name]
                if n == 0:
                    pe.wait_ge(const_ready, 1)
                for t in range(T):
                    pe.wait_ge(xg_ready, 2 * n + t + 1)
                    if n and t == 0:
                        pe.wait_ge(tl_ready, 4 * n)
                    for k in range(K):
                        i = nc.tensor.transpose(ps[:, k // 2, (k % 2) * S + t * P:(k % 2) * S + (t + 1) * P],
                                                src[:, t, k * P:(k + 1) * P], ident[:])
                        if t == T - 1 and k % 2:
                            i.then_inc(turned, 1)

            def turned_in(name, k):
                pe.wait_ge(tl_ready, 4 * turn_at[name] + k // 2 + 1)

            def rowwise(name, act, turn_name, banks):
                for i in range(2):
                    slot, n = unit[(name, i)]
                    take(slot, n)
                    w = parts(slot, 4)
                    for t in range(T):
                        for k in range(4):
                            if t == 0:
                                turned_in(turn_name, 4 * i + k)
                            last = three(ps[:, banks[t], :], act, w, np.s_[:, 4 * i + k, t * P:(t + 1) * P],
                                         np.s_[:, k, :], start=(i == 0 and k == 0), stop=(i == 1 and k == 3))
                    last.then_inc(w_used[slot], 1)

            def colwise(name, act, turn_name, banks):
                for i in range(2):
                    slot, n = unit[(name, i)]
                    take(slot, n)
                    w = parts(slot, 4)
                    for k in range(4):
                        turned_in(turn_name, 4 * i + k)
                        for h in range(4):
                            last = three(ps[:, banks[h // 2], (h % 2) * S:(h % 2 + 1) * S], w, act,
                                         np.s_[:, k, h * P:(h + 1) * P], np.s_[:, 4 * i + k, :],
                                         start=(i == 0 and k == 0 and h % 2 == 0), stop=(i == 1 and k == 3),
                                         group=True)
                    last.then_inc(w_used[slot], 1)

            def ffn(f, between=None):
                base = ffn_base[f]
                tname = f"x{(0, 2, 3, 5)[f]}"

                def up(c, h, first=False):
                    take(h, c + base[h])
                    w = parts(h, 4)
                    for t in range(T):
                        if h == 0 and not first:
                            pe.wait_ge(gated, c * 2 + (2 * NCH * f - 1 + t))
                        for k in range(4):
                            if first and t == 0:
                                turned_in(tname, 4 * h + k)
                            last = three(ps[:, 4 + t, :], x_act, w, np.s_[:, 4 * h + k, t * P:(t + 1) * P],
                                         np.s_[:, k, :], start=(h == 0 and k == 0), stop=(h == 1 and k == 3))
                        if h == 1 and t == 0:
                            last.then_inc(up_done, 1)
                    last.then_inc(w_used[h], 1)

                def turn_h(c):
                    pe.wait_ge(gated, c * 2 + (2 * NCH * f + 2))
                    if f or not isinstance(c, int) or c:
                        pe.wait_ge(hl_ready, c + NCH * f)
                    for j in range(2):
                        for t in range(T):
                            last = nc.tensor.transpose(ps[:, 6, j * S + t * P:j * S + (t + 1) * P],
                                                       hid[:, t, j * P:(j + 1) * P], ident[:])
                    last.then_inc(h_turned, 1)

                def down(c, start=False, stop=False):
                    take(2, c + base[2])
                    pe.wait_ge(hl_ready, c + (NCH * f + 1))
                    w = parts(2, 2)
                    for t in range(T):
                        for k in range(2):
                            for n in range(2):
                                last = three(ps[:, 2 * t + n, :], (hh, hl), w, np.s_[:, k, t * P:(t + 1) * P],
                                             np.s_[:, k, n * 512:(n + 1) * 512],
                                             start=(start and k == 0), stop=(stop and k == 1))
                        if stop and t == 0:
                            last.then_inc(y_done, 1)
                    last.then_inc(w_used[2], 1)

                up(0, 0, first=True)
                up(0, 1, first=True)
                if between is not None:
                    between()
                up(1, 0)
                turn_h(0)
                up(1, 1)
                down(0, start=True)
                with pe.Fori(2, NCH) as c:
                    up(c, 0)
                    turn_h(c - 1)
                    up(c, 1)
                    down(c - 1)
                turn_h(NCH - 1)
                down(NCH - 1, stop=True)

            def mixer_out(name, first_tile, tiles):
                order = [k for k in range(first_tile, first_tile + 4, 2)] + list(range(0, tiles, 2))
                for i, k0 in enumerate(order):
                    slot, n = unit[(name, k0)]
                    take(slot, n)
                    w = parts(slot, 2)
                    act, at = (m_act, k0 - first_tile) if k0 >= first_tile else (x_act, k0)
                    for t in range(T):
                        for k in range(2):
                            for c in range(2):
                                last = three(ps[:, 2 * t + c, :], act, w, np.s_[:, at + k, t * P:(t + 1) * P],
                                             np.s_[:, k, c * 512:(c + 1) * 512],
                                             start=(i == 0 and k == 0), stop=(i == len(order) - 1 and k == 1))
                        if i == len(order) - 1 and t == 0:
                            last.then_inc(y_done, 1)
                    last.then_inc(w_used[slot], 1)

            def mem_scores(t, b):
                for h in range(MH_):
                    last = mm(ps[:, b + h // 2, (h % 2) * S:(h % 2 + 1) * S], qmem[:, h, t * P:(t + 1) * P],
                              kmem[:, h, :], start=True, stop=True)
                last.then_inc(ms_done, 1)

            def mem_turn(t, b, layer):
                pe.wait_ge(mp_ready, T * layer + t + 1)
                for j in range(T):
                    for h in range(MH_):
                        last = nc.tensor.transpose(ps[:, b + j, h * P:(h + 1) * P],
                                                   pm[t][:, h * S + j * P:h * S + (j + 1) * P], ident[:])
                last.then_inc(mp_turned, 1)

            def mem_out(b, layer):
                pe.wait_ge(mpt_ready, T * (layer + 1))
                for h in range(MH_):
                    for j in range(T):
                        last = mm(ps[:, b + h // 2, (h % 2) * S:(h % 2 + 1) * S], vmem[:, j, h * MD:(h + 1) * MD],
                                  pmt[:, j, h * S:(h + 1) * S], start=(j == 0), stop=(j == T - 1))
                last.then_inc(mo_done, 1)

            def gla():
                colwise("mk0", m_act, "mem0", (4, 5))
                turn("x1", xg)
                rowwise("mv0", m_act, "mem0", (6, 7))
                pe.wait_ge(kmem_ready, 1)
                slot, n = unit[("ga", 0)]
                take(slot, n)
                w = parts(slot, K, K * P)
                for k in range(K):
                    turned_in("x1", k)
                    last = three(ps[:, 4, 0:S], w, x_act, np.s_[:, k, :], np.s_[:, k, :],
                                 start=(k == 0), stop=(k == K - 1))
                last.then_inc(w_used[slot], 1)
                pe.wait_ge(glr_ready, 1)
                pe.wait_ge(small_in, 16 * 5)
                for h in range(GH):
                    last = mm(ps[:, h // 2, (h % 2) * S:(h % 2 + 1) * S], wgu[:, h * DK:(h + 1) * DK], glr,
                              start=True, stop=True)
                last.then_inc(z_done, 1)
                colwise("ka", x_act, "x1", (2, 3))
                pe.wait_ge(vmem_ready, 1)
                colwise("qa", x_act, "x1", (6, 7))
                colwise("qma", x_act, "x1", (4, 5))
                pe.wait_ge(zb_ready, 1)
                rowwise("va0", x_act, "x1", (0, 1))
                pe.wait_ge(k_taken, 1)
                rowwise("va1", x_act, "x1", (2, 3))

                def scores(t):
                    if t:
                        pe.wait_ge(a_taken, t)
                    for b, keys, queries in ((6, kdn, qup), (7, kup, qdn)):
                        for h in range(GH):
                            at = np.s_[:, h * S + t * P:h * S + (t + 1) * P]
                            last = mm(ps[:, b, h * P:(h + 1) * P], keys[at], queries[at], start=True, stop=True)
                    last.then_inc(a_done, 1)

                def chunk_kv(n, b):
                    t, at = n // 2, np.s_[(n % 2) * CHUNK:(n % 2 + 1) * CHUNK]
                    for h in range(GH):
                        last = mm(ps[:, b + h // 2, (h % 2) * DV:(h % 2 + 1) * DV],
                                  ksk[at, (t * GH + h) * DK:(t * GH + h + 1) * DK], xg[at, t, h * DV:(h + 1) * DV],
                                  start=True, stop=True)
                    last.then_inc(kv_done, 1)

                pe.wait_ge(q_taken, 1)
                scores(0)
                pe.wait_ge(qmem_ready, 1)
                for t in range(T):
                    for h in range(GH):
                        last = nc.tensor.transpose(ps[:, 4 + t, h * P:(h + 1) * P],
                                                   kst[:, h * S + t * P:h * S + (t + 1) * P], ident[:])
                last.then_inc(kst_turned, 1)
                pe.wait_ge(v_ready, 1)
                rowwise("ra0", x_act, "x1", (0, 1))
                scores(1)
                pe.wait_ge(ksk_ready, 1)
                pe.wait_ge(v_ready, 2)
                chunk_kv(0, 4)
                rowwise("ra1", x_act, "x1", (2, 3))
                pe.wait_ge(a_taken, 2)
                chunk_kv(1, 6)
                pe.wait_ge(s_ready, 1)
                chunk_kv(2, 4)
                pe.wait_ge(silr_ready, 2)
                mem_scores(0, 0)
                mem_scores(1, 2)
                for t, b in ((0, 6), (1, 4)):
                    pe.wait_ge(s_ready, t + 2)
                    for h in range(GH):
                        dst = ps[:, b + h // 2, (h % 2) * DV:(h % 2 + 1) * DV]
                        at = np.s_[:, (t * GH + h) * P:(t * GH + h + 1) * P]
                        mm(dst, am[at], xg[:, t, h * DV:(h + 1) * DV], start=True, stop=False)
                        for e in range(2):
                            if 2 * t + e:
                                last = mm(dst, qe[e][:, h * S + t * P:h * S + (t + 1) * P],
                                          state[2 * t + e][:, h * DV:(h + 1) * DV], start=False, stop=(e == 1))
                    last.then_inc(o_done, 1)
                mem_turn(0, 0, 0)
                mem_turn(1, 2, 0)
                mem_out(0, 0)
                for t, b in ((0, 6), (1, 4)):
                    pe.wait_ge(on_ready, t + 1)
                    for k in range(K):
                        i = nc.tensor.transpose(ps[:, b + k // 4, (k % 4) * P:(k % 4 + 1) * P],
                                                gs[:, t, k * P:(k + 1) * P], ident[:])
                        if k % 4 == 3:
                            i.then_inc(o_turned, 1)
                pe.wait_ge(mo_lo, 1)
                pe.wait_ge(ol_ready, 4)
                mixer_out("oa", OT_A, OT_A)

            def window_kv():
                turn("kv", xg)
                slot, n = unit[("kv", 0)]
                take(slot, n)
                w = parts(slot, K)
                for t in range(T):
                    for k in range(K):
                        turned_in("kv", k)
                        last = three(ps[:, 7, t * S:(t + 1) * S], m_act, w, np.s_[:, k, t * P:(t + 1) * P],
                                     np.s_[:, k, :], start=(k == 0), stop=(k == K - 1))
                last.then_inc(w_used[slot], 1)

            def turn_keys_and_memory():
                pe.wait_ge(kr_ready, 1)
                for g in range(2):
                    for t in range(T):
                        last = nc.tensor.transpose(ps[:, 6, g * S + t * P:g * S + (t + 1) * P],
                                                   gs[:, 0, (t * 2 + g) * P:(t * 2 + g + 1) * P], ident[:])
                last.then_inc(k_turned, 1)
                turn("mem1", mx)
                pe.wait_ge(kt_ready, 1)
                pe.wait_ge(tl_ready, 4 * (turn_at["mem1"] + 1))

            def window():
                colwise("mk1", m_act, "mem1", (4, 5))
                turn("x4", xg)
                rowwise("mv1", m_act, "mem1", (6, 7))
                pe.wait_ge(tl_ready, 4 * (turn_at["x4"] + 1))
                rowwise("qb0", x_act, "x4", (0, 1))
                rowwise("qb1", x_act, "x4", (2, 3))
                pe.wait_ge(kmem_ready, 2)
                colwise("qmb", x_act, "x4", (4, 5))
                pe.wait_ge(vmem_ready, 2)
                pe.wait_ge(qr_ready, 4)
                for i in range(8):
                    b = (6, 7, 0, 1)[i // 2]
                    for t in range(T):
                        last = nc.tensor.transpose(ps[:, b, (i % 2) * S + t * P:(i % 2) * S + (t + 1) * P],
                                                   gs[:, t, i * P:(i + 1) * P], ident[:])
                    if i % 2:
                        last.then_inc(q_turned, 1)
                pe.wait_ge(qmem_ready, 2)
                mem_scores(0, 4)
                mem_scores(1, 2)
                mem_turn(0, 4, 1)
                mem_turn(1, 2, 1)
                mem_out(4, 1)
                pe.wait_ge(mo_lo, 2)
                pe.wait_ge(qt_ready, 4)

                def scores(s):
                    g, r, t = GROUPS[s]
                    if s >= 2:
                        pe.wait_ge(sw_taken, s - 1)
                    n = KEYS[t]
                    for i in range(HG):
                        at = np.s_[r * HD:(r + 1) * HD]
                        dst = ps[:, 0, i * n:(i + 1) * n] if t == 0 else ps[:, 1 + i // 2, (i % 2) * n:(i % 2 + 1) * n]
                        last = mm(dst, qt[at, (g * HG + i) * S + t * P:(g * HG + i) * S + (t + 1) * P],
                                  kt[at, g, S - n if t else 0:S if t else n], start=True, stop=True)
                    last.then_inc(sw_done, 1)

                def turn_p(s):
                    g, r, t = GROUPS[s]
                    pe.wait_ge(wp_ready, s + 1)
                    if s >= 2:
                        pe.wait_ge(wpt_ready, s - 1)
                    src = wsc[t].rearrange("p (h k) -> p h k", h=HG)
                    for i in range(HG):
                        if t == 0:
                            last = nc.tensor.transpose(ps[:, 3, i * P:(i + 1) * P], src[:, i, :], ident[:])
                        else:
                            nc.tensor.transpose(ps[0:CHUNK, 4, i * P:(i + 1) * P], src[:, i, 0:CHUNK], ident[:])
                            last = nc.tensor.transpose(ps[:, 5, i * P:(i + 1) * P], src[:, i, CHUNK:], ident[:])
                    last.then_inc(wp_turned, 1)

                def weigh(s):
                    g, r, t = GROUPS[s]
                    pe.wait_ge(wpt_ready, s + 1)
                    if s >= 2:
                        pe.wait_ge(of_ready, s - 1)
                    at = np.s_[g * HD:(g + 1) * HD]
                    dst = ps[0:HD, 6 + t, :]
                    if t == 0:
                        last = mm(dst, vs[:, 0, at], wpt0, start=True, stop=True)
                    else:
                        mm(dst, vsh[:, at], wpt1a, start=True, stop=False)
                        last = mm(dst, vs[:, 1, at], wpt1b, start=False, stop=True)
                    last.then_inc(pv_done, 1)

                for s in range(len(GROUPS) + 2):
                    if s < len(GROUPS):
                        scores(s)
                    if 1 <= s <= len(GROUPS):
                        turn_p(s - 1)
                    if s >= 2:
                        weigh(s - 2)
                pe.wait_ge(ol_ready, 6)
                mixer_out("ob", OT_B, OT_B)

            turn("mem0", mx)
            turn("x0", xg)
            pe.wait_ge(tl_ready, 4 * (turn_at["x0"] + 1))
            ffn(0)
            gla()
            turn("x2", xg)
            pe.wait_ge(tl_ready, 4 * (turn_at["x2"] + 1))
            ffn(1)
            window_kv()
            turn("x3", xg)
            ffn(2, between=turn_keys_and_memory)
            window()
            turn("x5", xg)
            pe.wait_ge(tl_ready, 4 * (turn_at["x5"] + 1))
            ffn(3)

        @block.scalar
        def _(act):
            act_count = [0]

            def link(ins):
                act_count[0] += 1
                ins.then_inc(act_step, 1)
                act.wait_ge(act_step, act_count[0])

            def gain(name):
                i = gain_at[name]
                if i >= NG:
                    act.wait_ge(*gain_free(i - NG))
                act.dma_start(gains[:, i % NG, :], GAINS[i][1].partition_broadcast(P)).then_inc(gain_in[i % NG], 16)

            def hi(slot, n, size=UNIT, land=None):
                act.wait_ge(landed[slot], landings(slot, n + 1) if land is None else land)
                if not isinstance(n, int) or n:
                    act.wait_ge(w_used[slot], n)
                act.activation(w_hi[:, slot, 0:size], raw[:, slot, 0:size], ACT.Copy).then_inc(hi_ready[slot], 1)

            units = iter(NAMES)

            def hi_next(count=1):
                for _ in range(count):
                    name = next(units)
                    hi(*unit[name], size=SIZE[name])

            squares = [0]

            def square(src, t, what):
                n = squares[0]
                squares[0] += 1
                if n >= 2:
                    act.wait_ge(ssq_ready, n - 1)
                act.activation(junk[n % 2], src, ACT.Square, accum_out=ssq[:, what, t:t + 1]).then_inc(ssq_ready, 1)

            def turned_hi(name, dst):
                n = turn_at[name]
                for i in range(4):
                    act.wait_ge(turned, 4 * n + i + 1)
                    act.activation(dst[:, 2 * i:2 * i + 2, :], ps[:, i, :].rearrange("p (k s) -> p k s", k=2),
                                   ACT.Copy).then_inc(th_ready, 1)

            def ffn_first(f):
                for s in range(2):
                    hi(s, ffn_base[f][s])

            def ffn(f, gain_names, between=None):
                base = ffn_base[f]

                def hi_f(s, c):
                    per = 32 if s < 2 else 16
                    hi(s, c + base[s], land=c * per + (landings(s, base[s]) + per))

                def silu(c):
                    for t in range(T):
                        if t == 0:
                            act.wait_ge(up_done, c + (NCH * f + 1))
                        else:
                            act.wait_ge(w_used[1], c + (base[1] + 1))
                        act.activation(sil[:, t, :], ps[:, 4 + t, 0:FC], ACT.Silu, scale=rr[:, RX, t:t + 1])\
                           .then_inc(sil_ready, 1)

                def hh_copy(c):
                    act.wait_ge(h_turned, c + (NCH * f + 1))
                    act.activation(hh[:], ps[:, 6, :].rearrange("p (k s) -> p k s", k=2), ACT.Copy)\
                       .then_inc(hh_ready, 1)

                for n in gain_names:
                    gain(n)
                hi_f(0, 1)
                act.wait_ge(rx_ready, f + 1)
                silu(0)
                hi_f(1, 1)
                if between is not None:
                    between()
                hi_f(2, 0)
                with act.Fori(1, NCH - 1) as c:
                    hh_copy(c - 1)
                    hi_f(0, c + 1)
                    silu(c)
                    hi_f(1, c + 1)
                    hi_f(2, c)
                hh_copy(NCH - 2)
                silu(NCH - 1)
                hi_f(2, NCH - 1)
                hh_copy(NCH - 1)

            Y_LAST = [(2, ffn_base[0][2] + NCH), None, (2, ffn_base[1][2] + NCH), (2, ffn_base[2][2] + NCH), None,
                      (2, ffn_base[3][2] + NCH)]
            for m, name in ((1, ("oa", OT_A - 2)), (4, ("ob", OT_B - 2))):
                Y_LAST[m] = (unit[name][0], unit[name][1] + 1)

            def square_y(m):
                act.wait_ge(y_done, m + 1)
                square(ps[:, 0:2, :].rearrange("p b n -> p (b n)"), 0, RY)
                slot, n = Y_LAST[m]
                act.wait_ge(w_used[slot], n)
                square(ps[:, 2:4, :].rearrange("p b n -> p (b n)"), 1, RY)

            def square_res(m):
                for t in range(T):
                    act.wait_ge(res_ready, 2 * m + t + 1)
                    square(res[:, t, :], t, RX)

            def two(b):
                return ps[:, b:b + 2, :].rearrange("p b n -> p (b n)")

            def mem_exp(t, b, layer):
                act.wait_ge(ms_max, T * layer + t + 1)
                for h in range(MH_):
                    act.activation(pm[t][:, h * S:(h + 1) * S], ps[:, b + h // 2, (h % 2) * S:(h % 2 + 1) * S],
                                   ACT.Exp, bias=smx[:, t, h:h + 1], scale=MD ** -0.5,
                                   accum_out=smx[:, 2 + t, h:h + 1]).then_inc(mp_raw, 1)

            def gla():
                hi_next(2)
                square_y(0)
                hi_next()
                square_res(0)
                hi_next()
                used(act, ("mk0", 1))
                act.activation(kmem[:].rearrange("p h s -> p (h s)"), two(4), ACT.Copy).then_inc(kmem_ready, 1)
                hi_next()
                turned_hi("x1", xh)
                hi_next()
                used(act, ("mv0", 1))
                act.activation(vmem[:].rearrange("p t n -> p (t n)"), two(6), ACT.Copy).then_inc(vmem_ready, 1)
                hi_next(2)
                act.wait_ge(zb_ready, 1)
                link(act.activation(sc[:, 1, :], sc[:, 1, :], ACT.Exp))
                act.activation(sc[:, 1, :], sc[:, 1, :], ACT.Ln, bias=1.0).then_inc(ln_ready, 1)
                hi_next(2)
                act.wait_ge(cum_ready, 2)
                cum = am
                act.activation(qup, qdn, ACT.Exp, scale=-1.0 / TAU).then_inc(decay_ready, 1)
                act.wait_ge(decay_ready, 1)
                act.activation(qdn, qdn, ACT.Exp, scale=1.0 / TAU).then_inc(decay_ready, 1)
                act.activation(kst, kst, ACT.Exp, scale=1.0 / TAU).then_inc(decay_ready, 1)
                act.activation(dec[:].rearrange("p h c -> p (h c)"),
                               cum.rearrange("p (c j) -> p c j", j=CHUNK)[:, :, CHUNK - 1], ACT.Exp, scale=1.0 / TAU)\
                   .then_inc(decay_ready, 1)
                act.wait_ge(decay_ready, 4)
                act.activation(cum, cum, ACT.Exp, scale=1.0 / TAU).then_inc(decay_ready, 1)
                hi_next(2)
                used(act, ("qma", 1))
                act.activation(qmem[:].rearrange("p h s -> p (h s)"), two(4), ACT.Copy).then_inc(qmem_ready, 1)
                hi_next(2)
                used(act, ("va0", 1))
                act.activation(xg[:, :, 0:512], ps[:, 0:2, :], ACT.Copy).then_inc(v_ready, 1)
                hi_next(2)
                used(act, ("va1", 1))
                act.activation(xg[:, :, 512:1024], ps[:, 2:4, :], ACT.Copy).then_inc(v_ready, 1)
                hi_next(2)
                act.wait_ge(kst_turned, 1)
                act.activation(ksk, two(4), ACT.Copy).then_inc(ksk_ready, 1)
                hi_next(2)
                used(act, ("ra0", 1))
                act.activation(gs[:, :, 0:512], ps[:, 0:2, :], ACT.Silu).then_inc(silr_ready, 1)
                hi_next()
                used(act, ("ra1", 1))
                act.activation(gs[:, :, 512:1024], ps[:, 2:4, :], ACT.Silu).then_inc(silr_ready, 1)
                hi_next()
                gain("post2")
                gain("pre2")
                mem_exp(0, 0, 0)
                mem_exp(1, 2, 0)
                for t, b in ((0, 6), (1, 4)):
                    act.wait_ge(o_done, t + 1)
                    for h in range(GH):
                        n = t * GH + h
                        if n >= 2:
                            act.wait_ge(osq_ready, n - 1)
                        act.activation(kt[:, h % 2, :], ps[:, b + h // 2, (h % 2) * DV:(h % 2 + 1) * DV], ACT.Square,
                                       accum_out=ssg[:, t * GH + h:t * GH + h + 1]).then_inc(osq_ready, 1)
                act.wait_ge(mp_turned, 1)
                act.activation(pmt.rearrange("p j (h s) -> p j h s", h=MH_)[:, :, :, 0:P],
                               ps[:, 0:2, :].rearrange("p j (h s) -> p j h s", h=MH_), ACT.Copy).then_inc(mpt_ready, 1)
                act.wait_ge(mo_done, 1)
                act.activation(mh[:, 0:4, :], two(0).rearrange("p (h s) -> p h s", h=MH_), ACT.Copy).then_inc(mo_hi, 1)
                for t, b in ((0, 6), (1, 4)):
                    for j in range(2):
                        act.wait_ge(o_turned, 2 * t + j + 1)
                        act.activation(xh[:, 4 * j:4 * j + 4, t * P:(t + 1) * P],
                                       ps[:, b + j, :].rearrange("p (k s) -> p k s", k=4), ACT.Copy)\
                           .then_inc(oh_ready, 1)
                hi_next(3)

            def window():
                hi_next(2)
                square_y(3)
                hi_next()
                square_res(3)
                hi_next()
                used(act, ("mk1", 1))
                act.activation(kmem[:].rearrange("p h s -> p (h s)"), two(4), ACT.Copy).then_inc(kmem_ready, 1)
                hi_next()
                turned_hi("x4", xh)
                hi_next()
                used(act, ("mv1", 1))
                act.activation(vmem[:].rearrange("p t n -> p (t n)"), two(6), ACT.Copy).then_inc(vmem_ready, 1)
                hi_next(4)
                used(act, ("qmb", 1))
                act.activation(qmem[:].rearrange("p h s -> p (h s)"), two(4), ACT.Copy).then_inc(qmem_ready, 1)
                for i in range(4):
                    b = (6, 7, 0, 1)[i]
                    act.wait_ge(q_turned, i + 1)
                    act.activation(qt[:, i * 512:(i + 1) * 512], ps[:, b, :], ACT.Copy).then_inc(qt_ready, 1)
                hi_next(3)
                gain("post5")
                gain("pre5")
                mem_exp(0, 4, 1)
                mem_exp(1, 2, 1)
                act.wait_ge(mp_turned, 3)
                act.activation(pmt.rearrange("p j (h s) -> p j h s", h=MH_)[:, :, :, 0:P],
                               ps[:, 4:6, :].rearrange("p j (h s) -> p j h s", h=MH_), ACT.Copy).then_inc(mpt_ready, 1)
                act.wait_ge(mo_done, 2)
                act.activation(mh[:, 0:4, :], two(4).rearrange("p (h s) -> p h s", h=MH_), ACT.Copy).then_inc(mo_hi, 1)

                def exps(s):
                    g, r, t = GROUPS[s]
                    act.wait_ge(sw_max, s + 1)
                    for i in range(HG):
                        row = wsc[t].rearrange("p (h k) -> p h k", h=HG)[:, i, :]
                        act.activation(row, row, ACT.Exp, bias=smx[:, 4 * t, i:i + 1],
                                       accum_out=smx[:, 4 * t + 1, i:i + 1]).then_inc(wp_raw, 1)
                    act.activation(smx[:, 4 * t + 2, 0:HG], smx[:, 4 * t + 2, 0:HG], ACT.Exp).then_inc(wp_raw, 1)

                def copy_p(s):
                    g, r, t = GROUPS[s]
                    act.wait_ge(wp_turned, s + 1)
                    if t == 0:
                        act.activation(wpt0, ps[:, 3, :], ACT.Copy).then_inc(wpt_ready, 1)
                    else:
                        act.activation(wpt1a, ps[0:CHUNK, 4, :], ACT.Copy)
                        act.activation(wpt1b, ps[:, 5, :], ACT.Copy).then_inc(wpt_ready, 1)

                def output_hi(g):
                    act.wait_ge(of_ready, 4 * (g + 1))
                    act.activation(xh[:, 4 * g:4 * g + 4, :], of[:, 4 * g:4 * g + 4, :], ACT.Copy).then_inc(oh_ready, 1)

                for s in range(len(GROUPS) + 1):
                    if s < len(GROUPS):
                        exps(s)
                    if s >= 1:
                        copy_p(s - 1)
                    if s == 6:
                        output_hi(0)
                output_hi(1)
                hi_next(3)

            gain("mem0")
            gain("pre0")
            act.dma_start(wgu[:], w_gate_up[0]).then_inc(small_in, 16)
            with nc.allow_non_contiguous_dma("one gate bias and two positions a partition"):
                act.dma_start(bg[:], b_gate[0].rearrange("(h p) -> p h", p=P)).then_inc(small_in, 16)
                act.dma_start(posi[:], positions[0].rearrange("(t p) -> p t", p=P)).then_inc(small_in, 16)
            act.dma_start(sink[:], sinks[0:1, :].partition_broadcast(P)).then_inc(small_in, 16)
            act.dma_start(glag[:], gla_norm_g[0:1, :].partition_broadcast(P)).then_inc(small_in, 16)
            act.wait_ge(mem_in, 16)
            for t in range(T):
                square(mx[:, t, :], t, RM)
            for t in range(T):
                act.wait_ge(res_in[t], 16)
                square(res[:, t, :], t, RX)
            turned_hi("mem0", mh)
            turned_hi("x0", xh)
            ffn_first(0)
            act.wait_ge(ang_ready, 1)
            act.activation(sinw[:, :, 1, :], ang[:, 0], ACT.Sin).then_inc(sin_ready, 1)
            act.activation(cosw[:], ang[:, 1], ACT.Sin).then_inc(sin_ready, 1)
            ffn(0, ["post1", "pre1"])
            gla()
            ffn_first(1)
            square_y(1)
            square_res(1)
            turned_hi("x2", xh)
            ffn(1, ["post3", "kv", "pre3"])
            hi_next()
            square_y(2)
            square_res(2)
            turned_hi("kv", mh)
            ffn_first(2)
            turned_hi("x3", xh)

            def between():
                act.wait_ge(k_turned, 1)
                act.activation(kt[:].rearrange("p g s -> p (g s)"), ps[:, 6, :], ACT.Copy).then_inc(kt_ready, 1)
                turned_hi("mem1", mh)

            gain("mem1")
            ffn(2, ["post4", "pre4"], between)
            window()
            ffn_first(3)
            square_y(4)
            square_res(4)
            turned_hi("x5", xh)
            ffn(3, ["post6"])
            square_y(5)

        @block.vector
        def _(dve):
            dve_count = [0]

            def link(ins):
                dve_count[0] += 1
                ins.then_inc(dve_step, 1)
                dve.wait_ge(dve_step, dve_count[0])

            def rsqrt(dst, src, n, scale):
                half, y, t, u = (nw[:, i, 0:n] for i in range(4))
                link(dve.tensor_scalar(half, src, 0.5 * scale, 0.5 * EPS, ALU.mult, ALU.add))
                link(dve.tensor_scalar(t.bitcast(I32), half.bitcast(I32), 1, None, ALU.logical_shift_right))
                link(dve.tensor_scalar(y.bitcast(I32), t.bitcast(I32), -1.0,
                                       float(RSQRT_MAGIC - 2 ** 22 - 2 ** 31), ALU.mult, ALU.add))
                for i in range(3):
                    link(dve.tensor_tensor(t, y, y, ALU.mult))
                    link(dve.tensor_tensor(u, t, half, ALU.mult))
                    link(dve.scalar_tensor_tensor(out=dst if i == 2 else y, in0=u, scalar=1.5, in1=y,
                                                  op0=ALU.subtract, op1=ALU.mult))

            def gain(name):
                i = gain_at[name]
                dve.wait_ge(gain_in[i % NG], 16 * (i // NG + 1))
                return gains[:, i % NG, :]

            def turned_lo(name, lead, dst):
                n = turn_at[name]
                for i in range(4):
                    dve.wait_ge(th_ready, 4 * n + i + 1)
                    dve.tensor_tensor(dst[:, 2 * i:2 * i + 2, :], ps[:, i, :].rearrange("p (k s) -> p k s", k=2),
                                      lead[:, 2 * i:2 * i + 2, :].bitcast(F32), ALU.subtract).then_inc(tl_ready, 1)

            def lo(slot, n):
                dve.wait_ge(hi_ready[slot], n + 1)
                dve.tensor_tensor(w_lo[:, slot, :], raw[:, slot, :], w_hi[:, slot, :].bitcast(F32),
                                  ALU.subtract).then_inc(lo_ready[slot], 1)

            def ffn(f, between=None):
                base = ffn_base[f]

                def gate(c):
                    for t in range(T):
                        dve.wait_ge(sil_ready, c * 2 + (2 * NCH * f + t + 1))
                        dve.scalar_tensor_tensor(out=hid[:, t, :], in0=ps[:, 4 + t, FC:2 * FC],
                                                 scalar=rr[:, RX, t:t + 1], in1=sil[:, t, :],
                                                 op0=ALU.mult, op1=ALU.mult).then_inc(gated, 1)

                def hl_sub(c):
                    dve.wait_ge(hh_ready, c + (NCH * f + 1))
                    dve.tensor_tensor(hl[:], ps[:, 6, :].rearrange("p (k s) -> p k s", k=2), hh[:].bitcast(F32),
                                      ALU.subtract).then_inc(hl_ready, 1)

                gate(0)
                if between is not None:
                    between()
                lo(2, base[2])
                with dve.Fori(1, NCH) as c:
                    hl_sub(c - 1)
                    gate(c)
                    lo(2, c + base[2])
                hl_sub(NCH - 1)

            squared = [0]

            def squares():
                squared[0] += 2
                dve.wait_ge(ssq_ready, squared[0])

            def post(m, name, weight):
                squares()
                rsqrt(rr[:, RY, :], ssq[:, RY, :], T, 1.0 / D)
                if weight != 1.0:
                    link(dve.tensor_scalar(rr[:, RY, :], rr[:, RY, :], weight, None, ALU.mult))
                g = gain(name)
                for t in range(T):
                    link(dve.scalar_tensor_tensor(out=xg[:, t, :],
                                                  in0=ps[:, 2 * t:2 * t + 2, :].rearrange("p b n -> p (b n)"),
                                                  scalar=rr[:, RY, t:t + 1], in1=g, op0=ALU.mult, op1=ALU.mult))
                    dve.tensor_tensor(res[:, t, :], res[:, t, :], xg[:, t, :], ALU.add).then_inc(res_ready, 1)
                dve.wait_ge(res_ready, 2 * (m + 1))

            def pre_raw(name, factor=True):
                g = gain(name)
                for t in range(T):
                    dve.tensor_tensor(xg[:, t, :], res[:, t, :], g, ALU.mult).then_inc(xg_ready, 1)

            def factor(f=None):
                squares()
                rsqrt(rr[:, RX, :], ssq[:, RX, :], T, 1.0 / D)

            def pre_normed(name):
                factor()
                g = gain(name)
                for t in range(T):
                    dve.scalar_tensor_tensor(out=xg[:, t, :], in0=res[:, t, :], scalar=rr[:, RX, t:t + 1], in1=g,
                                             op0=ALU.mult, op1=ALU.mult).then_inc(xg_ready, 1)

            def mem_normed(layer):
                g = gain(f"mem{layer}")
                for t in range(T):
                    dve.scalar_tensor_tensor(out=mx[:, t, :], in0=mx[:, t, :], scalar=rr[:, RM, t:t + 1], in1=g,
                                             op0=ALU.mult, op1=ALU.mult).then_inc(xg_ready, 1)

            def two(b):
                return ps[:, b:b + 2, :].rearrange("p b n -> p (b n)")

            def heads(ap, h):
                return ap.rearrange("p (h s) -> p h s", h=h)

            def rotate(dst, src, t, heads_n, tmp):
                half = HD // 2
                c = cosw[:, t, :].unsqueeze(1).unsqueeze(1).to_broadcast([P, heads_n, 2, half])
                s = [sinw[:, t, i, :].unsqueeze(1).to_broadcast([P, heads_n, half]) for i in range(2)]
                dve.tensor_tensor(tmp[:, :, 0, :], src[:, :, 1, :], s[0], ALU.mult)
                dve.tensor_tensor(tmp[:, :, 1, :], src[:, :, 0, :], s[1], ALU.mult)
                link(dve.tensor_tensor(dst, src, c, ALU.mult))
                return dve.tensor_tensor(dst, dst, tmp, ALU.add)

            def mem_maxima(t, b, layer):
                dve.wait_ge(ms_done, T * layer + t + 1)
                link(dve.tensor_reduce(smx[:, 6, 4 * t:4 * t + MH_], heads(two(b), MH_), AX.X, ALU.max))
                dve.tensor_scalar(smx[:, t, 0:MH_], smx[:, 6, 4 * t:4 * t + MH_], -MD ** -0.5, None, ALU.mult).then_inc(ms_max, 1)

            def mem_probs(t, layer):
                dve.wait_ge(mp_raw, MH_ * (T * layer + t + 1))
                link(dve.reciprocal(smx[:, 7, 4 * t:4 * t + MH_], smx[:, 2 + t, 0:MH_]))
                dve.tensor_tensor(heads(pm[t], MH_), heads(pm[t], MH_),
                                  smx[:, 7, 4 * t:4 * t + MH_].unsqueeze(2).to_broadcast([P, MH_, S]), ALU.mult)\
                   .then_inc(mp_ready, 1)

            def mem_turned(b, layer):
                dve.wait_ge(mp_turned, T * layer + 2)
                dve.tensor_copy(pmt.rearrange("p j (h s) -> p j h s", h=MH_)[:, :, :, P:2 * P],
                                ps[:, b:b + 2, :].rearrange("p j (h s) -> p j h s", h=MH_)).then_inc(mpt_ready, 1)

            def mem_lo(b, layer):
                dve.wait_ge(mo_hi, layer + 1)
                dve.tensor_tensor(ml[:, 0:4, :], heads(two(b), MH_), mh[:, 0:4, :].bitcast(F32),
                                  ALU.subtract).then_inc(mo_lo, 1)

            def gla():
                used(dve, ("ga", 0))
                dve.tensor_copy(glr, ps[0:RANK, 4, 0:S]).then_inc(glr_ready, 1)
                dve.wait_ge(z_done, 1)
                z, nab, cum = kst, sc[:, 1, :], am
                for h in range(GH):
                    link(dve.tensor_scalar(z[:, h * S:(h + 1) * S], ps[:, h // 2, (h % 2) * S:(h % 2 + 1) * S],
                                           bg[:, h:h + 1], None, ALU.add))
                dve.scalar_tensor_tensor(out=nab, in0=z, scalar=-1.0, in1=z, op0=ALU.mult, op1=ALU.min)\
                   .then_inc(zb_ready, 1)
                for e in range(2):
                    dve.memset(qe[e], 0.0)
                dve.wait_ge(ln_ready, 1)
                link(dve.scalar_tensor_tensor(out=z, in0=z, scalar=0.0, in1=nab, op0=ALU.min, op1=ALU.subtract))
                link(dve.tensor_tensor_scan(cum, cmask, z, 0.0, ALU.mult, ALU.add))
                cv = cum.rearrange("p (c j) -> p c j", j=CHUNK)
                total = cv[:, :, CHUNK - 1:CHUNK].to_broadcast([P, GH * 4, CHUNK])
                dve.scalar_tensor_tensor(out=qdn.rearrange("p (c j) -> p c j", j=CHUNK), in0=total, scalar=0.5,
                                         in1=cv, op0=ALU.mult, op1=ALU.subtract).then_inc(cum_ready, 1)
                dve.tensor_tensor(kst.rearrange("p (c j) -> p c j", j=CHUNK), total, cv, ALU.subtract)\
                   .then_inc(cum_ready, 1)
                dve.wait_ge(decay_ready, 3)
                used(dve, ("ka", 1))
                dve.tensor_tensor(kdn, two(2), qdn, ALU.mult)
                dve.tensor_tensor(kup, two(2), qup, ALU.mult)
                link(dve.tensor_tensor(kst, two(2), kst, ALU.mult))
                dve.engine_nop().then_inc(k_taken, 1)
                dve.wait_ge(decay_ready, 5)
                used(dve, ("qa", 1))
                for e in range(2):
                    at = np.s_[:, :, e * CHUNK:(e + 1) * CHUNK]
                    link(dve.scalar_tensor_tensor(out=qe[e].rearrange("p (x j) -> p x j", j=P)[at],
                                                  in0=two(6).rearrange("p (x j) -> p x j", j=P)[at], scalar=DK ** -0.5,
                                                  in1=cum.rearrange("p (x j) -> p x j", j=P)[at],
                                                  op0=ALU.mult, op1=ALU.mult))
                dve.scalar_tensor_tensor(out=qdn, in0=two(6), scalar=DK ** -0.5, in1=qdn, op0=ALU.mult, op1=ALU.mult)
                link(dve.memset(am, 0.0))
                dve.scalar_tensor_tensor(out=qup, in0=two(6), scalar=DK ** -0.5, in1=qup, op0=ALU.mult, op1=ALU.mult)\
                   .then_inc(q_taken, 1)

                def take_scores(t):
                    dve.wait_ge(a_done, t + 1)
                    dst = heads(am[:, t * GH * P:(t + 1) * GH * P], GH)
                    for b, mask in ((6, past), (7, fut)):
                        link(dve.copy_predicated(dst, mask[:].bitcast(I32).unsqueeze(1).to_broadcast([P, GH, P]),
                                                 heads(ps[:, b, :], GH)))
                    dve.engine_nop().then_inc(a_taken, 1)

                take_scores(0)
                take_scores(1)
                dve.wait_ge(kv_done, 1)
                dve.tensor_copy(state[1], two(4)).then_inc(s_ready, 1)
                dve.wait_ge(s_ready, 1)

                def next_state(n, b):
                    dve.wait_ge(kv_done, n + 1)
                    for h in range(GH):
                        at = np.s_[:, h * DV:(h + 1) * DV]
                        last = dve.scalar_tensor_tensor(out=state[n + 1][at], in0=state[n][at],
                                                        scalar=dec[:, h, n:n + 1], in1=two(b)[at],
                                                        op0=ALU.mult, op1=ALU.add)
                        if h < GH - 1:
                            link(last)
                    last.then_inc(s_ready, 1)
                    dve.wait_ge(s_ready, n + 1)

                next_state(1, 6)
                next_state(2, 4)
                for i in range(2):
                    dve.wait_ge(silr_ready, i + 1)
                    for t in range(T):
                        link(dve.tensor_tensor(heads(gs[:, t, i * 512:(i + 1) * 512], 2),
                                               heads(gs[:, t, i * 512:(i + 1) * 512], 2),
                                               glag[:].unsqueeze(1).to_broadcast([P, 2, DV]), ALU.mult))
                mem_maxima(0, 0, 0)
                mem_maxima(1, 2, 0)
                mem_probs(0, 0)
                mem_probs(1, 0)
                dve.wait_ge(osq_ready, T * GH)
                rsqrt(rsg[:], ssg[:], T * GH, 1.0 / DV)
                for t, b in ((0, 6), (1, 4)):
                    for h in range(GH):
                        at = np.s_[:, h * DV:(h + 1) * DV]
                        link(dve.scalar_tensor_tensor(out=gs[:, t, :][at], in0=two(b)[at],
                                                      scalar=rsg[:, t * GH + h:t * GH + h + 1], in1=gs[:, t, :][at],
                                                      op0=ALU.mult, op1=ALU.mult))
                    dve.engine_nop().then_inc(on_ready, 1)
                mem_turned(2, 0)
                mem_lo(0, 0)
                for t, b in ((0, 6), (1, 4)):
                    for j in range(2):
                        dve.wait_ge(oh_ready, 2 * t + j + 1)
                        at = np.s_[:, 4 * j:4 * j + 4, t * P:(t + 1) * P]
                        dve.tensor_tensor(xl[at], ps[:, b + j, :].rearrange("p (k s) -> p k s", k=4),
                                          xh[at].bitcast(F32), ALU.subtract).then_inc(ol_ready, 1)

            def window_kv():
                used(dve, ("kv", 0))
                for t in range(T):
                    src = ps[:, 7, t * S:(t + 1) * S]
                    link(dve.tensor_scalar(sc[:, 0, 0:2 * HD], src[:, 0:2 * HD], rr[:, RX, t:t + 1], None, ALU.mult))
                    dve.tensor_scalar(vs[:, t, :], src[:, 2 * HD:4 * HD], rr[:, RX, t:t + 1], None, ALU.mult)\
                       .then_inc(vs_ready, 1)
                    link(rotate(sc[:, 0, 256:256 + 2 * HD].rearrange("p (h a j) -> p h a j", h=2, a=2),
                                sc[:, 0, 0:2 * HD].rearrange("p (h a j) -> p h a j", h=2, a=2), t, 2,
                                sc[:, 0, 512:512 + 2 * HD].rearrange("p (h a j) -> p h a j", h=2, a=2)))
                    for twice in range(2):
                        link(dve.tensor_copy(gs[:, 0, t * 2 * P:(t + 1) * 2 * P]
                                             .rearrange("p (h w d) -> p h w d", h=2, w=2)[:, :, twice, :],
                                             sc[:, 0, 256:256 + 2 * HD].rearrange("p (h d) -> p h d", h=2)))
                dve.engine_nop().then_inc(kr_ready, 1)
                dve.wait_ge(vs_ready, 2)
                dve.tensor_copy(vsh[:], vs[64:128, 0, :]).then_inc(vs_ready, 1)

            def window():
                dve.wait_ge(sin_ready, 2)
                for i, (b, t) in enumerate(((0, 0), (1, 1), (2, 0), (3, 1))):
                    used(dve, (f"qb{i // 2}", 1))
                    v = "p (h a j) -> p h a j"
                    rotate(gs[:, t, (i // 2) * 512:(i // 2 + 1) * 512].rearrange(v, h=8, a=2),
                           ps[:, b, :].rearrange(v, h=8, a=2), t, 8,
                           sc[:, i % 2 * 6, 0:512].rearrange(v, h=8, a=2)).then_inc(qr_ready, 1)
                mem_maxima(0, 4, 1)
                mem_maxima(1, 2, 1)
                mem_probs(0, 1)
                mem_probs(1, 1)
                mem_turned(2, 1)
                mem_lo(4, 1)

                def take_scores(s):
                    g, r, t = GROUPS[s]
                    n = KEYS[t]
                    dve.wait_ge(sw_done, s + 1)
                    dst = wsc[t].rearrange("p (h k) -> p h k", h=HG)
                    mask = (band0, band1)[t]
                    if t == 0:
                        link(dve.scalar_tensor_tensor(out=dst, in0=heads(ps[:, 0, :], HG), scalar=HD ** -0.5,
                                                      in1=mask[:].unsqueeze(1).to_broadcast([P, HG, n]),
                                                      op0=ALU.mult, op1=ALU.add))
                    else:
                        for j in range(2):
                            link(dve.scalar_tensor_tensor(out=dst[:, 2 * j:2 * j + 2, :],
                                                          in0=heads(ps[:, 1 + j, 0:2 * n], 2), scalar=HD ** -0.5,
                                                          in1=mask[:].unsqueeze(1).to_broadcast([P, 2, n]),
                                                          op0=ALU.mult, op1=ALU.add))
                    dve.engine_nop().then_inc(sw_taken, 1)
                    snk = sink[:].rearrange("p (g i r) -> p g i r", g=2, r=2)[:, g, :, r]
                    link(dve.tensor_reduce(smx[:, 4 * t + 3, 0:HG], dst, AX.X, ALU.max))
                    link(dve.tensor_tensor(smx[:, 4 * t + 3, 0:HG], smx[:, 4 * t + 3, 0:HG], snk, ALU.max))
                    link(dve.tensor_tensor(smx[:, 4 * t + 2, 0:HG], snk, smx[:, 4 * t + 3, 0:HG], ALU.subtract))
                    dve.tensor_scalar(smx[:, 4 * t, 0:HG], smx[:, 4 * t + 3, 0:HG], -1.0, None, ALU.mult)\
                       .then_inc(sw_max, 1)

                def probs(s):
                    g, r, t = GROUPS[s]
                    dve.wait_ge(wp_raw, (HG + 1) * (s + 1))
                    link(dve.tensor_tensor(smx[:, 4 * t + 1, 4:8], smx[:, 4 * t + 1, 0:4], smx[:, 4 * t + 2, 0:4],
                                           ALU.add))
                    link(dve.reciprocal(smx[:, 4 * t + 3, 4:8], smx[:, 4 * t + 1, 4:8]))
                    p = wsc[t].rearrange("p (h k) -> p h k", h=HG)
                    dve.tensor_tensor(p, p, smx[:, 4 * t + 3, 4:8].unsqueeze(2).to_broadcast([P, HG, KEYS[t]]),
                                      ALU.mult).then_inc(wp_ready, 1)

                def take_out(s):
                    g, r, t = GROUPS[s]
                    dve.wait_ge(pv_done, s + 1)
                    dve.tensor_copy(of[r * HD:(r + 1) * HD, 4 * g:4 * g + 4, t * P:(t + 1) * P],
                                    heads(ps[0:HD, 6 + t, :], HG)).then_inc(of_ready, 1)

                def output_lo(g):
                    dve.wait_ge(oh_ready, 5 + g)
                    dve.tensor_tensor(xl[:, 4 * g:4 * g + 4, :], of[:, 4 * g:4 * g + 4, :],
                                      xh[:, 4 * g:4 * g + 4, :].bitcast(F32), ALU.subtract).then_inc(ol_ready, 1)

                for s in range(len(GROUPS) + 2):
                    if s < len(GROUPS):
                        if s >= 2:
                            dve.wait_ge(wp_turned, s - 1)
                        take_scores(s)
                    if 1 <= s <= len(GROUPS):
                        probs(s - 1)
                    if s >= 2:
                        take_out(s - 2)
                    if s == 6:
                        output_lo(0)
                output_lo(1)

            def angles():
                dve.wait_ge(small_in, 16 * 5)
                dve.wait_ge(const_ready, 2)
                link(dve.tensor_copy(posf[:], posi[:]))
                flat = [ang[:, i].rearrange("p t j -> p (t j)") for i in range(4)]
                a, k, kh, kl = flat
                for t in range(T):
                    link(dve.tensor_scalar(ang[:, 0, t, :], invf[:], posf[:, t:t + 1], None, ALU.mult))
                link(dve.tensor_scalar(k, a, 1.0 / TWO_PI, None, ALU.mult))
                big = 1.5 * 2.0 ** 23
                link(dve.tensor_scalar(k, k, big, None, ALU.add))
                link(dve.tensor_scalar(k, k, -big, None, ALU.add))
                link(dve.tensor_scalar(kh, k, big * 4096.0, None, ALU.add))
                link(dve.tensor_scalar(kh, kh, -big * 4096.0, None, ALU.add))
                link(dve.tensor_tensor(kl, k, kh, ALU.subtract))
                for part in parts_of(TWO_PI, 12, 4):
                    for n in (kh, kl):
                        link(dve.scalar_tensor_tensor(out=a, in0=n, scalar=-part, in1=a, op0=ALU.mult, op1=ALU.add))
                link(dve.tensor_scalar(a, a, PI_BELOW, -PI_BELOW, ALU.min, ALU.max))
                link(dve.scalar_tensor_tensor(out=k, in0=a, scalar=-1.0, in1=a, op0=ALU.mult, op1=ALU.min))
                dve.tensor_scalar(k, k, float(np.pi / 2), None, ALU.add).then_inc(ang_ready, 1)
                dve.wait_ge(sin_ready, 1)
                link(dve.tensor_scalar(sinw[:, :, 0, :], sinw[:, :, 1, :], -1.0, None, ALU.mult))

            squares()
            rsqrt(rr[:, RM, :], ssq[:, RM, :], T, 1.0 / D)
            mem_normed(0)
            pre_raw("pre0")
            turned_lo("mem0", mh, ml)
            turned_lo("x0", xh, xl)
            factor()
            dve.engine_nop().then_inc(rx_ready, 1)
            angles()
            ffn(0)
            post(0, "post1", 0.5)
            pre_normed("pre1")
            turned_lo("x1", xh, xl)
            gla()
            post(1, "post2", 1.0)
            pre_raw("pre2")
            factor()
            dve.engine_nop().then_inc(rx_ready, 1)
            turned_lo("x2", xh, xl)
            ffn(1)
            post(2, "post3", 0.5)
            pre_raw("kv")
            factor()
            dve.engine_nop().then_inc(rx_ready, 1)
            turned_lo("kv", mh, ml)
            pre_raw("pre3")
            turned_lo("x3", xh, xl)
            dve.wait_ge(sin_ready, 2)
            window_kv()
            dve.wait_ge(mem_in, 32)
            mem_normed(1)

            def between():
                turned_lo("mem1", mh, ml)

            ffn(2, between)
            post(3, "post4", 0.5)
            pre_normed("pre4")
            turned_lo("x4", xh, xl)
            window()
            post(4, "post5", 1.0)
            pre_raw("pre5")
            factor()
            dve.engine_nop().then_inc(rx_ready, 1)
            turned_lo("x5", xh, xl)
            ffn(3)
            post(5, "post6", 0.5)


_INS = ["x", "mem", "positions", "norm_g", "w_ffn_in", "w_ffn_out", "mem_norm_g", "w_mem_kv", "w_in_a",
        "w_gate_up", "b_gate", "gla_norm_g", "w_out_a", "kv_norm_g", "w_kv", "w_in_b", "sinks", "w_out_b"]


def kernel(**inputs):
    import numpy as _np
    import concourse.bacc as _bacc
    from concourse import mybir as _mybir
    from concourse.bass_utils import run_bass_kernel_spmd as _run

    nc = _bacc.Bacc("TRN2", target_bir_lowering=False, num_devices=1)
    arrays, args = {}, []
    for name in _INS:
        a = _np.ascontiguousarray(inputs[name])
        arrays[f"in_{name}"] = a
        args.append(nc.dram_tensor(f"in_{name}", a.shape, _mybir.dt.from_np(a.dtype), kind="ExternalInput").ap())
    args.append(nc.dram_tensor("out_0", inputs["x"].shape, F32, kind="ExternalOutput").ap())
    hybrid_kernel(nc, *args)
    r = _run(nc, [arrays], core_ids=[0])
    return r.results[0]["out_0"]
```

```python
from contextlib import ExitStack

import numpy as np

import concourse.bass as bass
from concourse import mybir

F32 = mybir.dt.float32
F32R = mybir.dt.float32r
I32 = mybir.dt.int32
ALU = mybir.AluOpType
ACT = mybir.ActivationFunctionType
AX = mybir.AxisListType

P = 128
EPS = 1e-6
NEG_INF = -1e30
ROPE_THETA = 10000.0
TAU = 16.0
CHUNK = 64
RSQRT_MAGIC = 0x5F3759DF
TWO_PI = 2.0 * np.pi
PI_BELOW = 3.1415925


def parts_of(value, bits, count):
    parts = []
    for _ in range(count):
        exponent = int(np.floor(np.log2(abs(value))))
        step = 2.0 ** (exponent - bits + 1)
        part = float(np.floor(value / step) * step)
        parts.append(part)
        value -= part
    return parts


def hybrid_kernel(nc, x, mem, positions, norm_g, w_ffn_in, w_ffn_out, mem_norm_g, w_mem_kv,
                  w_in_a, w_gate_up, b_gate, gla_norm_g, w_out_a, kv_norm_g, w_kv, w_in_b, sinks, w_out_b, out):
    _, S, D = x.shape
    F = w_ffn_out.shape[2]
    T = S // P
    K = D // P
    FC = 256
    NCH = F // FC
    GH, DK, DV = 4, D // 8, D // 4
    KW, VW = GH * DK, GH * DV
    RANK = w_gate_up.shape[1]
    MH_, MD = 4, 128
    MW = MH_ * MD
    HQ, HD = 16, 64
    COL_K, COL_V, COL_R = KW, 2 * KW, 2 * KW + VW
    COL_G = COL_R + VW
    COL_QM = COL_G + RANK
    UNIT = 2048
    inv_freq = np.power(np.float32(ROPE_THETA),
                        -np.arange(HD // 2, dtype=np.float32) * np.float32(2.0 / HD)).astype(np.float32)
    assert T == 2 and K == 8 and F % FC == 0 and x.shape[0] == 1

    def cols(w, k0, nk, c0, n):
        return w.rearrange("(k p) n -> p k n", p=P)[:, k0:k0 + nk, c0:c0 + n]

    def halves(name, w, c0):
        return [((name, i), cols(w, 4 * i, 4, c0, 512)) for i in range(2)]

    def rows(name, w, tiles):
        return [((name, k), cols(w, k, 2, 0, D)) for k in tiles]

    wa, woa, wb, wob = w_in_a[0], w_out_a[0], w_in_b[0], w_out_b[0]
    OT_A, OT_B = VW // P, HQ * HD // P
    SEG_A = (halves("mk0", w_mem_kv[0], 0) + halves("mv0", w_mem_kv[0], MW)
             + [(("ga", 0), cols(wa, 0, K, COL_G, P))]
             + halves("ka", wa, COL_K) + halves("qa", wa, 0) + halves("qma", wa, COL_QM)
             + halves("va0", wa, COL_V) + halves("va1", wa, COL_V + 512)
             + halves("ra0", wa, COL_R) + halves("ra1", wa, COL_R + 512)
             + rows("oa", woa, range(OT_A, OT_A + 4, 2)) + rows("oa", woa, range(0, OT_A, 2)))
    SEG_KV = [(("kv", 0), cols(w_kv, 0, K, 0, 256))]
    SEG_B = (halves("mk1", w_mem_kv[1], 0) + halves("mv1", w_mem_kv[1], MW)
             + halves("qmb", wb, HQ * HD) + halves("qb0", wb, 0) + halves("qb1", wb, 512)
             + rows("ob", wob, range(OT_B, OT_B + 4, 2)) + rows("ob", wob, range(0, OT_B, 2)))
    unit = {}
    ffn_base = []
    FFN_USES = (NCH + 1, NCH, NCH - 1)
    uses = [0, 0, 0]
    for seg in (0, SEG_A, 0, SEG_KV, 0, SEG_B, 0):
        if seg == 0:
            ffn_base.append(tuple(uses))
            uses = [u + v for u, v in zip(uses, FFN_USES)]
        else:
            for n, (name, _) in enumerate(seg):
                slot = 2 if seg is SEG_KV else (n + 1) % 3
                unit[name] = (slot, uses[slot])
                uses[slot] += 1

    GAINS = [("pre0", norm_g[0, 0:1, :]), ("mem0", mem_norm_g[0:1, :]),
             ("post1", norm_g[0, 1:2, :]), ("pre1", norm_g[0, 2:3, :]),
             ("post2", norm_g[0, 3:4, :]), ("pre2", norm_g[0, 4:5, :]),
             ("post3", norm_g[0, 5:6, :]), ("pre3", norm_g[1, 0:1, :]), ("kv", kv_norm_g.rearrange("(a d) -> a d", a=1)),
             ("mem1", mem_norm_g[1:2, :]),
             ("post4", norm_g[1, 1:2, :]), ("pre4", norm_g[1, 2:3, :]),
             ("post5", norm_g[1, 3:4, :]), ("pre5", norm_g[1, 4:5, :]),
             ("post6", norm_g[1, 5:6, :])]
    NG = 3
    gain_at = {name: i for i, (name, _) in enumerate(GAINS)}
    TURNS = ["x0", "mem0", "x1", "x2", "x3", "kv", "mem1", "x4", "x5"]
    turn_at = {name: i for i, name in enumerate(TURNS)}

    with ExitStack() as ctx:
        def sb(name, shape, dt=F32):
            return ctx.enter_context(nc.sbuf_tensor(name, shape, dt))

        def sem(name):
            return ctx.enter_context(nc.semaphore(name))

        ps = ctx.enter_context(nc.psum_tensor("ps", [P, 8, 512], F32))

        raw = sb("raw", [P, 3, UNIT])
        w_hi = sb("w_hi", [P, 3, UNIT], F32R)
        w_lo = sb("w_lo", [P, 3, UNIT], F32R)
        res = sb("res", [P, T, D])
        xg = sb("xg", [P, T, D])
        xh = sb("xh", [P, K, S], F32R)
        xl = sb("xl", [P, K, S], F32R)
        mh = sb("mh", [P, K, S], F32R)
        ml = sb("ml", [P, K, S], F32R)
        hh = sb("hh", [P, 2, S], F32R)
        hl = sb("hl", [P, 2, S], F32R)
        kmem = sb("kmem", [P, MH_, S])
        vmem = sb("vmem", [P, T, MW])
        qmem = sb("qmem", [P, MH_, S])
        gains = sb("gains", [P, NG, D])
        sc = sb("sc", [P, 10, 1024])
        gs = sb("gs", [P, T, D])
        kt = sb("kt", [P, 2, S])
        vs = sb("vs", [P, T, 2, 2, HD])
        wsm = sb("wsm", [P, 4, 6, 4])
        ident = sb("ident", [P, P])
        past = sb("past", [P, P])
        fut = sb("fut", [P, P])
        band0 = sb("band0", [P, 128])
        band1 = sb("band1", [P, 192])
        wgu = sb("wgu", [RANK, KW])
        bg = sb("bg", [P, GH])
        sink = sb("sink", [P, HQ])
        nsink = sb("nsink", [P, HQ])
        cosw = sb("cosw", [P, T, HD // 2])
        sinw = sb("sinw", [P, T, 2, HD // 2])
        posi = sb("posi", [P, T], I32)
        posf = sb("posf", [P, T])
        invf = sb("invf", [P, HD // 2])
        glag = sb("glag", [P, DV])
        ssq = sb("ssq", [P, 4, 2])
        rr = sb("rr", [P, 4, 2])
        nw = sb("nw", [P, 4, 8])
        smx = sb("smx", [P, 8, 8])
        dec = sb("dec", [P, GH, 4])
        ssg = sb("ssg", [P, T * GH])
        rsg = sb("rsg", [P, T * GH])
        RM, RX, RY = 0, 1, 2

        kst, qdn, qup, am, kdn, kup = (sc[:, i, :] for i in range(6))
        state = [None, sc[:, 1, :], sc[:, 2, :], sc[:, 0, :]]
        qe = [sc[:, 6, :], sc[:, 7, :]]
        ksk = sc[:, 8, :]
        cmask = sc[:, 8, :]
        glr = sc[0:RANK, 6, 0:S]
        sil = sc[:, 9, 0:512].rearrange("p (t f) -> p t f", t=T)
        hid = sc[:, 9, 512:1024].rearrange("p (t f) -> p t f", t=T)
        ang = sc[:, 9, 0:4 * T * HD // 2].rearrange("p (i t j) -> p i t j", i=4, t=T)
        junk = [sc[:, 4, :], sc[:, 5, :]]
        mx = sc[:, 6:8, :]
        pm = [sc[:, 4, :], sc[:, 5, :]]
        qt = sc[:, 1:3, :].rearrange("p a n -> p (a n)")
        wsc = [sc[:, 3, 0:512], sc[:, 6, 0:768], sc[:, 3, 512:1024], sc[:, 4, 0:768]]
        wpt = [(sc[:, 7, 0:512],), (sc[0:CHUNK, 7, 512:1024], sc[:, 0, 0:512]),
               (sc[:, 5, 0:512],), (sc[0:CHUNK, 5, 512:1024], sc[:, 8, 0:512])]
        kw = sc[:, 0, 0:768]
        vsh = sc[0:CHUNK, 0, 768:1024].rearrange("p (g w d) -> p g w d", g=2, w=2)
        pmt = sc[:, 8:10, :]

        landed = [sem(f"landed{i}") for i in range(3)]
        hi_ready = [sem(f"hi_ready{i}") for i in range(3)]
        lo_ready = [sem(f"lo_ready{i}") for i in range(3)]
        w_used = [sem(f"w_used{i}") for i in range(3)]
        gain_in = [sem(f"gain_in{i}") for i in range(NG)]
        res_in = [sem(f"res_in{t}") for t in range(T)]
        mem_in = sem("mem_in")
        small_in = sem("small_in")
        const_ready = sem("const_ready")
        pool_step = sem("pool_step")
        dve_step = sem("dve_step")
        act_step = sem("act_step")
        xg_ready = sem("xg_ready")
        turned = sem("turned")
        rx_ready = sem("rx_ready")
        th_ready = sem("th_ready")
        tl_ready = sem("tl_ready")
        ssq_ready = sem("ssq_ready")
        res_ready = sem("res_ready")
        up_done = sem("up_done")
        sil_ready = sem("sil_ready")
        gated = sem("gated")
        h_turned = sem("h_turned")
        hh_ready = sem("hh_ready")
        hl_ready = sem("hl_ready")
        y_done = sem("y_done")
        out_done = sem("out_done")
        ang_ready = sem("ang_ready")
        sin_ready = sem("sin_ready")
        kmem_ready = sem("kmem_ready")
        vmem_ready = sem("vmem_ready")
        qmem_ready = sem("qmem_ready")
        ms_done = sem("ms_done")
        ms_max = sem("ms_max")
        mp_raw = sem("mp_raw")
        mp_ready = sem("mp_ready")
        mp_turned = sem("mp_turned")
        mpt_ready = sem("mpt_ready")
        mo_done = sem("mo_done")
        mo_hi = sem("mo_hi")
        mo_lo = sem("mo_lo")
        glr_ready = sem("glr_ready")
        z_done = sem("z_done")
        zb_ready = sem("zb_ready")
        ln_ready = sem("ln_ready")
        cum_ready = sem("cum_ready")
        decay_ready = sem("decay_ready")
        k_taken = sem("k_taken")
        q_taken = sem("q_taken")
        v_ready = sem("v_ready")
        a_done = sem("a_done")
        a_taken = sem("a_taken")
        kst_turned = sem("kst_turned")
        ksk_ready = sem("ksk_ready")
        kv_done = sem("kv_done")
        s_ready = sem("s_ready")
        silr_ready = sem("silr_ready")
        o_done = sem("o_done")
        osq_ready = sem("osq_ready")
        on_ready = sem("on_ready")
        o_turned = sem("o_turned")
        oh_ready = sem("oh_ready")
        ol_ready = sem("ol_ready")
        kr_ready = sem("kr_ready")
        k_turned = sem("k_turned")
        kt_ready = sem("kt_ready")
        vs_ready = sem("vs_ready")
        qr_ready = sem("qr_ready")
        q_turned = sem("q_turned")
        qt_ready = sem("qt_ready")
        sw_done = sem("sw_done")
        sw_taken = sem("sw_taken")
        sw_max = sem("sw_max")
        wp_raw = sem("wp_raw")
        wp_ready = sem("wp_ready")
        wp_turned = sem("wp_turned")
        wpt_ready = sem("wpt_ready")
        pv_done = sem("pv_done")

        block = ctx.enter_context(nc.Block())

        def gain_free(i):
            name = GAINS[i][0]
            if name[:4] == "post":
                return res_ready, 2 * int(name[4:])
            turn_name = {"pre": "x" + name[3:], "mem": name, "kv": "kv"}[name[:3] if name != "kv" else "kv"]
            return xg_ready, 2 * (turn_at[turn_name] + 1)

        def landings(slot, n):
            two = sum(min(max(n - b[slot], 0), NCH) for b in ffn_base) if slot < 2 else 0
            return 16 * (n + two)

        SIZE = {name: src.shape[1] * src.shape[2] for seg in (SEG_A, SEG_KV, SEG_B) for name, src in seg}
        NAMES = [name for seg in (SEG_A, SEG_KV, SEG_B) for name, _ in seg]

        def used(eng, name):
            slot, n = unit[name]
            eng.wait_ge(w_used[slot], n + 1)

        GROUPS = [(g, r, t) for g in range(2) for r in range(2) for t in range(T)]
        KEYS = [128, 192]
        HG = 4

        @block.sync
        def _(sp):
            def load(name, src):
                slot, n = unit[name]
                if n:
                    sp.wait_ge(lo_ready[slot], n)
                nk, w = src.shape[1], src.shape[2]
                dst = raw[:, slot, 0:nk * w].rearrange("p (k n) -> p k n", k=nk)
                sp.dma_start(dst, src).then_inc(landed[slot], 16)

            def ffn_loads(f):
                w_in = w_ffn_in[f // 2, f % 2].rearrange("(k p) (s n) -> p k s n", p=P, s=2)
                w_out = w_ffn_out[f // 2, f % 2].rearrange("(c p) n -> p c n", p=P)
                base = ffn_base[f]

                def up(c, h, first=False):
                    if not first:
                        sp.wait_ge(lo_ready[h], c + base[h])
                    dst = raw[:, h, :].rearrange("p (k s n) -> p k s n", k=4, s=2)
                    for s in range(2):
                        sp.dma_start(dst[:, :, s, :], w_in[:, 4 * h:4 * h + 4, s, bass.ds(c * FC, FC)])\
                          .then_inc(landed[h], 16)

                def down(c, first=False, slot=2):
                    if not first:
                        sp.wait_ge(lo_ready[slot], (c if slot else NCH) + base[slot])
                    sp.dma_start(raw[:, slot, :].rearrange("p (k n) -> p k n", k=2),
                                 w_out[:, bass.ds(c * 2, 2), :]).then_inc(landed[slot], 16)

                up(0, 0, first=f == 0)
                if f == 0:
                    sp.dma_start(res[:, 1, :], xv[:, 1, :]).then_inc(res_in[1], 16)
                up(0, 1, first=f == 0)
                if f == 0:
                    sp.dma_start(mx, mem[0].rearrange("(t p) d -> p t d", p=P)).then_inc(mem_in, 16)
                up(1, 0)
                down(0, first=f == 0)
                up(1, 1)
                with sp.Fori(2, NCH) as c:
                    up(c, 0)
                    down(c - 1)
                    up(c, 1)
                down(NCH - 1, slot=0)

            xv = x[0].rearrange("(t p) d -> p t d", p=P)
            sp.dma_start(res[:, 0, :], xv[:, 0, :]).then_inc(res_in[0], 16)
            ffn_loads(0)
            for name, src in SEG_A:
                load(name, src)
            ffn_loads(1)
            for name, src in SEG_KV:
                load(name, src)
            sp.wait_ge(y_done, 2)
            sp.dma_start(mx, mem[0].rearrange("(t p) d -> p t d", p=P)).then_inc(mem_in, 16)
            ffn_loads(2)
            for name, src in SEG_B:
                load(name, src)
            ffn_loads(3)
            ov = out[0].rearrange("(t p) d -> p t d", p=P)
            for t in range(T):
                sp.wait_ge(res_ready, 2 * 5 + t + 1)
                sp.dma_start(ov[:, t, :], res[:, t, :]).then_inc(out_done, 16)
            sp.wait_ge(out_done, 16 * T)

        @block.gpsimd
        def _(pool):
            count = [0]

            def link(ins):
                count[0] += 1
                ins.then_inc(pool_step, 1)
                pool.wait_ge(pool_step, count[0])

            link(pool.memset(ident[:], 0.0))
            pool.affine_select(out=ident[:], in_=ident[:], compare_op=ALU.not_equal, fill=1.0, base=0,
                               pattern=[[-1, P]], channel_multiplier=1).then_inc(const_ready, 1)
            link(pool.memset(past[:], 1.0))
            link(pool.affine_select(out=past[:], in_=past[:], compare_op=ALU.is_ge, fill=0.0, base=0,
                                    pattern=[[1, P]], channel_multiplier=-1))
            link(pool.memset(past[0:64, 64:128], 0.0))
            link(pool.memset(fut[:], 1.0))
            link(pool.affine_select(out=fut[:], in_=fut[:], compare_op=ALU.is_gt, fill=0.0, base=0,
                                    pattern=[[-1, P]], channel_multiplier=1))
            link(pool.memset(fut[64:128, 0:64], 0.0))
            link(pool.memset(band0[:], 0.0))
            link(pool.memset(band0[0:64, 64:128], NEG_INF))
            link(pool.memset(band1[:], 0.0))
            link(pool.memset(band1[0:64, 128:192], NEG_INF))
            link(pool.memset(band1[64:128, 0:64], NEG_INF))
            for i in range(HD // 2):
                pool.memset(invf[:, i:i + 1], float(inv_freq[i]))
            link(pool.memset(cmask, 1.0))
            pool.memset(cmask.rearrange("p (c j) -> p c j", j=CHUNK)[:, :, 0:1], 0.0).then_inc(const_ready, 1)

            def lo(slot, n, size=UNIT):
                pool.wait_ge(hi_ready[slot], n + 1)
                pool.tensor_tensor(w_lo[:, slot, 0:size], raw[:, slot, 0:size], w_hi[:, slot, 0:size].bitcast(F32),
                                   ALU.subtract).then_inc(lo_ready[slot], 1)

            def seg(units):
                for name, src in units:
                    lo(*unit[name], size=SIZE[name])

            def ffn(f):
                if f:
                    lo(0, ffn_base[f][0])
                lo(1, ffn_base[f][1])
                lo(1, ffn_base[f][1] + 1)
                with pool.Fori(2, NCH) as c:
                    for h in range(2):
                        lo(h, c + ffn_base[f][h])

            ffn(0)
            seg(SEG_A)
            ffn(1)
            seg(SEG_KV)
            ffn(2)
            seg(SEG_B)
            ffn(3)

        @block.tensor
        def _(pe):
            mm = nc.tensor.matmul
            x_act, m_act = (xh, xl), (mh, ml)

            def take(slot, n):
                pe.wait_ge(lo_ready[slot], n + 1)

            def three(dst, a, b, at_a, at_b, start, stop, group=False):
                mm(dst, a[0][at_a], b[0][at_b], start=start, stop=False, skip_group_check=group)
                mm(dst, a[0][at_a], b[1][at_b], start=False, stop=False, skip_group_check=group)
                return mm(dst, a[1][at_a], b[0][at_b], start=False, stop=stop, skip_group_check=group)

            def parts(slot, k, n=UNIT):
                return tuple(w[:, slot, 0:n].rearrange("p (k n) -> p k n", k=k) for w in (w_hi, w_lo))

            def turn(name, src, t):
                n = turn_at[name]
                if n == 0 and t == 0:
                    pe.wait_ge(const_ready, 1)
                pe.wait_ge(xg_ready, 2 * n + t + 1)
                if n:
                    pe.wait_ge(tl_ready, 4 * n - 2 + 2 * t)
                for k in range(K):
                    i = nc.tensor.transpose(ps[:, 2 * t + k // 4, (k % 4) * P:(k % 4 + 1) * P],
                                            src[:, t, k * P:(k + 1) * P], ident[:])
                    if k % 4 == 3:
                        i.then_inc(turned, 1)

            def turned_in(name, k, t=T - 1):
                pe.wait_ge(tl_ready, 4 * turn_at[name] + 2 * t + k // 4 + 1)

            def rowwise(name, act, turn_name, banks, between=None):
                for i in range(2):
                    if i and between is not None:
                        between()
                    slot, n = unit[(name, i)]
                    take(slot, n)
                    w = parts(slot, 4)
                    for t in range(T):
                        turned_in(turn_name, 4 * i, t)
                        for k in range(4):
                            last = three(ps[:, banks[t], :], act, w, np.s_[:, 4 * i + k, t * P:(t + 1) * P],
                                         np.s_[:, k, :], start=(i == 0 and k == 0), stop=(i == 1 and k == 3))
                    last.then_inc(w_used[slot], 1)

            def colwise(name, act, turn_name, banks):
                for i in range(2):
                    slot, n = unit[(name, i)]
                    take(slot, n)
                    w = parts(slot, 4)
                    turned_in(turn_name, 4 * i)
                    for k in range(4):
                        for h in range(4):
                            last = three(ps[:, banks[h // 2], (h % 2) * S:(h % 2 + 1) * S], w, act,
                                         np.s_[:, k, h * P:(h + 1) * P], np.s_[:, 4 * i + k, :],
                                         start=(i == 0 and k == 0 and h % 2 == 0), stop=(i == 1 and k == 3),
                                         group=True)
                    last.then_inc(w_used[slot], 1)

            def ffn(f, after_01=None, after_10=None, before_11=None):
                base = ffn_base[f]
                tname = f"x{(0, 2, 3, 5)[f]}"

                def up(c, h, first=False):
                    take(h, c + base[h])
                    w = parts(h, 4)
                    for t in range(T):
                        if h == 0 and not first:
                            pe.wait_ge(gated, c * 2 + (2 * NCH * f - 1 + t))
                        if first and h == 0:
                            if t:
                                turn(tname, xg, t)
                            turned_in(tname, 0, t)
                        for k in range(4):
                            if first and h == 1 and k == 0:
                                turned_in(tname, 4, t)
                            last = three(ps[:, 4 + t, :], x_act, w, np.s_[:, 4 * h + k, t * P:(t + 1) * P],
                                         np.s_[:, k, :], start=(h == 0 and k == 0), stop=(h == 1 and k == 3))
                        if h == 1 and t == 0:
                            last.then_inc(up_done, 1)
                    last.then_inc(w_used[h], 1)

                def turn_h(c):
                    pe.wait_ge(gated, c * 2 + (2 * NCH * f + 2))
                    if f or not isinstance(c, int) or c:
                        pe.wait_ge(hl_ready, c + NCH * f)
                    for j in range(2):
                        for t in range(T):
                            last = nc.tensor.transpose(ps[:, 6, j * S + t * P:j * S + (t + 1) * P],
                                                       hid[:, t, j * P:(j + 1) * P], ident[:])
                    last.then_inc(h_turned, 1)

                def down(c, start=False, stop=False, slot=2):
                    take(slot, (c if slot else NCH) + base[slot])
                    pe.wait_ge(hl_ready, c + (NCH * f + 1))
                    w = parts(slot, 2)
                    for t in range(T):
                        for k in range(2):
                            for n in range(2):
                                last = three(ps[:, 2 * t + n, :], (hh, hl), w, np.s_[:, k, t * P:(t + 1) * P],
                                             np.s_[:, k, n * 512:(n + 1) * 512],
                                             start=(start and k == 0), stop=(stop and k == 1))
                        if stop and t == 0:
                            last.then_inc(y_done, 1)
                    last.then_inc(w_used[slot], 1)

                turn(tname, xg, 0)
                up(0, 0, first=True)
                up(0, 1, first=True)
                if after_01 is not None:
                    after_01()
                up(1, 0)
                if after_10 is not None:
                    after_10()
                turn_h(0)
                if before_11 is not None:
                    before_11()
                up(1, 1)
                if before_11 is not None or after_10 is not None:
                    pe.wait_ge(tl_ready, 4 * (turn_at[f"mem{f // 2}"] + 1))
                down(0, start=True)
                with pe.Fori(2, NCH) as c:
                    up(c, 0)
                    turn_h(c - 1)
                    up(c, 1)
                    down(c - 1)
                turn_h(NCH - 1)
                down(NCH - 1, stop=True, slot=0)

            def mixer_out(name, first_tile, tiles, outputs):
                order = [k for k in range(first_tile, first_tile + 4, 2)] + list(range(0, tiles, 2))
                for i, k0 in enumerate(order):
                    slot, n = unit[(name, k0)]
                    take(slot, n)
                    w = parts(slot, 2)
                    act, at = (m_act, k0 - first_tile) if k0 >= first_tile else (x_act, k0)
                    if k0 < first_tile:
                        pe.wait_ge(ol_ready, outputs(k0))
                    for t in range(T):
                        for k in range(2):
                            for c in range(2):
                                last = three(ps[:, 2 * t + c, :], act, w, np.s_[:, at + k, t * P:(t + 1) * P],
                                             np.s_[:, k, c * 512:(c + 1) * 512],
                                             start=(i == 0 and k == 0), stop=(i == len(order) - 1 and k == 1))
                        if i == len(order) - 1 and t == 0:
                            last.then_inc(y_done, 1)
                    last.then_inc(w_used[slot], 1)

            def mem_scores(t, b):
                for h in range(MH_):
                    last = mm(ps[:, b + h // 2, (h % 2) * S:(h % 2 + 1) * S], qmem[:, h, t * P:(t + 1) * P],
                              kmem[:, h, :], start=True, stop=True)
                last.then_inc(ms_done, 1)

            def mem_turn(t, b, layer):
                pe.wait_ge(mp_ready, T * layer + t + 1)
                for j in range(T):
                    for h in range(MH_):
                        last = nc.tensor.transpose(ps[:, b + j, h * P:(h + 1) * P],
                                                   pm[t][:, h * S + j * P:h * S + (j + 1) * P], ident[:])
                last.then_inc(mp_turned, 1)

            def mem_out(b, layer):
                pe.wait_ge(mpt_ready, T * (layer + 1))
                for h in range(MH_):
                    for j in range(T):
                        last = mm(ps[:, b + h // 2, (h % 2) * S:(h % 2 + 1) * S], vmem[:, j, h * MD:(h + 1) * MD],
                                  pmt[:, j, h * S:(h + 1) * S], start=(j == 0), stop=(j == T - 1))
                last.then_inc(mo_done, 1)

            def gla():
                colwise("mk0", m_act, "mem0", (4, 5))
                turn("x1", xg, 0)
                rowwise("mv0", m_act, "mem0", (6, 7), lambda: turn("x1", xg, 1))
                pe.wait_ge(kmem_ready, 1)
                slot, n = unit[("ga", 0)]
                take(slot, n)
                w = parts(slot, K, K * P)
                turned_in("x1", K - 1)
                for k in range(K):
                    last = three(ps[:, 4, 0:S], w, x_act, np.s_[:, k, :], np.s_[:, k, :],
                                 start=(k == 0), stop=(k == K - 1))
                last.then_inc(w_used[slot], 1)
                pe.wait_ge(glr_ready, 1)
                pe.wait_ge(small_in, 16 * 5)
                for h in range(GH):
                    last = mm(ps[:, h // 2, (h % 2) * S:(h % 2 + 1) * S], wgu[:, h * DK:(h + 1) * DK], glr,
                              start=True, stop=True)
                last.then_inc(z_done, 1)
                colwise("ka", x_act, "x1", (2, 3))
                pe.wait_ge(vmem_ready, 1)
                colwise("qa", x_act, "x1", (6, 7))
                colwise("qma", x_act, "x1", (4, 5))
                pe.wait_ge(zb_ready, 1)
                rowwise("va0", x_act, "x1", (0, 1))
                pe.wait_ge(k_taken, 1)
                rowwise("va1", x_act, "x1", (2, 3))

                def scores(t):
                    if t:
                        pe.wait_ge(a_taken, t)
                    for b, keys, queries in ((6, kdn, qup), (7, kup, qdn)):
                        for h in range(GH):
                            at = np.s_[:, h * S + t * P:h * S + (t + 1) * P]
                            last = mm(ps[:, b, h * P:(h + 1) * P], keys[at], queries[at], start=True, stop=True)
                    last.then_inc(a_done, 1)

                def chunk_kv(n, b):
                    t, at = n // 2, np.s_[(n % 2) * CHUNK:(n % 2 + 1) * CHUNK]
                    for h in range(GH):
                        last = mm(ps[:, b + h // 2, (h % 2) * DV:(h % 2 + 1) * DV],
                                  ksk[at, (t * GH + h) * DK:(t * GH + h + 1) * DK], xg[at, t, h * DV:(h + 1) * DV],
                                  start=True, stop=True)
                    last.then_inc(kv_done, 1)

                pe.wait_ge(q_taken, 1)
                scores(0)
                pe.wait_ge(qmem_ready, 1)
                for t in range(T):
                    for h in range(GH):
                        last = nc.tensor.transpose(ps[:, 4 + t, h * P:(h + 1) * P],
                                                   kst[:, h * S + t * P:h * S + (t + 1) * P], ident[:])
                last.then_inc(kst_turned, 1)
                pe.wait_ge(v_ready, 1)
                rowwise("ra0", x_act, "x1", (0, 1))
                scores(1)
                pe.wait_ge(ksk_ready, 1)
                pe.wait_ge(v_ready, 2)
                chunk_kv(0, 4)
                rowwise("ra1", x_act, "x1", (2, 3))
                pe.wait_ge(a_taken, 2)
                chunk_kv(1, 6)
                pe.wait_ge(s_ready, 1)
                chunk_kv(2, 4)
                pe.wait_ge(silr_ready, 2)
                mem_scores(0, 0)
                mem_scores(1, 2)
                for t, b in ((0, 6), (1, 4)):
                    pe.wait_ge(s_ready, t + 2)
                    for h in range(GH):
                        dst = ps[:, b + h // 2, (h % 2) * DV:(h % 2 + 1) * DV]
                        at = np.s_[:, (t * GH + h) * P:(t * GH + h + 1) * P]
                        mm(dst, am[at], xg[:, t, h * DV:(h + 1) * DV], start=True, stop=False)
                        for e in range(2):
                            if 2 * t + e:
                                last = mm(dst, qe[e][:, h * S + t * P:h * S + (t + 1) * P],
                                          state[2 * t + e][:, h * DV:(h + 1) * DV], start=False, stop=(e == 1))
                    last.then_inc(o_done, 1)
                mem_turn(0, 0, 0)
                mem_turn(1, 2, 0)
                mem_out(0, 0)
                for t, b in ((0, 6), (1, 4)):
                    pe.wait_ge(on_ready, t + 1)
                    for k in range(K):
                        i = nc.tensor.transpose(ps[:, b + k // 4, (k % 4) * P:(k % 4 + 1) * P],
                                                gs[:, t, k * P:(k + 1) * P], ident[:])
                        if k % 4 == 3:
                            i.then_inc(o_turned, 1)
                pe.wait_ge(mo_lo, 1)
                mixer_out("oa", OT_A, OT_A, lambda k: 4)

            def turn_kv():
                for t in range(T):
                    turn("kv", xg, t)

            def window_kv():
                slot, n = unit[("kv", 0)]
                take(slot, n)
                w = parts(slot, K)
                for t in range(T):
                    turned_in("kv", K - 1, t)
                    for k in range(K):
                        last = three(ps[:, 7, t * S:(t + 1) * S], m_act, w, np.s_[:, k, t * P:(t + 1) * P],
                                     np.s_[:, k, :], start=(k == 0), stop=(k == K - 1))
                last.then_inc(w_used[slot], 1)
                turn_memory(1)

            def turn_memory(layer):
                for t in range(T):
                    turn(f"mem{layer}", mx, t)

            def turn_keys():
                pe.wait_ge(kr_ready, 1)
                for g in range(2):
                    for t in range(T):
                        last = nc.tensor.transpose(ps[:, 6, g * S + t * P:g * S + (t + 1) * P],
                                                   gs[:, 0, (t * 2 + g) * P:(t * 2 + g + 1) * P], ident[:])
                last.then_inc(k_turned, 1)

            def window():
                colwise("mk1", m_act, "mem1", (4, 5))
                turn_keys()
                turn("x4", xg, 0)
                pe.wait_ge(kt_ready, 1)
                rowwise("mv1", m_act, "mem1", (6, 7), lambda: turn("x4", xg, 1))
                pe.wait_ge(kmem_ready, 2)
                colwise("qmb", x_act, "x4", (4, 5))
                rowwise("qb0", x_act, "x4", (0, 1))
                pe.wait_ge(qmem_ready, 2)
                mem_scores(0, 4)
                mem_scores(1, 2)
                pe.wait_ge(vmem_ready, 2)
                rowwise("qb1", x_act, "x4", (6, 7))

                def turn_q(i, b):
                    for j in range(2):
                        for t in range(T):
                            last = nc.tensor.transpose(ps[:, b, j * S + t * P:j * S + (t + 1) * P],
                                                       gs[:, t, (i + j) * P:(i + j + 1) * P], ident[:])
                    last.then_inc(q_turned, 1)

                def scores(s):
                    g, r, t = GROUPS[s]
                    pe.wait_ge(qt_ready, 2 * g + 2)
                    if s >= 2:
                        pe.wait_ge(sw_taken, s - 1)
                    n = KEYS[t]
                    for i in range(HG):
                        at = np.s_[r * HD:(r + 1) * HD]
                        dst = ps[:, 0, i * n:(i + 1) * n] if t == 0 else ps[:, 1 + i // 2, (i % 2) * n:(i % 2 + 1) * n]
                        last = mm(dst, qt[at, (g * HG + i) * S + t * P:(g * HG + i) * S + (t + 1) * P],
                                  kt[at, g, S - n if t else 0:S if t else n], start=True, stop=True)
                    last.then_inc(sw_done, 1)

                def turn_p(s):
                    g, r, t = GROUPS[s]
                    pe.wait_ge(wp_ready, s + 1)
                    if s >= 2:
                        pe.wait_ge(wpt_ready, s - 1)
                    src = wsc[s % 4].rearrange("p (h k) -> p h k", h=HG)
                    for i in range(HG):
                        if t == 0:
                            last = nc.tensor.transpose(ps[:, 3, i * P:(i + 1) * P], src[:, i, :], ident[:])
                        else:
                            nc.tensor.transpose(ps[0:CHUNK, 4, i * P:(i + 1) * P], src[:, i, 0:CHUNK], ident[:])
                            last = nc.tensor.transpose(ps[:, 5, i * P:(i + 1) * P], src[:, i, CHUNK:], ident[:])
                    last.then_inc(wp_turned, 1)

                def weigh(s):
                    g, r, t = GROUPS[s]
                    pe.wait_ge(wpt_ready, s + 1)
                    if s >= 2:
                        pe.wait_ge(ol_ready, 4 + s - 1)
                    dst = ps[:, 6 + t, :]
                    values = vs[:, t, g].rearrange("p w d -> p (w d)")
                    if t == 0:
                        last = mm(dst, values, wpt[s % 4][0], start=True, stop=True)
                    else:
                        mm(dst, vsh[:, g].rearrange("p w d -> p (w d)"), wpt[s % 4][0], start=True, stop=False)
                        last = mm(dst, values, wpt[s % 4][1], start=False, stop=True)
                    last.then_inc(pv_done, 1)

                pe.wait_ge(qr_ready, 2)
                turn_q(0, 0)
                turn_q(2, 1)
                mem_turn(0, 4, 1)
                mem_turn(1, 2, 1)
                scores(0)
                pe.wait_ge(mpt_ready, 4)
                scores(1)
                mem_out(4, 1)
                pe.wait_ge(qr_ready, 4)
                turn_q(4, 6)
                turn_q(6, 7)
                n = len(GROUPS)
                for s in range(2, n + 2):
                    if s < n:
                        scores(s)
                    if s == 3:
                        pe.wait_ge(mo_lo, 2)
                    turn_p(s - 2)
                    if s == 3:
                        pe.wait_ge(qt_ready, 4)
                    if s >= 3:
                        weigh(s - 3)
                weigh(n - 1)
                mixer_out("ob", OT_B, OT_B, lambda k: 4 + (4 if k < 4 else 8))

            ffn(0, after_10=lambda: turn_memory(0))
            gla()
            ffn(1)
            ffn(2, after_01=turn_kv, before_11=window_kv)
            window()
            ffn(3)

        @block.scalar
        def _(act):
            act_count = [0]

            def link(ins):
                act_count[0] += 1
                ins.then_inc(act_step, 1)
                act.wait_ge(act_step, act_count[0])

            def gain(name):
                i = gain_at[name]
                if i >= NG:
                    act.wait_ge(*gain_free(i - NG))
                act.dma_start(gains[:, i % NG, :], GAINS[i][1].partition_broadcast(P)).then_inc(gain_in[i % NG], 16)

            def hi(slot, n, size=UNIT, land=None):
                act.wait_ge(landed[slot], landings(slot, n + 1) if land is None else land)
                if not isinstance(n, int) or n:
                    act.wait_ge(w_used[slot], n)
                act.activation(w_hi[:, slot, 0:size], raw[:, slot, 0:size], ACT.Copy).then_inc(hi_ready[slot], 1)

            units = iter(NAMES)

            def hi_next(count=1):
                for _ in range(count):
                    name = next(units)
                    hi(*unit[name], size=SIZE[name])

            squares = [0]

            def square(src, t, what):
                n = squares[0]
                squares[0] += 1
                if n >= 2:
                    act.wait_ge(ssq_ready, n - 1)
                act.activation(junk[n % 2], src, ACT.Square, accum_out=ssq[:, what, t:t + 1]).then_inc(ssq_ready, 1)

            def turned_hi(name, dst, t):
                for j in range(2):
                    act.wait_ge(turned, 4 * turn_at[name] + 2 * t + j + 1)
                    act.activation(dst[:, 4 * j:4 * j + 4, t * P:(t + 1) * P],
                                   ps[:, 2 * t + j, :].rearrange("p (k s) -> p k s", k=4),
                                   ACT.Copy).then_inc(th_ready, 1)

            def ffn_first(f, s):
                hi(s, ffn_base[f][s])

            def ffn(f, gain_names, between=None, after_20=None):
                base = ffn_base[f]

                def hi_f(s, c):
                    per = 32 if s < 2 else 16
                    hi(s, c + base[s], land=c * per + (landings(s, base[s]) + per))

                def silu(c):
                    for t in range(T):
                        if t == 0:
                            act.wait_ge(up_done, c + (NCH * f + 1))
                        else:
                            act.wait_ge(w_used[1], c + (base[1] + 1))
                        act.activation(sil[:, t, :], ps[:, 4 + t, 0:FC], ACT.Silu, scale=rr[:, RX, t:t + 1])\
                           .then_inc(sil_ready, 1)

                def hh_copy(c):
                    act.wait_ge(h_turned, c + (NCH * f + 1))
                    act.activation(hh[:], ps[:, 6, :].rearrange("p (k s) -> p k s", k=2), ACT.Copy)\
                       .then_inc(hh_ready, 1)

                for n in gain_names:
                    gain(n)
                hi_f(0, 1)
                act.wait_ge(rx_ready, f + 1)
                silu(0)
                hi_f(1, 1)
                if between is not None:
                    between()
                hi_f(2, 0)
                if after_20 is not None:
                    after_20()
                with act.Fori(1, NCH - 1) as c:
                    hh_copy(c - 1)
                    hi_f(0, c + 1)
                    silu(c)
                    hi_f(1, c + 1)
                    hi_f(2, c)
                hh_copy(NCH - 2)
                hi(0, NCH + base[0])
                silu(NCH - 1)
                hh_copy(NCH - 1)

            Y_LAST = [(0, ffn_base[f][0] + NCH + 1) if f is not None else None for f in (0, None, 1, 2, None, 3)]
            for m, name in ((1, ("oa", OT_A - 2)), (4, ("ob", OT_B - 2))):
                Y_LAST[m] = (unit[name][0], unit[name][1] + 1)

            def square_y(m):
                act.wait_ge(y_done, m + 1)
                square(ps[:, 0:2, :].rearrange("p b n -> p (b n)"), 0, RY)
                slot, n = Y_LAST[m]
                act.wait_ge(w_used[slot], n)
                square(ps[:, 2:4, :].rearrange("p b n -> p (b n)"), 1, RY)

            def square_res(m, t):
                act.wait_ge(res_ready, 2 * m + t + 1)
                square(res[:, t, :], t, RX)

            def into_ffn(f, m):
                square_y(m)
                name = f"x{(0, 2, 3, 5)[f]}"
                if m == 2:
                    ffn_first(f, 0)
                ffn_first(f, 1)
                for t in range(T):
                    turned_hi(name, xh, t)
                    square_res(m, t)

            def two(b):
                return ps[:, b:b + 2, :].rearrange("p b n -> p (b n)")

            def mem_exp(t, b, layer):
                act.wait_ge(ms_max, T * layer + t + 1)
                for h in range(MH_):
                    act.activation(pm[t][:, h * S:(h + 1) * S], ps[:, b + h // 2, (h % 2) * S:(h % 2 + 1) * S],
                                   ACT.Exp, bias=smx[:, t, h:h + 1], scale=MD ** -0.5,
                                   accum_out=smx[:, 2 + t, h:h + 1]).then_inc(mp_raw, 1)

            def gla():
                hi_next(2)
                square_y(0)
                hi_next()
                square_res(0, 0)
                square_res(0, 1)
                hi_next()
                used(act, ("mk0", 1))
                act.activation(kmem[:].rearrange("p h s -> p (h s)"), two(4), ACT.Copy).then_inc(kmem_ready, 1)
                hi_next()
                turned_hi("x1", xh, 0)
                turned_hi("x1", xh, 1)
                hi_next()
                used(act, ("mv0", 1))
                act.activation(vmem[:].rearrange("p t n -> p (t n)"), two(6), ACT.Copy).then_inc(vmem_ready, 1)
                hi_next(2)
                act.wait_ge(ang_ready, 1)
                act.activation(sinw[:, :, 1, :], ang[:, 0], ACT.Sin).then_inc(sin_ready, 1)
                act.activation(cosw[:], ang[:, 1], ACT.Sin).then_inc(sin_ready, 1)
                act.wait_ge(zb_ready, 1)
                link(act.activation(sc[:, 1, :], sc[:, 1, :], ACT.Exp))
                act.activation(sc[:, 1, :], sc[:, 1, :], ACT.Ln, bias=1.0).then_inc(ln_ready, 1)
                hi_next(2)
                act.wait_ge(cum_ready, 2)
                cum = am
                act.activation(qup, qdn, ACT.Exp, scale=-1.0 / TAU).then_inc(decay_ready, 1)
                act.wait_ge(decay_ready, 1)
                act.activation(qdn, qdn, ACT.Exp, scale=1.0 / TAU).then_inc(decay_ready, 1)
                act.activation(kst, kst, ACT.Exp, scale=1.0 / TAU).then_inc(decay_ready, 1)
                act.activation(dec[:].rearrange("p h c -> p (h c)"),
                               cum.rearrange("p (c j) -> p c j", j=CHUNK)[:, :, CHUNK - 1], ACT.Exp, scale=1.0 / TAU)\
                   .then_inc(decay_ready, 1)
                act.wait_ge(decay_ready, 4)
                act.activation(cum, cum, ACT.Exp, scale=1.0 / TAU).then_inc(decay_ready, 1)
                hi_next(2)
                used(act, ("qma", 1))
                act.activation(qmem[:].rearrange("p h s -> p (h s)"), two(4), ACT.Copy).then_inc(qmem_ready, 1)
                hi_next(2)
                used(act, ("va0", 1))
                act.activation(xg[:, :, 0:512], ps[:, 0:2, :], ACT.Copy).then_inc(v_ready, 1)
                hi_next(2)
                used(act, ("va1", 1))
                act.activation(xg[:, :, 512:1024], ps[:, 2:4, :], ACT.Copy).then_inc(v_ready, 1)
                hi_next(2)
                act.wait_ge(kst_turned, 1)
                act.activation(ksk, two(4), ACT.Copy).then_inc(ksk_ready, 1)
                hi_next(2)
                used(act, ("ra0", 1))
                act.activation(gs[:, :, 0:512], ps[:, 0:2, :], ACT.Silu).then_inc(silr_ready, 1)
                hi_next()
                used(act, ("ra1", 1))
                act.activation(gs[:, :, 512:1024], ps[:, 2:4, :], ACT.Silu).then_inc(silr_ready, 1)
                hi_next()
                gain("post2")
                gain("pre2")
                mem_exp(0, 0, 0)
                mem_exp(1, 2, 0)
                for t, b in ((0, 6), (1, 4)):
                    act.wait_ge(o_done, t + 1)
                    for h in range(GH):
                        n = t * GH + h
                        if n >= 2:
                            act.wait_ge(osq_ready, n - 1)
                        act.activation(kt[:, h % 2, :], ps[:, b + h // 2, (h % 2) * DV:(h % 2 + 1) * DV], ACT.Square,
                                       accum_out=ssg[:, t * GH + h:t * GH + h + 1]).then_inc(osq_ready, 1)
                act.wait_ge(mp_turned, 1)
                act.activation(pmt.rearrange("p j (h s) -> p j h s", h=MH_)[:, :, :, 0:P],
                               ps[:, 0:2, :].rearrange("p j (h s) -> p j h s", h=MH_), ACT.Copy).then_inc(mpt_ready, 1)
                act.wait_ge(mo_done, 1)
                act.activation(mh[:, 0:4, :], two(0).rearrange("p (h s) -> p h s", h=MH_), ACT.Copy).then_inc(mo_hi, 1)
                for t, b in ((0, 6), (1, 4)):
                    for j in range(2):
                        act.wait_ge(o_turned, 2 * t + j + 1)
                        act.activation(xh[:, 4 * j:4 * j + 4, t * P:(t + 1) * P],
                                       ps[:, b + j, :].rearrange("p (k s) -> p k s", k=4), ACT.Copy)\
                           .then_inc(oh_ready, 1)
                hi_next(3)
                ffn_first(1, 0)

            def window():
                hi_next(2)
                square_y(3)
                hi_next()
                square_res(3, 0)
                square_res(3, 1)
                hi_next()
                used(act, ("mk1", 1))
                act.activation(kmem[:].rearrange("p h s -> p (h s)"), two(4), ACT.Copy).then_inc(kmem_ready, 1)
                hi_next()
                act.wait_ge(k_turned, 1)
                act.activation(kt[:].rearrange("p g s -> p (g s)"), ps[:, 6, :], ACT.Copy).then_inc(kt_ready, 1)
                turned_hi("x4", xh, 0)
                turned_hi("x4", xh, 1)
                hi_next()
                used(act, ("mv1", 1))
                act.activation(vmem[:].rearrange("p t n -> p (t n)"), two(6), ACT.Copy).then_inc(vmem_ready, 1)
                hi_next(2)
                used(act, ("qmb", 1))
                act.activation(qmem[:].rearrange("p h s -> p (h s)"), two(4), ACT.Copy).then_inc(qmem_ready, 1)
                hi_next(2)
                hi_next()
                gain("post5")
                gain("pre5")
                mem_exp(0, 4, 1)
                mem_exp(1, 2, 1)
                hi_next(2)

                def copy_q(i, b):
                    act.wait_ge(q_turned, i + 1)
                    act.activation(qt[:, i * 512:(i + 1) * 512], ps[:, b, :], ACT.Copy).then_inc(qt_ready, 1)

                def exps(s):
                    m = wsm[:, s % 4]
                    act.wait_ge(sw_max, s + 1)
                    for i in range(HG):
                        row = wsc[s % 4].rearrange("p (h k) -> p h k", h=HG)[:, i, :]
                        act.activation(row, row, ACT.Exp, bias=m[:, 1, i:i + 1],
                                       accum_out=m[:, 2, i:i + 1]).then_inc(wp_raw, 1)
                    act.activation(m[:, 3, :], m[:, 3, :], ACT.Exp).then_inc(wp_raw, 1)

                def copy_p(s):
                    g, r, t = GROUPS[s]
                    act.wait_ge(wp_turned, s + 1)
                    if t == 0:
                        act.activation(wpt[s % 4][0], ps[:, 3, :], ACT.Copy).then_inc(wpt_ready, 1)
                    else:
                        act.activation(wpt[s % 4][0], ps[0:CHUNK, 4, :], ACT.Copy)
                        act.activation(wpt[s % 4][1], ps[:, 5, :], ACT.Copy).then_inc(wpt_ready, 1)

                def output_hi(s):
                    g, r, t = GROUPS[s]
                    rows = np.s_[r * HD:(r + 1) * HD]
                    act.wait_ge(pv_done, s + 1)
                    act.activation(xh[rows, 4 * g:4 * g + 4, t * P:(t + 1) * P],
                                   ps[rows, 6 + t, :].rearrange("p (h s) -> p h s", h=HG), ACT.Copy).then_inc(oh_ready, 1)

                copy_q(0, 0)
                copy_q(1, 1)
                act.wait_ge(mp_turned, 3)
                act.activation(pmt.rearrange("p j (h s) -> p j h s", h=MH_)[:, :, :, 0:P],
                               ps[:, 4:6, :].rearrange("p j (h s) -> p j h s", h=MH_), ACT.Copy).then_inc(mpt_ready, 1)
                exps(0)
                act.wait_ge(mo_done, 2)
                act.activation(mh[:, 0:4, :], two(4).rearrange("p (h s) -> p h s", h=MH_), ACT.Copy).then_inc(mo_hi, 1)
                exps(1)
                copy_q(2, 6)
                copy_q(3, 7)
                n = len(GROUPS)
                for s in range(2, n + 2):
                    if s < n:
                        exps(s)
                    copy_p(s - 2)
                    if s >= 3:
                        output_hi(s - 3)
                output_hi(n - 1)
                hi_next(3)
                ffn_first(3, 0)

            gain("pre0")
            act.wait_ge(res_in[0], 16)
            square(res[:, 0, :], 0, RX)
            ffn_first(0, 0)
            act.wait_ge(res_in[1], 16)
            square(res[:, 1, :], 1, RX)
            gain("mem0")
            turned_hi("x0", xh, 0)
            ffn_first(0, 1)
            turned_hi("x0", xh, 1)
            act.wait_ge(mem_in, 16)
            for t in range(T):
                square(mx[:, t, :], t, RM)
            act.dma_start(wgu[:], w_gate_up[0]).then_inc(small_in, 16)
            with nc.allow_non_contiguous_dma("one gate bias and two positions a partition"):
                act.dma_start(bg[:], b_gate[0].rearrange("(h p) -> p h", p=P)).then_inc(small_in, 16)
                act.dma_start(posi[:], positions[0].rearrange("(t p) -> p t", p=P)).then_inc(small_in, 16)
            act.dma_start(sink[:], sinks[0:1, :].partition_broadcast(P)).then_inc(small_in, 16)
            act.dma_start(glag[:], gla_norm_g[0:1, :].partition_broadcast(P)).then_inc(small_in, 16)

            def memory(layer):
                for t in range(T):
                    turned_hi(f"mem{layer}", mh, t)

            ffn(0, ["post1", "pre1"], between=lambda: memory(0))
            gla()
            into_ffn(1, 1)
            ffn(1, ["post3", "pre3"])
            hi_next()
            into_ffn(2, 2)

            def kv():
                for t in range(T):
                    turned_hi("kv", mh, t)

            gain("kv")
            gain("mem1")
            ffn(2, ["post4", "pre4"], between=kv, after_20=lambda: memory(1))
            window()
            into_ffn(3, 4)
            ffn(3, ["post6"])
            square_y(5)

        @block.vector
        def _(dve):
            dve_count = [0]

            def link(ins):
                dve_count[0] += 1
                ins.then_inc(dve_step, 1)
                dve.wait_ge(dve_step, dve_count[0])

            def rsqrt(dst, src, n, scale):
                half, y, t, u = (nw[:, i, 0:n] for i in range(4))
                link(dve.tensor_scalar(half, src, 0.5 * scale, 0.5 * EPS, ALU.mult, ALU.add))
                link(dve.tensor_scalar(t.bitcast(I32), half.bitcast(I32), 1, None, ALU.logical_shift_right))
                link(dve.tensor_scalar(y.bitcast(I32), t.bitcast(I32), -1.0,
                                       float(RSQRT_MAGIC - 2 ** 22 - 2 ** 31), ALU.mult, ALU.add))
                for i in range(3):
                    if n == 1:
                        link(dve.scalar_tensor_tensor(out=u, in0=y, scalar=y, in1=half, op0=ALU.mult, op1=ALU.mult))
                    else:
                        link(dve.tensor_tensor(t, y, y, ALU.mult))
                        link(dve.tensor_tensor(u, t, half, ALU.mult))
                    link(dve.scalar_tensor_tensor(out=dst if i == 2 else y, in0=u, scalar=1.5, in1=y,
                                                  op0=ALU.subtract, op1=ALU.mult))

            def gain(name):
                i = gain_at[name]
                dve.wait_ge(gain_in[i % NG], 16 * (i // NG + 1))
                return gains[:, i % NG, :]

            def turned_lo(name, lead, dst, t):
                for j in range(2):
                    dve.wait_ge(th_ready, 4 * turn_at[name] + 2 * t + j + 1)
                    at = np.s_[:, 4 * j:4 * j + 4, t * P:(t + 1) * P]
                    dve.tensor_tensor(dst[at], ps[:, 2 * t + j, :].rearrange("p (k s) -> p k s", k=4),
                                      lead[at].bitcast(F32), ALU.subtract).then_inc(tl_ready, 1)

            def lo(slot, n):
                dve.wait_ge(hi_ready[slot], n + 1)
                dve.tensor_tensor(w_lo[:, slot, :], raw[:, slot, :], w_hi[:, slot, :].bitcast(F32),
                                  ALU.subtract).then_inc(lo_ready[slot], 1)

            def ffn(f, between=None, after_20=None):
                base = ffn_base[f]

                def gate(c):
                    for t in range(T):
                        dve.wait_ge(sil_ready, c * 2 + (2 * NCH * f + t + 1))
                        dve.scalar_tensor_tensor(out=hid[:, t, :], in0=ps[:, 4 + t, FC:2 * FC],
                                                 scalar=rr[:, RX, t:t + 1], in1=sil[:, t, :],
                                                 op0=ALU.mult, op1=ALU.mult).then_inc(gated, 1)

                def hl_sub(c):
                    dve.wait_ge(hh_ready, c + (NCH * f + 1))
                    dve.tensor_tensor(hl[:], ps[:, 6, :].rearrange("p (k s) -> p k s", k=2), hh[:].bitcast(F32),
                                      ALU.subtract).then_inc(hl_ready, 1)

                lo(0, 1 + base[0])
                gate(0)
                if between is not None:
                    between()
                lo(2, base[2])
                if after_20 is not None:
                    after_20()
                with dve.Fori(1, NCH - 1) as c:
                    hl_sub(c - 1)
                    gate(c)
                    lo(2, c + base[2])
                hl_sub(NCH - 2)
                lo(0, NCH + base[0])
                gate(NCH - 1)
                hl_sub(NCH - 1)

            squared = [0]

            def root(what, t=None, weight=1.0, n=1):
                squared[0] += n
                dve.wait_ge(ssq_ready, squared[0])
                tiles = slice(0, T) if t is None else slice(t, t + 1)
                rsqrt(rr[:, what, tiles], ssq[:, what, tiles], T if t is None else 1, 1.0 / D)
                if weight != 1.0:
                    link(dve.tensor_scalar(rr[:, what, tiles], rr[:, what, tiles], weight, None, ALU.mult))

            def update(m, name, weight, t):
                root(RY, t, weight)
                link(dve.scalar_tensor_tensor(out=xg[:, t, :], in0=two(2 * t), scalar=rr[:, RY, t:t + 1],
                                              in1=gain(name), op0=ALU.mult, op1=ALU.mult))
                dve.tensor_tensor(res[:, t, :], res[:, t, :], xg[:, t, :], ALU.add).then_inc(res_ready, 1)
                dve.wait_ge(res_ready, 2 * m + t + 1)

            def pre(name, t):
                dve.tensor_tensor(xg[:, t, :], res[:, t, :], gain("kv" if name == "kv" else "pre" + name[1:]), ALU.mult).then_inc(xg_ready, 1)

            def into_ffn(f, m, weight):
                name = f"x{(0, 2, 3, 5)[f]}"
                update(m, f"post{m + 1}", weight, 0)
                pre(name, 0)
                update(m, f"post{m + 1}", weight, 1)
                turned_lo(name, xh, xl, 0)
                pre(name, 1)
                turned_lo(name, xh, xl, 1)
                factor()

            def factor():
                root(RX, n=T)
                dve.engine_nop().then_inc(rx_ready, 1)

            def into_mixer(m, pre_name):
                for t in range(T):
                    update(m, f"post{m + 1}", 0.5, t)
                for t in range(T):
                    root(RX, t)
                    dve.scalar_tensor_tensor(out=xg[:, t, :], in0=res[:, t, :], scalar=rr[:, RX, t:t + 1],
                                             in1=gain(pre_name), op0=ALU.mult, op1=ALU.mult).then_inc(xg_ready, 1)

            def mem_normed(layer):
                g = gain(f"mem{layer}")
                dve.wait_ge(mem_in, 16 * (layer + 1))
                for t in range(T):
                    dve.scalar_tensor_tensor(out=mx[:, t, :], in0=mx[:, t, :], scalar=rr[:, RM, t:t + 1], in1=g,
                                             op0=ALU.mult, op1=ALU.mult).then_inc(xg_ready, 1)

            def two(b):
                return ps[:, b:b + 2, :].rearrange("p b n -> p (b n)")

            def heads(ap, h):
                return ap.rearrange("p (h s) -> p h s", h=h)

            def rotate(dst, src, t, heads_n, tmp):
                half = HD // 2
                c = cosw[:, t, :].unsqueeze(1).unsqueeze(1).to_broadcast([P, heads_n, 2, half])
                s = [sinw[:, t, i, :].unsqueeze(1).to_broadcast([P, heads_n, half]) for i in range(2)]
                dve.tensor_tensor(tmp[:, :, 0, :], src[:, :, 1, :], s[0], ALU.mult)
                dve.tensor_tensor(tmp[:, :, 1, :], src[:, :, 0, :], s[1], ALU.mult)
                link(dve.tensor_tensor(dst, src, c, ALU.mult))
                return dve.tensor_tensor(dst, dst, tmp, ALU.add)

            def mem_maxima(t, b, layer):
                dve.wait_ge(ms_done, T * layer + t + 1)
                link(dve.tensor_reduce(smx[:, 6, 4 * t:4 * t + MH_], heads(two(b), MH_), AX.X, ALU.max))
                dve.tensor_scalar(smx[:, t, 0:MH_], smx[:, 6, 4 * t:4 * t + MH_], -MD ** -0.5, None, ALU.mult).then_inc(ms_max, 1)

            def mem_probs(t, layer):
                dve.wait_ge(mp_raw, MH_ * (T * layer + t + 1))
                link(dve.reciprocal(smx[:, 7, 4 * t:4 * t + MH_], smx[:, 2 + t, 0:MH_]))
                dve.tensor_tensor(heads(pm[t], MH_), heads(pm[t], MH_),
                                  smx[:, 7, 4 * t:4 * t + MH_].unsqueeze(2).to_broadcast([P, MH_, S]), ALU.mult)\
                   .then_inc(mp_ready, 1)

            def mem_turned(b, layer):
                dve.wait_ge(mp_turned, T * layer + 2)
                dve.tensor_copy(pmt.rearrange("p j (h s) -> p j h s", h=MH_)[:, :, :, P:2 * P],
                                ps[:, b:b + 2, :].rearrange("p j (h s) -> p j h s", h=MH_)).then_inc(mpt_ready, 1)

            def mem_lo(b, layer):
                dve.wait_ge(mo_hi, layer + 1)
                dve.tensor_tensor(ml[:, 0:4, :], heads(two(b), MH_), mh[:, 0:4, :].bitcast(F32),
                                  ALU.subtract).then_inc(mo_lo, 1)

            def gla():
                used(dve, ("ga", 0))
                dve.tensor_copy(glr, ps[0:RANK, 4, 0:S]).then_inc(glr_ready, 1)
                dve.wait_ge(z_done, 1)
                z, nab, cum = kst, sc[:, 1, :], am
                for h in range(GH):
                    link(dve.tensor_scalar(z[:, h * S:(h + 1) * S], ps[:, h // 2, (h % 2) * S:(h % 2 + 1) * S],
                                           bg[:, h:h + 1], None, ALU.add))
                dve.scalar_tensor_tensor(out=nab, in0=z, scalar=-1.0, in1=z, op0=ALU.mult, op1=ALU.min)\
                   .then_inc(zb_ready, 1)
                for e in range(2):
                    dve.memset(qe[e], 0.0)
                dve.wait_ge(ln_ready, 1)
                link(dve.scalar_tensor_tensor(out=z, in0=z, scalar=0.0, in1=nab, op0=ALU.min, op1=ALU.subtract))
                link(dve.tensor_tensor_scan(cum, cmask, z, 0.0, ALU.mult, ALU.add))
                cv = cum.rearrange("p (c j) -> p c j", j=CHUNK)
                total = cv[:, :, CHUNK - 1:CHUNK].to_broadcast([P, GH * 4, CHUNK])
                dve.scalar_tensor_tensor(out=qdn.rearrange("p (c j) -> p c j", j=CHUNK), in0=total, scalar=0.5,
                                         in1=cv, op0=ALU.mult, op1=ALU.subtract).then_inc(cum_ready, 1)
                dve.tensor_tensor(kst.rearrange("p (c j) -> p c j", j=CHUNK), total, cv, ALU.subtract)\
                   .then_inc(cum_ready, 1)
                dve.wait_ge(decay_ready, 3)
                used(dve, ("ka", 1))
                dve.tensor_tensor(kdn, two(2), qdn, ALU.mult)
                dve.tensor_tensor(kup, two(2), qup, ALU.mult)
                link(dve.tensor_tensor(kst, two(2), kst, ALU.mult))
                dve.engine_nop().then_inc(k_taken, 1)
                dve.wait_ge(decay_ready, 5)
                used(dve, ("qa", 1))
                for e in range(2):
                    at = np.s_[:, :, e * CHUNK:(e + 1) * CHUNK]
                    link(dve.scalar_tensor_tensor(out=qe[e].rearrange("p (x j) -> p x j", j=P)[at],
                                                  in0=two(6).rearrange("p (x j) -> p x j", j=P)[at], scalar=DK ** -0.5,
                                                  in1=cum.rearrange("p (x j) -> p x j", j=P)[at],
                                                  op0=ALU.mult, op1=ALU.mult))
                dve.scalar_tensor_tensor(out=qdn, in0=two(6), scalar=DK ** -0.5, in1=qdn, op0=ALU.mult, op1=ALU.mult)
                link(dve.memset(am, 0.0))
                dve.scalar_tensor_tensor(out=qup, in0=two(6), scalar=DK ** -0.5, in1=qup, op0=ALU.mult, op1=ALU.mult)\
                   .then_inc(q_taken, 1)

                def take_scores(t):
                    dve.wait_ge(a_done, t + 1)
                    dst = heads(am[:, t * GH * P:(t + 1) * GH * P], GH)
                    for b, mask in ((6, past), (7, fut)):
                        link(dve.copy_predicated(dst, mask[:].bitcast(I32).unsqueeze(1).to_broadcast([P, GH, P]),
                                                 heads(ps[:, b, :], GH)))
                    dve.engine_nop().then_inc(a_taken, 1)

                take_scores(0)
                take_scores(1)
                dve.wait_ge(kv_done, 1)
                dve.tensor_copy(state[1], two(4)).then_inc(s_ready, 1)
                dve.wait_ge(s_ready, 1)

                def next_state(n, b):
                    dve.wait_ge(kv_done, n + 1)
                    for h in range(GH):
                        at = np.s_[:, h * DV:(h + 1) * DV]
                        last = dve.scalar_tensor_tensor(out=state[n + 1][at], in0=state[n][at],
                                                        scalar=dec[:, h, n:n + 1], in1=two(b)[at],
                                                        op0=ALU.mult, op1=ALU.add)
                        if h < GH - 1:
                            link(last)
                    last.then_inc(s_ready, 1)
                    dve.wait_ge(s_ready, n + 1)

                next_state(1, 6)
                next_state(2, 4)
                for i in range(2):
                    dve.wait_ge(silr_ready, i + 1)
                    for t in range(T):
                        link(dve.tensor_tensor(heads(gs[:, t, i * 512:(i + 1) * 512], 2),
                                               heads(gs[:, t, i * 512:(i + 1) * 512], 2),
                                               glag[:].unsqueeze(1).to_broadcast([P, 2, DV]), ALU.mult))
                mem_maxima(0, 0, 0)
                mem_maxima(1, 2, 0)
                mem_probs(0, 0)
                mem_probs(1, 0)
                dve.wait_ge(osq_ready, T * GH)
                rsqrt(rsg[:], ssg[:], T * GH, 1.0 / DV)
                for t, b in ((0, 6), (1, 4)):
                    for h in range(GH):
                        at = np.s_[:, h * DV:(h + 1) * DV]
                        link(dve.scalar_tensor_tensor(out=gs[:, t, :][at], in0=two(b)[at],
                                                      scalar=rsg[:, t * GH + h:t * GH + h + 1], in1=gs[:, t, :][at],
                                                      op0=ALU.mult, op1=ALU.mult))
                    dve.engine_nop().then_inc(on_ready, 1)
                mem_turned(2, 0)
                mem_lo(0, 0)
                for t, b in ((0, 6), (1, 4)):
                    for j in range(2):
                        dve.wait_ge(oh_ready, 2 * t + j + 1)
                        at = np.s_[:, 4 * j:4 * j + 4, t * P:(t + 1) * P]
                        dve.tensor_tensor(xl[at], ps[:, b + j, :].rearrange("p (k s) -> p k s", k=4),
                                          xh[at].bitcast(F32), ALU.subtract).then_inc(ol_ready, 1)

            def window_kv():
                used(dve, ("kv", 0))
                for t in range(T):
                    src = ps[:, 7, t * S:(t + 1) * S]
                    link(dve.tensor_scalar(kw[:, t * 2 * HD:(t + 1) * 2 * HD], src[:, 0:2 * HD], rr[:, RX, t:t + 1],
                                           None, ALU.mult))
                    for twice in range(2):
                        dve.tensor_scalar(vs[:, t, :, twice, :],
                                          src[:, 2 * HD:4 * HD].rearrange("p (g d) -> p g d", g=2),
                                          rr[:, RX, t:t + 1], None, ALU.mult).then_inc(vs_ready, 1)

            def rotate_keys():
                dve.wait_ge(sin_ready, 2)
                link(dve.tensor_scalar(sinw[:, :, 0, :], sinw[:, :, 1, :], -1.0, None, ALU.mult))
                v = "p (h a j) -> p h a j"
                for t in range(T):
                    rotated = kw[:, 256 + t * 2 * HD:256 + (t + 1) * 2 * HD]
                    link(rotate(rotated.rearrange(v, h=2, a=2), kw[:, t * 2 * HD:(t + 1) * 2 * HD].rearrange(v, h=2, a=2),
                                t, 2, kw[:, 512 + t * 2 * HD:512 + (t + 1) * 2 * HD].rearrange(v, h=2, a=2)))
                    for twice in range(2):
                        link(dve.tensor_copy(gs[:, 0, t * 2 * P:(t + 1) * 2 * P]
                                             .rearrange("p (h w d) -> p h w d", h=2, w=2)[:, :, twice, :],
                                             rotated.rearrange("p (h d) -> p h d", h=2)))
                dve.engine_nop().then_inc(kr_ready, 1)
                dve.wait_ge(vs_ready, 4)
                dve.tensor_copy(vsh, vs[64:128, 0]).then_inc(vs_ready, 1)

            def window():
                dve.wait_ge(sin_ready, 2)

                def rotate_q(i):
                    half, t = i // 2, i % 2
                    used(dve, (f"qb{half}", 1))
                    v = "p (h a j) -> p h a j"
                    rotate(gs[:, t, half * 512:(half + 1) * 512].rearrange(v, h=8, a=2),
                           ps[:, 6 * half + t, :].rearrange(v, h=8, a=2), t, 8,
                           sc[:, t * 6, 0:512].rearrange(v, h=8, a=2)).then_inc(qr_ready, 1)

                def take_scores(s):
                    g, r, t = GROUPS[s]
                    n, m = KEYS[t], wsm[:, s % 4]
                    dve.wait_ge(sw_done, s + 1)
                    if s >= 4:
                        dve.wait_ge(wp_turned, s - 3)
                    dst = wsc[s % 4].rearrange("p (h k) -> p h k", h=HG)
                    mask = (band0, band1)[t]
                    if t == 0:
                        link(dve.scalar_tensor_tensor(out=dst, in0=heads(ps[:, 0, :], HG), scalar=HD ** -0.5,
                                                      in1=mask[:].unsqueeze(1).to_broadcast([P, HG, n]),
                                                      op0=ALU.mult, op1=ALU.add))
                    else:
                        for j in range(2):
                            link(dve.scalar_tensor_tensor(out=dst[:, 2 * j:2 * j + 2, :],
                                                          in0=heads(ps[:, 1 + j, 0:2 * n], 2), scalar=HD ** -0.5,
                                                          in1=mask[:].unsqueeze(1).to_broadcast([P, 2, n]),
                                                          op0=ALU.mult, op1=ALU.add))
                    dve.engine_nop().then_inc(sw_taken, 1)
                    own, negated = (v[:].rearrange("p (g i r) -> p g i r", g=2, r=2)[:, g, :, r] for v in (sink, nsink))
                    link(dve.tensor_reduce(m[:, 0, :], dst, AX.X, ALU.max))
                    link(dve.scalar_tensor_tensor(out=m[:, 1, :], in0=m[:, 0, :], scalar=-1.0,
                                                  in1=negated, op0=ALU.mult, op1=ALU.min))
                    dve.tensor_tensor(m[:, 3, :], own, m[:, 1, :], ALU.add).then_inc(sw_max, 1)

                def probs(s):
                    g, r, t = GROUPS[s]
                    m = wsm[:, s % 4]
                    dve.wait_ge(wp_raw, (HG + 1) * (s + 1))
                    link(dve.tensor_tensor(m[:, 4, :], m[:, 2, :], m[:, 3, :], ALU.add))
                    link(dve.reciprocal(m[:, 5, :], m[:, 4, :]))
                    p = wsc[s % 4].rearrange("p (h k) -> p h k", h=HG)
                    dve.tensor_tensor(p, p, m[:, 5, :].unsqueeze(2).to_broadcast([P, HG, KEYS[t]]),
                                      ALU.mult).then_inc(wp_ready, 1)

                def output_lo(s):
                    g, r, t = GROUPS[s]
                    at = np.s_[r * HD:(r + 1) * HD, 4 * g:4 * g + 4, t * P:(t + 1) * P]
                    dve.wait_ge(oh_ready, 4 + s + 1)
                    dve.tensor_tensor(xl[at], heads(ps[r * HD:(r + 1) * HD, 6 + t, :], HG), xh[at].bitcast(F32),
                                      ALU.subtract).then_inc(ol_ready, 1)

                link(dve.tensor_scalar(nsink[:], sink[:], -1.0, None, ALU.mult))
                mem_maxima(0, 4, 1)
                mem_maxima(1, 2, 1)
                rotate_q(0)
                rotate_q(1)
                mem_probs(0, 1)
                mem_probs(1, 1)
                rotate_q(2)
                mem_turned(2, 1)
                take_scores(0)
                rotate_q(3)
                dve.wait_ge(qr_ready, 4)
                take_scores(1)
                probs(0)
                mem_lo(4, 1)
                n = len(GROUPS)
                for s in range(2, n + 3):
                    if s < n:
                        take_scores(s)
                    if s <= n:
                        probs(s - 1)
                    if s >= 4:
                        output_lo(s - 4)
                output_lo(n - 1)

            def angles():
                dve.wait_ge(small_in, 16 * 5)
                dve.wait_ge(const_ready, 2)
                link(dve.tensor_copy(posf[:], posi[:]))
                flat = [ang[:, i].rearrange("p t j -> p (t j)") for i in range(4)]
                a, k, kh, kl = flat
                for t in range(T):
                    link(dve.tensor_scalar(ang[:, 0, t, :], invf[:], posf[:, t:t + 1], None, ALU.mult))
                link(dve.tensor_scalar(k, a, 1.0 / TWO_PI, None, ALU.mult))
                big = 1.5 * 2.0 ** 23
                link(dve.tensor_scalar(k, k, big, None, ALU.add))
                link(dve.tensor_scalar(k, k, -big, None, ALU.add))
                link(dve.tensor_scalar(kh, k, big * 4096.0, None, ALU.add))
                link(dve.tensor_scalar(kh, kh, -big * 4096.0, None, ALU.add))
                link(dve.tensor_tensor(kl, k, kh, ALU.subtract))
                for part in parts_of(TWO_PI, 12, 4):
                    for n in (kh, kl):
                        link(dve.scalar_tensor_tensor(out=a, in0=n, scalar=-part, in1=a, op0=ALU.mult, op1=ALU.add))
                link(dve.tensor_scalar(a, a, PI_BELOW, -PI_BELOW, ALU.min, ALU.max))
                link(dve.scalar_tensor_tensor(out=k, in0=a, scalar=-1.0, in1=a, op0=ALU.mult, op1=ALU.min))
                dve.tensor_scalar(k, k, float(np.pi / 2), None, ALU.add).then_inc(ang_ready, 1)

            dve.wait_ge(res_in[0], 16)
            pre("x0", 0)
            dve.wait_ge(res_in[1], 16)
            pre("x0", 1)
            lo(0, ffn_base[0][0])
            turned_lo("x0", xh, xl, 0)
            turned_lo("x0", xh, xl, 1)
            factor()

            def memory():
                for t in range(T):
                    turned_lo("mem0", mh, ml, t)

            def first_memory():
                root(RM, n=T)
                mem_normed(0)
                memory()

            ffn(0, between=first_memory)
            into_mixer(0, "pre1")
            turned_lo("x1", xh, xl, 0)
            turned_lo("x1", xh, xl, 1)
            angles()
            gla()
            into_ffn(1, 1, 1.0)
            ffn(1)
            into_ffn(2, 2, 0.5)
            for t in range(T):
                dve.wait_ge(turned, 4 * turn_at["x3"] + 2 * t + 2)
                pre("kv", t)

            def kv():
                for t in range(T):
                    turned_lo("kv", mh, ml, t)
                mem_normed(1)
                window_kv()

            def second_memory():
                for t in range(T):
                    turned_lo("mem1", mh, ml, t)

            ffn(2, kv, second_memory)
            rotate_keys()
            into_mixer(3, "pre4")
            turned_lo("x4", xh, xl, 0)
            turned_lo("x4", xh, xl, 1)
            window()
            into_ffn(3, 4, 1.0)
            ffn(3)
            for t in range(T):
                update(5, "post6", 0.5, t)


_INS = ["x", "mem", "positions", "norm_g", "w_ffn_in", "w_ffn_out", "mem_norm_g", "w_mem_kv", "w_in_a",
        "w_gate_up", "b_gate", "gla_norm_g", "w_out_a", "kv_norm_g", "w_kv", "w_in_b", "sinks", "w_out_b"]


def kernel(**inputs):
    import numpy as _np
    import concourse.bacc as _bacc
    from concourse import mybir as _mybir
    from concourse.bass_utils import run_bass_kernel_spmd as _run

    nc = _bacc.Bacc("TRN2", target_bir_lowering=False, num_devices=1)
    arrays, args = {}, []
    for name in _INS:
        a = _np.ascontiguousarray(inputs[name])
        arrays[f"in_{name}"] = a
        args.append(nc.dram_tensor(f"in_{name}", a.shape, _mybir.dt.from_np(a.dtype), kind="ExternalInput").ap())
    args.append(nc.dram_tensor("out_0", inputs["x"].shape, F32, kind="ExternalOutput").ap())
    hybrid_kernel(nc, *args)
    r = _run(nc, [arrays], core_ids=[0])
    return r.results[0]["out_0"]
```

```python
from contextlib import ExitStack

import numpy as np

import concourse.bass as bass
from concourse import mybir

F32 = mybir.dt.float32
F32R = mybir.dt.float32r
I32 = mybir.dt.int32
ALU = mybir.AluOpType
ACT = mybir.ActivationFunctionType
AX = mybir.AxisListType

P = 128
EPS = 1e-6
NEG_INF = -1e30
ROPE_THETA = 10000.0
TAU = 16.0
CHUNK = 64
RSQRT_MAGIC = 0x5F3759DF
TWO_PI = 2.0 * np.pi
PI_BELOW = 3.1415925


def parts_of(value, bits, count):
    parts = []
    for _ in range(count):
        exponent = int(np.floor(np.log2(abs(value))))
        step = 2.0 ** (exponent - bits + 1)
        part = float(np.floor(value / step) * step)
        parts.append(part)
        value -= part
    return parts


def hybrid_kernel(nc, x, mem, positions, norm_g, w_ffn_in, w_ffn_out, mem_norm_g, w_mem_kv,
                  w_in_a, w_gate_up, b_gate, gla_norm_g, w_out_a, kv_norm_g, w_kv, w_in_b, sinks, w_out_b, out):
    _, S, D = x.shape
    F = w_ffn_out.shape[2]
    T = S // P
    K = D // P
    FC = 256
    NCH = F // FC
    GH, DK, DV = 4, D // 8, D // 4
    KW, VW = GH * DK, GH * DV
    RANK = w_gate_up.shape[1]
    MHEADS, MD = 4, 128
    MW = MHEADS * MD
    HQ, HD = 16, 64
    COL_K, COL_V, COL_R = KW, 2 * KW, 2 * KW + VW
    COL_G = COL_R + VW
    COL_QM = COL_G + RANK
    UNIT = 2048
    inv_freq = np.power(np.float32(ROPE_THETA),
                        -np.arange(HD // 2, dtype=np.float32) * np.float32(2.0 / HD)).astype(np.float32)
    assert T == 2 and K == 8 and F % FC == 0 and x.shape[0] == 1

    def cols(w, k0, nk, c0, n):
        return w.rearrange("(k p) n -> p k n", p=P)[:, k0:k0 + nk, c0:c0 + n]

    def halves(name, w, c0):
        return [((name, i), cols(w, 4 * i, 4, c0, 512)) for i in range(2)]

    def rows(name, w, tiles):
        return [((name, k), cols(w, k, 2, 0, D)) for k in tiles]

    wa, woa, wb, wob = w_in_a[0], w_out_a[0], w_in_b[0], w_out_b[0]
    OT_A, OT_B = VW // P, HQ * HD // P
    SEG_A = (halves("mk0", w_mem_kv[0], 0) + halves("mv0", w_mem_kv[0], MW)
             + [(("ga", 0), cols(wa, 0, K, COL_G, P))]
             + halves("ka", wa, COL_K) + halves("qa", wa, 0) + halves("qma", wa, COL_QM)
             + halves("va0", wa, COL_V) + halves("va1", wa, COL_V + 512)
             + halves("ra0", wa, COL_R) + halves("ra1", wa, COL_R + 512)
             + rows("oa", woa, range(OT_A, OT_A + 4, 2)) + rows("oa", woa, range(0, OT_A, 2)))
    mem_values = [(("mv1", i), cols(w_mem_kv[1], 0, K, MW + 256 * i, 256)) for i in range(2)]
    SEG_V = mem_values[:1]
    SEG_KV = mem_values[1:] + [(("kv", 0), cols(w_kv, 0, K, 0, 256))]
    FIXED_SLOT = {("mv1", 0): 2, ("mv1", 1): 1, ("kv", 0): 2}
    SEG_B = (halves("mk1", w_mem_kv[1], 0)
             + halves("qmb", wb, HQ * HD) + halves("qb0", wb, 0) + halves("qb1", wb, 512)
             + rows("ob", wob, range(OT_B, OT_B + 4, 2)) + rows("ob", wob, range(0, OT_B, 2)))
    unit = {}
    ffn_base = []
    FFN_USES = (NCH + 1, NCH, NCH - 1)
    uses = [0, 0, 0]
    for seg in (0, SEG_A, SEG_V, 0, SEG_KV, 0, SEG_B, 0):
        if seg == 0:
            ffn_base.append(tuple(uses))
            uses = [u + v for u, v in zip(uses, FFN_USES)]
        else:
            for n, (name, _) in enumerate(seg):
                slot = FIXED_SLOT.get(name, (n + 1) % 3)
                unit[name] = (slot, uses[slot])
                uses[slot] += 1

    GAINS = [("pre0", norm_g[0, 0:1, :]), ("mem0", mem_norm_g[0:1, :]),
             ("post1", norm_g[0, 1:2, :]), ("pre1", norm_g[0, 2:3, :]),
             ("mem1", mem_norm_g[1:2, :]),
             ("post2", norm_g[0, 3:4, :]), ("pre2", norm_g[0, 4:5, :]),
             ("post3", norm_g[0, 5:6, :]), ("pre3", norm_g[1, 0:1, :]),
             ("kv", kv_norm_g.rearrange("(a d) -> a d", a=1)),
             ("post4", norm_g[1, 1:2, :]), ("pre4", norm_g[1, 2:3, :]),
             ("post5", norm_g[1, 3:4, :]), ("pre5", norm_g[1, 4:5, :]),
             ("post6", norm_g[1, 5:6, :])]
    NG = 3
    gain_at = {name: i for i, (name, _) in enumerate(GAINS)}
    TURNS = ["x0", "mem0", "x1", "mem1", "x2", "x3", "kv", "mem1 again", "x4", "x5"]
    turn_at = {name: i for i, name in enumerate(TURNS)}
    PIECES = [(t, j) for j in range(2) for t in range(T)]

    def bank_of(name, t, j):
        return 2 * t + j + (4 if name == "mem1" else 0)

    def piece(name, t, j):
        return 4 * turn_at[name] + PIECES.index((t, j)) + 1

    with ExitStack() as ctx:
        def sb(name, shape, dt=F32):
            return ctx.enter_context(nc.sbuf_tensor(name, shape, dt))

        def sem(name):
            return ctx.enter_context(nc.semaphore(name))

        ps = ctx.enter_context(nc.psum_tensor("ps", [P, 8, 512], F32))

        raw = sb("raw", [P, 3, UNIT])
        w_hi = sb("w_hi", [P, 3, UNIT], F32R)
        w_lo = sb("w_lo", [P, 3, UNIT], F32R)
        res = sb("res", [P, T, D])
        xg = sb("xg", [P, T, D])
        xh = sb("xh", [P, K, S], F32R)
        xl = sb("xl", [P, K, S], F32R)
        mh = sb("mh", [P, K, S], F32R)
        ml = sb("ml", [P, K, S], F32R)
        hh = sb("hh", [P, 2, S], F32R)
        hl = sb("hl", [P, 2, S], F32R)
        kmem = sb("kmem", [P, MHEADS, S])
        vmem = sb("vmem", [P, T, MW])
        qmem = sb("qmem", [P, MHEADS, S])
        gains = sb("gains", [P, NG, D])
        sc = sb("sc", [P, 10, 1024])
        gs = sb("gs", [P, T, D])
        kt = sb("kt", [P, 2, S])
        vs = sb("vs", [P, T, 2, 2, HD])
        wsm = sb("wsm", [P, 4, 6, 4])
        ident = sb("ident", [P, P])
        past = sb("past", [P, P])
        fut = sb("fut", [P, P])
        band0 = sb("band0", [P, 128])
        band1 = sb("band1", [P, 192])
        wgu = sb("wgu", [RANK, KW])
        bg = sb("bg", [P, GH])
        sink = sb("sink", [P, HQ])
        nsink = sb("nsink", [P, HQ])
        cosw = sb("cosw", [P, T, HD // 2])
        sinw = sb("sinw", [P, T, 2, HD // 2])
        posi = sb("posi", [P, T], I32)
        posf = sb("posf", [P, T])
        invf = sb("invf", [P, HD // 2])
        glag = sb("glag", [P, DV])
        ssq = sb("ssq", [P, 4, 2])
        rr = sb("rr", [P, 4, 2])
        nw = sb("nw", [P, 4, 8])
        smx = sb("smx", [P, 8, 8])
        dec = sb("dec", [P, GH, 4])
        ssg = sb("ssg", [P, T * GH])
        rsg = sb("rsg", [P, T * GH])
        RM, RX, RY = 0, 1, 2

        kst, qdn, qup, am, kdn, kup = (sc[:, i, :] for i in range(6))
        state = [None, sc[:, 1, :], sc[:, 2, :], sc[:, 0, :]]
        qe = [sc[:, 6, :], sc[:, 7, :]]
        ksk = sc[:, 8, :]
        cmask = sc[:, 8, :]
        glr = sc[0:RANK, 6, 0:S]
        sil = sc[:, 9, 0:512].rearrange("p (t f) -> p t f", t=T)
        hid = sc[:, 9, 512:1024].rearrange("p (t f) -> p t f", t=T)
        ang = sc[:, 9, 0:4 * T * HD // 2].rearrange("p (i t j) -> p i t j", i=4, t=T)
        last_h = [xh[:, 0:2, :], xl[:, 0:2, :]]
        junk = [sc[:, 4, :], sc[:, 5, :]]
        mx = sc[:, 6:8, :]
        pm = [sc[:, 4, :], sc[:, 5, :]]
        qt = sc[:, 1:3, :].rearrange("p a n -> p (a n)")
        wsc = [sc[:, 3, 0:512], sc[:, 6, 0:768], sc[:, 3, 512:1024], sc[:, 4, 0:768]]
        wpt = [(sc[:, 7, 0:512],), (sc[0:CHUNK, 7, 512:1024], sc[:, 0, 0:512]),
               (sc[:, 5, 0:512],), (sc[0:CHUNK, 5, 512:1024], sc[:, 8, 0:512])]
        kw = sc[:, 0, 0:768]
        vsh = sc[0:CHUNK, 0, 768:1024].rearrange("p (g w d) -> p g w d", g=2, w=2)
        pmt = sc[:, 8:10, :]

        landed = [sem(f"landed{i}") for i in range(3)]
        hi_ready = [sem(f"hi_ready{i}") for i in range(3)]
        lo_ready = [sem(f"lo_ready{i}") for i in range(3)]
        w_used = [sem(f"w_used{i}") for i in range(3)]
        gain_in = [sem(f"gain_in{i}") for i in range(NG)]
        res_in = [sem(f"res_in{t}") for t in range(T)]
        mem_in = sem("mem_in")
        small_in = sem("small_in")
        const_ready = sem("const_ready")
        pool_step = sem("pool_step")
        dve_step = sem("dve_step")
        act_step = sem("act_step")
        xg_ready = sem("xg_ready")
        turned = sem("turned")
        rx_ready = sem("rx_ready")
        th_ready = sem("th_ready")
        tl_ready = sem("tl_ready")
        ssq_ready = sem("ssq_ready")
        res_ready = sem("res_ready")
        up_done = sem("up_done")
        sil_ready = sem("sil_ready")
        gated = sem("gated")
        h_turned = sem("h_turned")
        hh_ready = sem("hh_ready")
        hl_ready = sem("hl_ready")
        y_done = sem("y_done")
        out_ready = sem("out_ready")
        out_done = sem("out_done")
        ang_ready = sem("ang_ready")
        sin_ready = sem("sin_ready")
        kmem_ready = sem("kmem_ready")
        vmem_ready = sem("vmem_ready")
        qmem_ready = sem("qmem_ready")
        ms_done = sem("ms_done")
        ms_max = sem("ms_max")
        mp_raw = sem("mp_raw")
        mp_ready = sem("mp_ready")
        mp_turned = sem("mp_turned")
        mpt_ready = sem("mpt_ready")
        mo_done = sem("mo_done")
        mo_hi = sem("mo_hi")
        mo_lo = sem("mo_lo")
        glr_ready = sem("glr_ready")
        z_done = sem("z_done")
        zb_ready = sem("zb_ready")
        ln_ready = sem("ln_ready")
        cum_ready = sem("cum_ready")
        decay_ready = sem("decay_ready")
        k_taken = sem("k_taken")
        q_taken = sem("q_taken")
        v_ready = sem("v_ready")
        a_done = sem("a_done")
        a_taken = sem("a_taken")
        kst_turned = sem("kst_turned")
        ksk_ready = sem("ksk_ready")
        kv_done = sem("kv_done")
        s_ready = sem("s_ready")
        silr_ready = sem("silr_ready")
        o_done = sem("o_done")
        osq_ready = sem("osq_ready")
        on_ready = sem("on_ready")
        o_turned = sem("o_turned")
        oh_ready = sem("oh_ready")
        ol_ready = sem("ol_ready")
        kr_ready = sem("kr_ready")
        k_turned = sem("k_turned")
        kt_ready = sem("kt_ready")
        vs_ready = sem("vs_ready")
        qr_ready = sem("qr_ready")
        q_turned = sem("q_turned")
        qt_ready = sem("qt_ready")
        sw_done = sem("sw_done")
        sw_taken = sem("sw_taken")
        sw_max = sem("sw_max")
        wp_raw = sem("wp_raw")
        wr_ready = sem("wr_ready")
        wp_ready = sem("wp_ready")
        wp_turned = sem("wp_turned")
        wpt_ready = sem("wpt_ready")
        pv_done = sem("pv_done")

        block = ctx.enter_context(nc.Block())

        def gain_free(i):
            name = GAINS[i][0]
            if name[:4] == "post":
                return res_ready, 2 * int(name[4:])
            turn_name = {"pre": "x" + name[3:], "mem": name, "kv": "kv"}[name[:3] if name != "kv" else "kv"]
            return xg_ready, 4 * (turn_at[turn_name] + 1)

        def landings(slot, n):
            two = sum(min(max(n - b[slot], 0), NCH) for b in ffn_base) if slot < 2 else 0
            return 16 * (n + two)

        SIZE = {name: src.shape[1] * src.shape[2] for seg in (SEG_A, SEG_V, SEG_KV, SEG_B) for name, src in seg}
        NAMES = [name for seg in (SEG_A, SEG_V, SEG_KV, SEG_B) for name, _ in seg]

        def used(eng, name):
            slot, n = unit[name]
            eng.wait_ge(w_used[slot], n + 1)

        GROUPS = [(g, r, t) for g in range(2) for r in range(2) for t in range(T)]
        KEYS = [128, 192]
        HG = 4

        @block.sync
        def _(sp):
            def load(name, src):
                slot, n = unit[name]
                if n:
                    sp.wait_ge(lo_ready[slot], n)
                nk, w = src.shape[1], src.shape[2]
                dst = raw[:, slot, 0:nk * w].rearrange("p (k n) -> p k n", k=nk)
                sp.dma_start(dst, src).then_inc(landed[slot], 16)

            def ffn_loads(f):
                w_in = w_ffn_in[f // 2, f % 2].rearrange("(k p) (s n) -> p k s n", p=P, s=2)
                w_out = w_ffn_out[f // 2, f % 2].rearrange("(c p) n -> p c n", p=P)
                base = ffn_base[f]

                def up(c, h, first=False):
                    if not first:
                        sp.wait_ge(lo_ready[h], c + base[h])
                    dst = raw[:, h, :].rearrange("p (k s n) -> p k s n", k=4, s=2)
                    for s in range(2):
                        sp.dma_start(dst[:, :, s, :], w_in[:, 4 * h:4 * h + 4, s, bass.ds(c * FC, FC)])\
                          .then_inc(landed[h], 16)

                def down(c, first=False, slot=2):
                    if not first:
                        sp.wait_ge(lo_ready[slot], (c if slot else NCH) + base[slot])
                    sp.dma_start(raw[:, slot, :].rearrange("p (k n) -> p k n", k=2),
                                 w_out[:, bass.ds(c * 2, 2), :]).then_inc(landed[slot], 16)

                up(0, 0, first=f == 0)
                if f == 0:
                    sp.dma_start(res[:, 1, :], xv[:, 1, :]).then_inc(res_in[1], 16)
                up(0, 1, first=f == 0)
                up(1, 0)
                if f == 0:
                    sp.dma_start(mx, mem[0].rearrange("(t p) d -> p t d", p=P)).then_inc(mem_in, 16)
                down(0, first=f == 0)
                up(1, 1)
                with sp.Fori(2, NCH) as c:
                    up(c, 0)
                    down(c - 1)
                    up(c, 1)
                down(NCH - 1, slot=0)

            xv = x[0].rearrange("(t p) d -> p t d", p=P)
            sp.dma_start(res[:, 0, :], xv[:, 0, :]).then_inc(res_in[0], 16)
            ffn_loads(0)
            for name, src in SEG_A + SEG_V:
                if name == ("oa", 2):
                    sp.wait_ge(o_done, T)
                    sp.dma_start(mx, mem[0].rearrange("(t p) d -> p t d", p=P)).then_inc(mem_in, 16)
                load(name, src)
            ffn_loads(1)
            for name, src in SEG_KV:
                load(name, src)
            ffn_loads(2)
            for name, src in SEG_B:
                load(name, src)
            ffn_loads(3)
            ov = out[0].rearrange("(t p) d -> p t d", p=P)
            for t in range(T):
                for j in range(2):
                    sp.wait_ge(out_ready, 2 * t + j + 1)
                    at = np.s_[:, t, j * 512:(j + 1) * 512]
                    sp.dma_start(ov[at], res[at]).then_inc(out_done, 16)
            sp.wait_ge(out_done, 16 * 2 * T)

        @block.gpsimd
        def _(pool):
            count = [0]

            def link(ins):
                count[0] += 1
                ins.then_inc(pool_step, 1)
                pool.wait_ge(pool_step, count[0])

            link(pool.memset(ident[:], 0.0))
            pool.affine_select(out=ident[:], in_=ident[:], compare_op=ALU.not_equal, fill=1.0, base=0,
                               pattern=[[-1, P]], channel_multiplier=1).then_inc(const_ready, 1)
            link(pool.memset(past[:], 1.0))
            link(pool.affine_select(out=past[:], in_=past[:], compare_op=ALU.is_ge, fill=0.0, base=0,
                                    pattern=[[1, P]], channel_multiplier=-1))
            link(pool.memset(past[0:64, 64:128], 0.0))
            link(pool.memset(fut[:], 1.0))
            link(pool.affine_select(out=fut[:], in_=fut[:], compare_op=ALU.is_gt, fill=0.0, base=0,
                                    pattern=[[-1, P]], channel_multiplier=1))
            link(pool.memset(fut[64:128, 0:64], 0.0))
            link(pool.memset(band0[:], 0.0))
            link(pool.memset(band0[0:64, 64:128], NEG_INF))
            link(pool.memset(band1[:], 0.0))
            link(pool.memset(band1[0:64, 128:192], NEG_INF))
            link(pool.memset(band1[64:128, 0:64], NEG_INF))
            for i in range(HD // 2):
                pool.memset(invf[:, i:i + 1], float(inv_freq[i]))
            link(pool.memset(cmask, 1.0))
            pool.memset(cmask.rearrange("p (c j) -> p c j", j=CHUNK)[:, :, 0:1], 0.0).then_inc(const_ready, 1)

            def lo(slot, n, size=UNIT):
                pool.wait_ge(hi_ready[slot], n + 1)
                pool.tensor_tensor(w_lo[:, slot, 0:size], raw[:, slot, 0:size], w_hi[:, slot, 0:size].bitcast(F32),
                                   ALU.subtract).then_inc(lo_ready[slot], 1)

            def seg(units):
                for name, src in units:
                    lo(*unit[name], size=SIZE[name])

            def ffn(f):
                if f:
                    lo(0, ffn_base[f][0])
                lo(1, ffn_base[f][1])
                with pool.Fori(1, NCH) as c:
                    for h in range(2):
                        lo(h, c + ffn_base[f][h])

            ffn(0)
            seg(SEG_A + SEG_V)
            ffn(1)
            seg(SEG_KV)
            ffn(2)
            early = len(SEG_B) - 3
            seg(SEG_B[:early])
            for s, (g, r, t) in enumerate(GROUPS):
                pool.wait_ge(wr_ready, s + 1)
                p = wsc[s % 4].rearrange("p (h k) -> p h k", h=HG)
                pool.tensor_tensor(p, p, wsm[:, s % 4, 5, :].unsqueeze(2).to_broadcast([P, HG, KEYS[t]]),
                                   ALU.mult).then_inc(wp_ready, 1)
            seg(SEG_B[early:])
            ffn(3)

        @block.tensor
        def _(pe):
            mm = nc.tensor.matmul
            x_act, m_act = (xh, xl), (mh, ml)

            def take(slot, n):
                pe.wait_ge(lo_ready[slot], n + 1)

            def three(dst, a, b, at_a, at_b, start, stop, group=False):
                mm(dst, a[0][at_a], b[0][at_b], start=start, stop=False, skip_group_check=group)
                mm(dst, a[0][at_a], b[1][at_b], start=False, stop=False, skip_group_check=group)
                return mm(dst, a[1][at_a], b[0][at_b], start=False, stop=stop, skip_group_check=group)

            def parts(slot, k, n=UNIT):
                return tuple(w[:, slot, 0:n].rearrange("p (k n) -> p k n", k=k) for w in (w_hi, w_lo))

            def turn(name, src, t, j):
                n = piece(name, t, j)
                if n == 1:
                    pe.wait_ge(const_ready, 1)
                pe.wait_ge(xg_ready, n)
                if n > 4:
                    pe.wait_ge(tl_ready, n - 4)
                for k in range(4):
                    last = nc.tensor.transpose(ps[:, bank_of(name, t, j), k * P:(k + 1) * P],
                                               src[:, t, (4 * j + k) * P:(4 * j + k + 1) * P], ident[:])
                last.then_inc(turned, 1)

            def turned_in(name, t, j):
                pe.wait_ge(tl_ready, piece(name, t, j))

            def rowwise(name, act, turn_name, banks, between=None):
                for i in range(2):
                    if i and between is not None:
                        between()
                    slot, n = unit[(name, i)]
                    take(slot, n)
                    w = parts(slot, 4)
                    for t in range(T):
                        turned_in(turn_name, t, i)
                        for k in range(4):
                            last = three(ps[:, banks[t], :], act, w, np.s_[:, 4 * i + k, t * P:(t + 1) * P],
                                         np.s_[:, k, :], start=(i == 0 and k == 0), stop=(i == 1 and k == 3))
                    last.then_inc(w_used[slot], 1)

            def colwise(name, act, turn_name, banks):
                for i in range(2):
                    slot, n = unit[(name, i)]
                    take(slot, n)
                    w = parts(slot, 4)
                    turned_in(turn_name, T - 1, i)
                    for k in range(4):
                        for h in range(4):
                            last = three(ps[:, banks[h // 2], (h % 2) * S:(h % 2 + 1) * S], w, act,
                                         np.s_[:, k, h * P:(h + 1) * P], np.s_[:, 4 * i + k, :],
                                         start=(i == 0 and k == 0 and h % 2 == 0), stop=(i == 1 and k == 3),
                                         group=True)
                    last.then_inc(w_used[slot], 1)

            def ffn(f, filler=None, after_01=None, after_10=None, before_11=None):
                base = ffn_base[f]
                name = f"x{(0, 2, 3, 5)[f]}"

                def up(c, h):
                    take(h, c + base[h])
                    w = parts(h, 4)
                    for t in range(T):
                        if h == 0:
                            pe.wait_ge(gated, c * 2 + (2 * NCH * f - 1 + t))
                        for k in range(4):
                            last = three(ps[:, 4 + t, :], x_act, w, np.s_[:, 4 * h + k, t * P:(t + 1) * P],
                                         np.s_[:, k, :], start=(h == 0 and k == 0), stop=(h == 1 and k == 3))
                        if h == 1 and t == 0:
                            last.then_inc(up_done, 1)
                    last.then_inc(w_used[h], 1)

                def second_up():
                    pe.wait_ge(hi_ready[0], base[0] + 2)
                    w_hi_0, w_lo_0 = parts(0, 4)
                    for t in range(T):
                        pe.wait_ge(gated, 2 * NCH * f + 1 + t)
                        for k in range(4):
                            at = np.s_[:, k, t * P:(t + 1) * P]
                            mm(ps[:, 4 + t, :], xh[at], w_hi_0[:, k, :], start=(k == 0), stop=False)
                            mm(ps[:, 4 + t, :], xl[at], w_hi_0[:, k, :], start=False, stop=False)
                        if t == 0:
                            take(0, base[0] + 1)
                        for k in range(4):
                            last = mm(ps[:, 4 + t, :], xh[:, k, t * P:(t + 1) * P], w_lo_0[:, k, :],
                                      start=False, stop=False)
                    last.then_inc(w_used[0], 1)

                def first_up(h):
                    w_hi_0, w_lo_0 = parts(h, 4)
                    for t in range(T):
                        if h == 0 and t:
                            turn(name, xg, 1, 0)
                            turn(name, xg, 0, 1)
                        elif h and t == 0:
                            turn(name, xg, 1, 1)
                        dst = ps[:, 4 + t, :]
                        if t == 0:
                            pe.wait_ge(hi_ready[h], base[h] + 1)
                        pe.wait_ge(th_ready, piece(name, t, h))
                        for k in range(4):
                            mm(dst, xh[:, 4 * h + k, t * P:(t + 1) * P], w_hi_0[:, k, :],
                               start=(h == 0 and k == 0), stop=False)
                        if t == 0:
                            take(h, base[h])
                        for k in range(4):
                            mm(dst, xh[:, 4 * h + k, t * P:(t + 1) * P], w_lo_0[:, k, :], start=False, stop=False)
                        turned_in(name, t, h)
                        for k in range(4):
                            last = mm(dst, xl[:, 4 * h + k, t * P:(t + 1) * P], w_hi_0[:, k, :], start=False,
                                      stop=(h == 1 and k == 3))
                        if h == 1 and t == 0:
                            last.then_inc(up_done, 1)
                    last.then_inc(w_used[h], 1)

                def turn_h(c, b=6):
                    pe.wait_ge(gated, c * 2 + (2 * NCH * f + 2))
                    if b == 6 and (f or not isinstance(c, int) or c):
                        pe.wait_ge(hl_ready, c + NCH * f)
                    for j in range(2):
                        for t in range(T):
                            last = nc.tensor.transpose(ps[:, b, j * S + t * P:j * S + (t + 1) * P],
                                                       hid[:, t, j * P:(j + 1) * P], ident[:])
                    last.then_inc(h_turned, 1)

                def down(c, start=False, stop=False, slot=2, act=(hh, hl), between=None):
                    take(slot, (c if slot else NCH) + base[slot])
                    pe.wait_ge(hl_ready, c + (NCH * f + 1))
                    w = parts(slot, 2)
                    for t in range(T):
                        if t and between is not None:
                            between()
                        for k in range(2):
                            for n in range(2):
                                last = three(ps[:, 2 * t + n, :], act, w, np.s_[:, k, t * P:(t + 1) * P],
                                             np.s_[:, k, n * 512:(n + 1) * 512],
                                             start=(start and k == 0), stop=(stop and k == 1))
                        if stop and t == 0:
                            last.then_inc(y_done, 1)
                    last.then_inc(w_used[slot], 1)

                if filler is None:
                    turn(name, xg, 0, 0)
                else:
                    filler(lambda: turn(name, xg, 0, 0))
                first_up(0)
                first_up(1)
                if after_01 is not None:
                    after_01()
                second_up()
                if after_10 is not None:
                    after_10()
                turn_h(0)
                if before_11 is not None:
                    before_11()
                up(1, 1)
                if f in (0, 2):
                    turned_in(("mem0", None, "mem1 again")[f], 1, 1)
                down(0, start=True)
                with pe.Fori(2, NCH - 1) as c:
                    up(c, 0)
                    turn_h(c - 1)
                    up(c, 1)
                    down(c - 1)
                up(NCH - 1, 0)
                turn_h(NCH - 2)
                up(NCH - 1, 1)
                down(NCH - 2, between=lambda: turn_h(NCH - 1, 7))
                down(NCH - 1, stop=True, slot=0, act=last_h)

            def mixer_out(layer, name, first_tile, tiles, outputs, before=()):
                order = [k for k in range(first_tile, first_tile + 4, 2)] + list(range(0, tiles, 2))
                def add(i, t):
                    k0 = order[i]
                    slot, n = unit[(name, k0)]
                    w = parts(slot, 2)
                    act, at = (m_act, k0 - first_tile) if k0 >= first_tile else (x_act, k0)
                    if k0 < first_tile:
                        pe.wait_ge(ol_ready, outputs(k0, t))
                    elif layer == 0 and i == 0:
                        pe.wait_ge(mo_lo, t + 1)
                    for k in range(2):
                        for c in range(2):
                            last = three(ps[:, 2 * t + c, :], act, w, np.s_[:, at + k, t * P:(t + 1) * P],
                                         np.s_[:, k, c * 512:(c + 1) * 512],
                                         start=(i == 0 and k == 0), stop=(i == len(order) - 1 and k == 1))
                    if t == T - 1:
                        last.then_inc(w_used[slot], 1)
                    elif i == len(order) - 1:
                        last.then_inc(y_done, 1)

                for units in [(i,) for i in range(len(order) - 2)] + [(len(order) - 2, len(order) - 1)]:
                    if units[0] in before:
                        before[units[0]]()
                    for t in range(T):
                        for i in units:
                            if t == 0:
                                take(*unit[(name, order[i])])
                            add(i, t)

            def mem_scores(t, b):
                for h in range(MHEADS):
                    last = mm(ps[:, b + h // 2, (h % 2) * S:(h % 2 + 1) * S], qmem[:, h, t * P:(t + 1) * P],
                              kmem[:, h, :], start=True, stop=True)
                last.then_inc(ms_done, 1)

            def mem_turn(t, b, layer):
                pe.wait_ge(mp_ready, T * layer + t + 1)
                for j in range(T):
                    for h in range(MHEADS):
                        last = nc.tensor.transpose(ps[:, b + j, h * P:(h + 1) * P],
                                                   pm[t][:, h * S + j * P:h * S + (j + 1) * P], ident[:])
                last.then_inc(mp_turned, 1)

            def mem_out(b, layer):
                pe.wait_ge(mpt_ready, T * (layer + 1))
                for h in range(MHEADS):
                    for j in range(T):
                        last = mm(ps[:, b + h // 2, (h % 2) * S:(h % 2 + 1) * S], vmem[:, j, h * MD:(h + 1) * MD],
                                  pmt[:, j, h * S:(h + 1) * S], start=(j == 0), stop=(j == T - 1))
                    if h % 2:
                        last.then_inc(mo_done, 1)

            def turn_x(name, j):
                for t in range(T):
                    turn(name, xg, t, j)

            def gla():
                colwise("mk0", m_act, "mem0", (4, 5))

                def between():
                    turn_x("x1", 0)
                    turn_x("x1", 1)

                rowwise("mv0", m_act, "mem0", (6, 7), between)
                pe.wait_ge(kmem_ready, 1)
                slot, n = unit[("ga", 0)]
                take(slot, n)
                w = parts(slot, K, K * P)
                turned_in("x1", 1, 1)
                for k in range(K):
                    last = three(ps[:, 4, 0:S], w, x_act, np.s_[:, k, :], np.s_[:, k, :],
                                 start=(k == 0), stop=(k == K - 1))
                last.then_inc(w_used[slot], 1)
                pe.wait_ge(glr_ready, 1)
                pe.wait_ge(small_in, 16 * 5)
                for h in range(GH):
                    last = mm(ps[:, h // 2, (h % 2) * S:(h % 2 + 1) * S], wgu[:, h * DK:(h + 1) * DK], glr,
                              start=True, stop=True)
                last.then_inc(z_done, 1)
                colwise("ka", x_act, "x1", (2, 3))
                pe.wait_ge(vmem_ready, 1)
                colwise("qa", x_act, "x1", (6, 7))
                colwise("qma", x_act, "x1", (4, 5))
                pe.wait_ge(zb_ready, 1)
                rowwise("va0", x_act, "x1", (0, 1))
                pe.wait_ge(k_taken, 1)
                rowwise("va1", x_act, "x1", (2, 3))

                def scores(t):
                    if t:
                        pe.wait_ge(a_taken, t)
                    for b, keys, queries in ((6, kdn, qup), (7, kup, qdn)):
                        for h in range(GH):
                            at = np.s_[:, h * S + t * P:h * S + (t + 1) * P]
                            last = mm(ps[:, b, h * P:(h + 1) * P], keys[at], queries[at], start=True, stop=True)
                    last.then_inc(a_done, 1)

                def chunk_kv(n, b):
                    t, at = n // 2, np.s_[(n % 2) * CHUNK:(n % 2 + 1) * CHUNK]
                    for h in range(GH):
                        last = mm(ps[:, b + h // 2, (h % 2) * DV:(h % 2 + 1) * DV],
                                  ksk[at, (t * GH + h) * DK:(t * GH + h + 1) * DK], xg[at, t, h * DV:(h + 1) * DV],
                                  start=True, stop=True)
                    last.then_inc(kv_done, 1)

                pe.wait_ge(q_taken, 1)
                scores(0)
                pe.wait_ge(qmem_ready, 1)
                for t in range(T):
                    for h in range(GH):
                        last = nc.tensor.transpose(ps[:, 4 + t, h * P:(h + 1) * P],
                                                   kst[:, h * S + t * P:h * S + (t + 1) * P], ident[:])
                last.then_inc(kst_turned, 1)
                pe.wait_ge(v_ready, 1)
                rowwise("ra0", x_act, "x1", (0, 1))
                scores(1)
                pe.wait_ge(ksk_ready, 1)
                pe.wait_ge(v_ready, 2)
                chunk_kv(0, 4)
                pe.wait_ge(silr_ready, 1)
                mem_scores(0, 0)

                def between():
                    pe.wait_ge(a_taken, 2)
                    chunk_kv(1, 6)
                    pe.wait_ge(s_ready, 1)
                    chunk_kv(2, 4)
                    mem_turn(0, 0, 0)

                rowwise("ra1", x_act, "x1", (2, 3), between)
                pe.wait_ge(mpt_ready, 1)
                mem_scores(1, 0)
                for t, b in ((0, 6), (1, 4)):
                    pe.wait_ge(s_ready, t + 2)
                    for h in range(GH):
                        dst = ps[:, b + h // 2, (h % 2) * DV:(h % 2 + 1) * DV]
                        at = np.s_[:, (t * GH + h) * P:(t * GH + h + 1) * P]
                        mm(dst, am[at], xg[:, t, h * DV:(h + 1) * DV], start=True, stop=False)
                        for e in range(2):
                            if 2 * t + e:
                                last = mm(dst, qe[e][:, h * S + t * P:h * S + (t + 1) * P],
                                          state[2 * t + e][:, h * DV:(h + 1) * DV], start=False, stop=(e == 1))
                    last.then_inc(o_done, 1)
                    if t == 0:
                        mem_turn(1, 0, 0)
                pe.wait_ge(silr_ready, 2)
                mem_out(2, 0)

                def turn_o(t, b):
                    pe.wait_ge(on_ready, t + 1)
                    for k in range(K):
                        i = nc.tensor.transpose(ps[:, b + k // 4, (k % 4) * P:(k % 4 + 1) * P],
                                                gs[:, t, k * P:(k + 1) * P], ident[:])
                        if k % 4 == 3:
                            i.then_inc(o_turned, 1)

                mixer_out(0, "oa", OT_A, OT_A, lambda k, t: 2 * (t + 1),
                          {1: lambda: turn_o(0, 6), 2: lambda: turn_o(1, 4), 4: lambda: turn_memory("mem1")})

            def turn_kv():
                for t, j in PIECES:
                    turn("kv", xg, t, j)

            def narrow(name, act, turn_name, between=None):
                slot, n = unit[name]
                take(slot, n)
                turned_in(turn_name, 1, 1)
                w = parts(slot, K)
                for t in range(T):
                    if t and between is not None:
                        between()
                    for k in range(K):
                        last = three(ps[:, 7, t * S:(t + 1) * S], act, w, np.s_[:, k, t * P:(t + 1) * P],
                                     np.s_[:, k, :], start=(k == 0), stop=(k == K - 1))
                last.then_inc(w_used[slot], 1)

            def window_kv():
                pe.wait_ge(vmem_ready, 3)
                narrow(("kv", 0), m_act, "kv")
                turn_memory("mem1 again")

            def turn_memory(name):
                for t, j in PIECES:
                    turn(name, mx, t, j)

            def turn_keys():
                pe.wait_ge(kr_ready, 1)
                for g in range(2):
                    for t in range(T):
                        last = nc.tensor.transpose(ps[:, 6, g * S + t * P:g * S + (t + 1) * P],
                                                   gs[:, 0, (t * 2 + g) * P:(t * 2 + g + 1) * P], ident[:])
                last.then_inc(k_turned, 1)

            def window():
                colwise("mk1", m_act, "mem1 again", (4, 5))
                turn_keys()
                turn_x("x4", 0)
                turn_x("x4", 1)
                pe.wait_ge(kmem_ready, 2)
                colwise("qmb", x_act, "x4", (4, 5))
                rowwise("qb0", x_act, "x4", (0, 1))
                pe.wait_ge(qmem_ready, 2)
                mem_scores(0, 4)
                mem_scores(1, 2)
                pe.wait_ge(kt_ready, 1)
                rowwise("qb1", x_act, "x4", (6, 7))

                def turn_q(i, b):
                    for j in range(2):
                        for t in range(T):
                            last = nc.tensor.transpose(ps[:, b, j * S + t * P:j * S + (t + 1) * P],
                                                       gs[:, t, (i + j) * P:(i + j + 1) * P], ident[:])
                    last.then_inc(q_turned, 1)

                def scores(s):
                    g, r, t = GROUPS[s]
                    pe.wait_ge(qt_ready, 2 * g + 2)
                    if s >= 2:
                        pe.wait_ge(sw_taken, s - 1)
                    n = KEYS[t]
                    for i in range(HG):
                        at = np.s_[r * HD:(r + 1) * HD]
                        dst = ps[:, 0, i * n:(i + 1) * n] if t == 0 else ps[:, 1 + i // 2, (i % 2) * n:(i % 2 + 1) * n]
                        last = mm(dst, qt[at, (g * HG + i) * S + t * P:(g * HG + i) * S + (t + 1) * P],
                                  kt[at, g, S - n if t else 0:S if t else n], start=True, stop=True)
                    last.then_inc(sw_done, 1)

                def turn_p(s):
                    g, r, t = GROUPS[s]
                    pe.wait_ge(wp_ready, s + 1)
                    if s >= 2:
                        pe.wait_ge(wpt_ready, s - 1)
                    src = wsc[s % 4].rearrange("p (h k) -> p h k", h=HG)
                    for i in range(HG):
                        if t == 0:
                            last = nc.tensor.transpose(ps[:, 3, i * P:(i + 1) * P], src[:, i, :], ident[:])
                        else:
                            nc.tensor.transpose(ps[0:CHUNK, 4, i * P:(i + 1) * P], src[:, i, 0:CHUNK], ident[:])
                            last = nc.tensor.transpose(ps[:, 5, i * P:(i + 1) * P], src[:, i, CHUNK:], ident[:])
                    last.then_inc(wp_turned, 1)

                def weigh(s):
                    g, r, t = GROUPS[s]
                    pe.wait_ge(wpt_ready, s + 1)
                    if s >= 2:
                        pe.wait_ge(ol_ready, 4 + s - 1)
                    dst = ps[:, 6 + t, :]
                    values = vs[:, t, g].rearrange("p w d -> p (w d)")
                    if t == 0:
                        last = mm(dst, values, wpt[s % 4][0], start=True, stop=True)
                    else:
                        mm(dst, vsh[:, g].rearrange("p w d -> p (w d)"), wpt[s % 4][0], start=True, stop=False)
                        last = mm(dst, values, wpt[s % 4][1], start=False, stop=True)
                    last.then_inc(pv_done, 1)

                pe.wait_ge(qr_ready, 2)
                turn_q(0, 0)
                turn_q(2, 1)
                mem_turn(0, 4, 1)
                mem_turn(1, 2, 1)
                scores(0)
                pe.wait_ge(mpt_ready, 4)
                scores(1)
                mem_out(4, 1)
                pe.wait_ge(qr_ready, 4)
                turn_q(4, 6)
                turn_q(6, 7)
                n = len(GROUPS)
                for s in range(2, n + 2):
                    if s < n:
                        scores(s)
                    if s == 3:
                        pe.wait_ge(mo_lo, 4)
                    turn_p(s - 2)
                    if s == 3:
                        pe.wait_ge(qt_ready, 4)
                    if s >= 3:
                        weigh(s - 3)
                weigh(n - 1)
                mixer_out(1, "ob", OT_B, OT_B, lambda k, t: 4 + (4 if k < 4 else 8))

            ffn(0, after_10=lambda: turn_memory("mem0"))
            gla()
            ffn(1, lambda between: narrow(("mv1", 0), m_act, "mem1", between))
            ffn(2, lambda between: narrow(("mv1", 1), m_act, "mem1", between), after_01=turn_kv, before_11=window_kv)
            window()
            ffn(3)

        @block.scalar
        def _(act):
            act_count = [0]

            def link(ins):
                act_count[0] += 1
                ins.then_inc(act_step, 1)
                act.wait_ge(act_step, act_count[0])

            def gain(name):
                i = gain_at[name]
                if i >= NG:
                    act.wait_ge(*gain_free(i - NG))
                act.dma_start(gains[:, i % NG, :], GAINS[i][1].partition_broadcast(P)).then_inc(gain_in[i % NG], 16)

            def hi(slot, n, size=UNIT, land=None):
                act.wait_ge(landed[slot], landings(slot, n + 1) if land is None else land)
                if not isinstance(n, int) or n:
                    act.wait_ge(w_used[slot], n)
                act.activation(w_hi[:, slot, 0:size], raw[:, slot, 0:size], ACT.Copy).then_inc(hi_ready[slot], 1)

            units = iter(NAMES)

            def hi_next(count=1):
                for _ in range(count):
                    name = next(units)
                    hi(*unit[name], size=SIZE[name])

            squares = [0]

            def square(src, t, what):
                n = squares[0]
                squares[0] += 1
                if n >= 2:
                    act.wait_ge(ssq_ready, n - 1)
                act.activation(junk[n % 2], src, ACT.Square, accum_out=ssq[:, what, t:t + 1]).then_inc(ssq_ready, 1)

            def turned_hi(name, dst, pieces=PIECES):
                for t, j in pieces:
                    act.wait_ge(turned, piece(name, t, j))
                    act.activation(dst[:, 4 * j:4 * j + 4, t * P:(t + 1) * P],
                                   ps[:, bank_of(name, t, j), :].rearrange("p (k s) -> p k s", k=4),
                                   ACT.Copy).then_inc(th_ready, 1)

            def ffn_first(f, s):
                hi(s, ffn_base[f][s])

            def ffn(f, gain_names, early=None, between=None):
                base = ffn_base[f]

                def hi_f(s, c):
                    per = 32 if s < 2 else 16
                    hi(s, c + base[s], land=c * per + (landings(s, base[s]) + per))

                def silu(c):
                    for t in range(T):
                        if t == 0:
                            act.wait_ge(up_done, c + (NCH * f + 1))
                        else:
                            act.wait_ge(w_used[1], c + (base[1] + 1))
                        act.activation(sil[:, t, :], ps[:, 4 + t, 0:FC], ACT.Silu, scale=rr[:, RX, t:t + 1])\
                           .then_inc(sil_ready, 1)

                def hh_copy(c):
                    act.wait_ge(h_turned, c + (NCH * f + 1))
                    act.activation(hh[:], ps[:, 6, :].rearrange("p (k s) -> p k s", k=2), ACT.Copy)\
                       .then_inc(hh_ready, 1)

                hi_f(0, 1)
                if early is not None:
                    early()
                act.wait_ge(rx_ready, f + 1)
                silu(0)
                if f in (1, 2):
                    used(act, ("mv1", f - 1))
                    act.activation(vmem[:, :, (f - 1) * 256:f * 256], ps[:, 7, :].rearrange("p (t n) -> p t n", t=T),
                                   ACT.Copy).then_inc(vmem_ready, 1)
                hi_f(1, 1)
                if f != 2:
                    hi_f(2, 0)
                if between is not None:
                    between()
                if f == 2:
                    hi_f(2, 0)
                    turned_hi("mem1 again", mh)
                for n in gain_names:
                    gain(n)
                with act.Fori(1, NCH - 1) as c:
                    hh_copy(c - 1)
                    hi_f(0, c + 1)
                    silu(c)
                    hi_f(1, c + 1)
                    hi_f(2, c)
                hh_copy(NCH - 2)
                hi(0, NCH + base[0])
                silu(NCH - 1)
                act.wait_ge(h_turned, NCH * (f + 1))
                act.activation(last_h[0], ps[:, 7, :].rearrange("p (k s) -> p k s", k=2), ACT.Copy)\
                   .then_inc(hh_ready, 1)

            Y_LAST = [(0, ffn_base[f][0] + NCH + 1) if f is not None else None for f in (0, None, 1, 2, None, 3)]
            for m, name in ((1, ("oa", OT_A - 2)), (4, ("ob", OT_B - 2))):
                Y_LAST[m] = (unit[name][0], unit[name][1] + 1)

            def square_y(m, t):
                if t == 0:
                    act.wait_ge(y_done, m + 1)
                else:
                    slot, n = Y_LAST[m]
                    act.wait_ge(w_used[slot], n)
                square(ps[:, 2 * t:2 * t + 2, :].rearrange("p b n -> p (b n)"), t, RY)

            def square_res(m, t):
                act.wait_ge(res_ready, 2 * m + t + 1)
                square(res[:, t, :], t, RX)

            def into_ffn(f, m):
                name = f"x{(0, 2, 3, 5)[f]}"
                square_y(m, 0)
                if m == 1:
                    ffn_first(f, 0)
                square_y(m, 1)
                if m == 2:
                    ffn_first(f, 0)
                turned_hi(name, xh, PIECES[:1])
                ffn_first(f, 1)
                turned_hi(name, xh, PIECES[1:3])
                square_res(m, 0)
                turned_hi(name, xh, PIECES[3:])
                square_res(m, 1)

            def two(b):
                return ps[:, b:b + 2, :].rearrange("p b n -> p (b n)")

            def mem_exp(t, b, layer):
                act.wait_ge(ms_max, T * layer + t + 1)
                for h in range(MHEADS):
                    act.activation(pm[t][:, h * S:(h + 1) * S], ps[:, b + h // 2, (h % 2) * S:(h % 2 + 1) * S],
                                   ACT.Exp, bias=smx[:, t, h:h + 1], scale=MD ** -0.5,
                                   accum_out=smx[:, 2 + t, h:h + 1]).then_inc(mp_raw, 1)

            def mem_hi(b, layer):
                for i in range(2):
                    act.wait_ge(mo_done, 2 * layer + i + 1)
                    act.activation(mh[:, 2 * i:2 * i + 2, :], ps[:, b + i, :].rearrange("p (h s) -> p h s", h=2),
                                   ACT.Copy).then_inc(mo_hi, 1)

            def gla():
                hi_next(2)
                square_y(0, 0)
                square_y(0, 1)
                hi_next()
                square_res(0, 0)
                square_res(0, 1)
                hi_next()
                used(act, ("mk0", 1))
                act.activation(kmem[:].rearrange("p h s -> p (h s)"), two(4), ACT.Copy).then_inc(kmem_ready, 1)
                hi_next()
                turned_hi("x1", xh)
                hi_next()
                used(act, ("mv0", 1))
                act.activation(vmem[:].rearrange("p t n -> p (t n)"), two(6), ACT.Copy).then_inc(vmem_ready, 1)
                hi_next(2)
                act.wait_ge(ang_ready, 1)
                act.activation(sinw[:, :, 1, :], ang[:, 0], ACT.Sin).then_inc(sin_ready, 1)
                act.activation(cosw[:], ang[:, 1], ACT.Sin).then_inc(sin_ready, 1)
                act.wait_ge(zb_ready, 1)
                link(act.activation(sc[:, 1, :], sc[:, 1, :], ACT.Exp))
                act.activation(sc[:, 1, :], sc[:, 1, :], ACT.Ln, bias=1.0).then_inc(ln_ready, 1)
                hi_next(2)
                act.wait_ge(cum_ready, 2)
                cum = am
                act.activation(qup, qdn, ACT.Exp, scale=-1.0 / TAU).then_inc(decay_ready, 1)
                act.wait_ge(decay_ready, 1)
                act.activation(qdn, qdn, ACT.Exp, scale=1.0 / TAU).then_inc(decay_ready, 1)
                act.activation(kst, kst, ACT.Exp, scale=1.0 / TAU).then_inc(decay_ready, 1)
                act.activation(dec[:].rearrange("p h c -> p (h c)"),
                               cum.rearrange("p (c j) -> p c j", j=CHUNK)[:, :, CHUNK - 1], ACT.Exp, scale=1.0 / TAU)\
                   .then_inc(decay_ready, 1)
                act.wait_ge(decay_ready, 4)
                act.activation(cum, cum, ACT.Exp, scale=1.0 / TAU).then_inc(decay_ready, 1)
                hi_next(3)
                used(act, ("qma", 1))
                act.activation(qmem[:].rearrange("p h s -> p (h s)"), two(4), ACT.Copy).then_inc(qmem_ready, 1)
                hi_next(2)
                used(act, ("va0", 1))
                act.activation(xg[:, :, 0:512], ps[:, 0:2, :], ACT.Copy).then_inc(v_ready, 1)
                hi_next(2)
                used(act, ("va1", 1))
                act.activation(xg[:, :, 512:1024], ps[:, 2:4, :], ACT.Copy).then_inc(v_ready, 1)
                act.wait_ge(kst_turned, 1)
                act.activation(ksk, two(4), ACT.Copy).then_inc(ksk_ready, 1)
                hi_next(2)
                used(act, ("ra0", 1))
                act.activation(gs[:, :, 0:512], ps[:, 0:2, :], ACT.Silu).then_inc(silr_ready, 1)
                hi_next()
                mem_exp(0, 0, 0)
                hi_next()
                act.wait_ge(mp_turned, 1)
                act.activation(pmt.rearrange("p j (h s) -> p j h s", h=MHEADS)[:, :, :, 0:P],
                               ps[:, 0:2, :].rearrange("p j (h s) -> p j h s", h=MHEADS), ACT.Copy).then_inc(mpt_ready, 1)
                used(act, ("ra1", 1))
                act.activation(gs[:, :, 512:1024], ps[:, 2:4, :], ACT.Silu).then_inc(silr_ready, 1)
                mem_exp(1, 0, 0)
                for t, b in ((0, 6), (1, 4)):
                    act.wait_ge(o_done, t + 1)
                    for h in range(GH):
                        n = t * GH + h
                        if n >= 2:
                            act.wait_ge(osq_ready, n - 1)
                        act.activation(kt[:, h % 2, :], ps[:, b + h // 2, (h % 2) * DV:(h % 2 + 1) * DV], ACT.Square,
                                       accum_out=ssg[:, t * GH + h:t * GH + h + 1]).then_inc(osq_ready, 1)
                hi_next()
                gain("mem1")
                gain("post2")
                gain("pre2")
                mem_hi(2, 0)
                for t, b in ((0, 6), (1, 4)):
                    for j in range(2):
                        act.wait_ge(o_turned, 2 * t + j + 1)
                        act.activation(xh[:, 4 * j:4 * j + 4, t * P:(t + 1) * P],
                                       ps[:, b + j, :].rearrange("p (k s) -> p k s", k=4), ACT.Copy)\
                           .then_inc(oh_ready, 1)
                    if t == 0:
                        hi_next()
                hi_next(2)
                turned_hi("mem1", mh)
                hi_next()

            def window():
                hi_next(2)
                square_y(3, 0)
                square_y(3, 1)
                hi_next()
                square_res(3, 0)
                square_res(3, 1)
                hi_next()
                used(act, ("mk1", 1))
                act.activation(kmem[:].rearrange("p h s -> p (h s)"), two(4), ACT.Copy).then_inc(kmem_ready, 1)
                hi_next()
                act.wait_ge(k_turned, 1)
                act.activation(kt[:].rearrange("p g s -> p (g s)"), ps[:, 6, :], ACT.Copy).then_inc(kt_ready, 1)
                turned_hi("x4", xh)
                hi_next()
                used(act, ("qmb", 1))
                act.activation(qmem[:].rearrange("p h s -> p (h s)"), two(4), ACT.Copy).then_inc(qmem_ready, 1)
                hi_next(2)
                hi_next()
                gain("post5")
                gain("pre5")
                mem_exp(0, 4, 1)
                mem_exp(1, 2, 1)
                hi_next(2)

                def copy_q(i, b):
                    act.wait_ge(q_turned, i + 1)
                    act.activation(qt[:, i * 512:(i + 1) * 512], ps[:, b, :], ACT.Copy).then_inc(qt_ready, 1)

                def exps(s):
                    m = wsm[:, s % 4]
                    act.wait_ge(sw_max, s + 1)
                    for i in range(HG):
                        row = wsc[s % 4].rearrange("p (h k) -> p h k", h=HG)[:, i, :]
                        act.activation(row, row, ACT.Exp, bias=m[:, 1, i:i + 1],
                                       accum_out=m[:, 2, i:i + 1]).then_inc(wp_raw, 1)
                    act.activation(m[:, 3, :], m[:, 3, :], ACT.Exp).then_inc(wp_raw, 1)

                def copy_p(s):
                    g, r, t = GROUPS[s]
                    act.wait_ge(wp_turned, s + 1)
                    if t == 0:
                        act.activation(wpt[s % 4][0], ps[:, 3, :], ACT.Copy).then_inc(wpt_ready, 1)
                    else:
                        act.activation(wpt[s % 4][0], ps[0:CHUNK, 4, :], ACT.Copy)
                        act.activation(wpt[s % 4][1], ps[:, 5, :], ACT.Copy).then_inc(wpt_ready, 1)

                def output_hi(s):
                    g, r, t = GROUPS[s]
                    rows = np.s_[r * HD:(r + 1) * HD]
                    act.wait_ge(pv_done, s + 1)
                    act.activation(xh[rows, 4 * g:4 * g + 4, t * P:(t + 1) * P],
                                   ps[rows, 6 + t, :].rearrange("p (h s) -> p h s", h=HG), ACT.Copy)\
                       .then_inc(oh_ready, 1)

                copy_q(0, 0)
                copy_q(1, 1)
                act.wait_ge(mp_turned, 3)
                act.activation(pmt.rearrange("p j (h s) -> p j h s", h=MHEADS)[:, :, :, 0:P],
                               ps[:, 4:6, :].rearrange("p j (h s) -> p j h s", h=MHEADS), ACT.Copy).then_inc(mpt_ready, 1)
                exps(0)
                mem_hi(4, 1)
                exps(1)
                copy_q(2, 6)
                copy_q(3, 7)
                n = len(GROUPS)
                for s in range(2, n + 2):
                    if s == 2:
                        exps(s)
                    copy_p(s - 2)
                    if 2 < s < n:
                        exps(s)
                    if s >= 3:
                        output_hi(s - 3)
                output_hi(n - 1)
                hi_next(3)
                ffn_first(3, 0)

            gain("pre0")
            act.wait_ge(res_in[0], 16)
            square(res[:, 0, :], 0, RX)
            turned_hi("x0", xh, PIECES[:1])
            ffn_first(0, 0)
            act.wait_ge(res_in[1], 16)
            square(res[:, 1, :], 1, RX)
            gain("mem0")
            ffn_first(0, 1)
            act.dma_start(wgu[:], w_gate_up[0]).then_inc(small_in, 16)
            with nc.allow_non_contiguous_dma("one gate bias and two positions a partition"):
                act.dma_start(bg[:], b_gate[0].rearrange("(h p) -> p h", p=P)).then_inc(small_in, 16)
                act.dma_start(posi[:], positions[0].rearrange("(t p) -> p t", p=P)).then_inc(small_in, 16)
            act.dma_start(sink[:], sinks[0:1, :].partition_broadcast(P)).then_inc(small_in, 16)
            act.dma_start(glag[:], gla_norm_g[0:1, :].partition_broadcast(P)).then_inc(small_in, 16)
            gain("post1")
            gain("pre1")
            turned_hi("x0", xh, PIECES[1:])
            def square_memory():
                act.wait_ge(mem_in, 16)
                for t in range(T):
                    square(mx[:, t, :], t, RM)

            ffn(0, [], square_memory, lambda: turned_hi("mem0", mh))
            gla()
            into_ffn(1, 1)
            ffn(1, ["post3", "pre3", "kv"])
            hi_next(2)
            into_ffn(2, 2)

            def kv():
                turned_hi("kv", mh)

            ffn(2, ["post4", "pre4"], between=kv)
            window()
            into_ffn(3, 4)
            ffn(3, ["post6"])
            square_y(5, 0)
            square_y(5, 1)

        @block.vector
        def _(dve):
            dve_count = [0]

            def link(ins):
                dve_count[0] += 1
                ins.then_inc(dve_step, 1)
                dve.wait_ge(dve_step, dve_count[0])

            def rsqrt(dst, src, n, scale):
                half, y, t, u = (nw[:, i, 0:n] for i in range(4))
                link(dve.tensor_scalar(half, src, 0.5 * scale, 0.5 * EPS, ALU.mult, ALU.add))
                link(dve.tensor_scalar(t.bitcast(I32), half.bitcast(I32), 1, None, ALU.logical_shift_right))
                link(dve.tensor_scalar(y.bitcast(I32), t.bitcast(I32), -1.0,
                                       float(RSQRT_MAGIC - 2 ** 22 - 2 ** 31), ALU.mult, ALU.add))
                for i in range(3):
                    if n == 1:
                        link(dve.scalar_tensor_tensor(out=u, in0=y, scalar=y, in1=half, op0=ALU.mult, op1=ALU.mult))
                    else:
                        link(dve.tensor_tensor(t, y, y, ALU.mult))
                        link(dve.tensor_tensor(u, t, half, ALU.mult))
                    link(dve.scalar_tensor_tensor(out=dst if i == 2 else y, in0=u, scalar=1.5, in1=y,
                                                  op0=ALU.subtract, op1=ALU.mult))

            def gain(name):
                i = gain_at[name]
                dve.wait_ge(gain_in[i % NG], 16 * (i // NG + 1))
                return gains[:, i % NG, :]

            def turned_lo(name, lead, dst, pieces=PIECES):
                for t, j in pieces:
                    dve.wait_ge(th_ready, piece(name, t, j))
                    at = np.s_[:, 4 * j:4 * j + 4, t * P:(t + 1) * P]
                    dve.tensor_tensor(dst[at], ps[:, bank_of(name, t, j), :].rearrange("p (k s) -> p k s", k=4),
                                      lead[at].bitcast(F32), ALU.subtract).then_inc(tl_ready, 1)

            def lo(slot, n):
                dve.wait_ge(hi_ready[slot], n + 1)
                dve.tensor_tensor(w_lo[:, slot, :], raw[:, slot, :], w_hi[:, slot, :].bitcast(F32),
                                  ALU.subtract).then_inc(lo_ready[slot], 1)

            def ffn(f, between=None, after_20=None):
                base = ffn_base[f]

                def gate(c):
                    for t in range(T):
                        dve.wait_ge(sil_ready, c * 2 + (2 * NCH * f + t + 1))
                        dve.scalar_tensor_tensor(out=hid[:, t, :], in0=ps[:, 4 + t, FC:2 * FC],
                                                 scalar=rr[:, RX, t:t + 1], in1=sil[:, t, :],
                                                 op0=ALU.mult, op1=ALU.mult).then_inc(gated, 1)

                def hl_sub(c):
                    dve.wait_ge(hh_ready, c + (NCH * f + 1))
                    dve.tensor_tensor(hl[:], ps[:, 6, :].rearrange("p (k s) -> p k s", k=2), hh[:].bitcast(F32),
                                      ALU.subtract).then_inc(hl_ready, 1)

                gate(0)
                if between is not None:
                    between()
                lo(2, base[2])
                if after_20 is not None:
                    after_20()
                with dve.Fori(1, NCH - 1) as c:
                    hl_sub(c - 1)
                    gate(c)
                    lo(2, c + base[2])
                hl_sub(NCH - 2)
                lo(0, NCH + base[0])
                gate(NCH - 1)
                dve.wait_ge(hh_ready, NCH * (f + 1))
                dve.tensor_tensor(last_h[1], ps[:, 7, :].rearrange("p (k s) -> p k s", k=2), last_h[0].bitcast(F32),
                                  ALU.subtract).then_inc(hl_ready, 1)

            squared = [0]

            def root(what, t=None, n=1):
                squared[0] += n
                dve.wait_ge(ssq_ready, squared[0])
                tiles = slice(0, T) if t is None else slice(t, t + 1)
                rsqrt(rr[:, what, tiles], ssq[:, what, tiles], T if t is None else 1, 1.0 / D)

            def update(m, weight, t, j):
                at = np.s_[:, t, j * 512:(j + 1) * 512]
                link(dve.scalar_tensor_tensor(out=xg[at], in0=ps[:, 2 * t + j, :], scalar=rr[:, RY, t:t + 1],
                                              in1=gain(f"post{m + 1}")[:, j * 512:(j + 1) * 512],
                                              op0=ALU.mult, op1=ALU.mult))
                last = dve.scalar_tensor_tensor(out=res[at], in0=xg[at], scalar=weight, in1=res[at],
                                                op0=ALU.mult, op1=ALU.add)
                if m == 5:
                    last.then_inc(out_ready, 1)
                elif j:
                    last.then_inc(res_ready, 1)
                    dve.wait_ge(res_ready, 2 * m + t + 1)
                else:
                    link(last)

            def pre(name, t, j):
                at = np.s_[:, t, j * 512:(j + 1) * 512]
                g = gain("kv" if name == "kv" else "pre" + name[1:])
                dve.tensor_tensor(xg[at], res[at], g[:, j * 512:(j + 1) * 512], ALU.mult).then_inc(xg_ready, 1)

            def into_ffn(f, m, weight):
                name = f"x{(0, 2, 3, 5)[f]}"
                done = 0
                for t, j in PIECES:
                    if j == 0:
                        root(RY, t)
                    update(m, weight, t, j)
                    pre(name, t, j)
                    if (t, j) != PIECES[0]:
                        turned_lo(name, xh, xl, PIECES[done:done + 1])
                        done += 1
                turned_lo(name, xh, xl, PIECES[done:])
                factor()

            def factor():
                root(RX, n=T)
                dve.engine_nop().then_inc(rx_ready, 1)

            def normed(what, dst, src, g):
                for t, j in PIECES:
                    at = np.s_[:, t, j * 512:(j + 1) * 512]
                    dve.scalar_tensor_tensor(out=dst[at], in0=src[at], scalar=rr[:, what, t:t + 1],
                                             in1=g[:, j * 512:(j + 1) * 512],
                                             op0=ALU.mult, op1=ALU.mult).then_inc(xg_ready, 1)

            def into_mixer(m, pre_name):
                for t in range(T):
                    root(RY, t)
                    for j in range(2):
                        update(m, 0.5, t, j)
                root(RX, n=T)
                normed(RX, xg, res, gain(pre_name))

            def mem_normed(layer):
                dve.wait_ge(mem_in, 16 * (layer + 1))
                normed(RM, mx, mx, gain(f"mem{layer}"))

            def two(b):
                return ps[:, b:b + 2, :].rearrange("p b n -> p (b n)")

            def heads(ap, h):
                return ap.rearrange("p (h s) -> p h s", h=h)

            def rotate(dst, src, t, heads_n, tmp):
                half = HD // 2
                c = cosw[:, t, :].unsqueeze(1).unsqueeze(1).to_broadcast([P, heads_n, 2, half])
                s = [sinw[:, t, i, :].unsqueeze(1).to_broadcast([P, heads_n, half]) for i in range(2)]
                dve.tensor_tensor(tmp[:, :, 0, :], src[:, :, 1, :], s[0], ALU.mult)
                dve.tensor_tensor(tmp[:, :, 1, :], src[:, :, 0, :], s[1], ALU.mult)
                link(dve.tensor_tensor(dst, src, c, ALU.mult))
                return dve.tensor_tensor(dst, dst, tmp, ALU.add)

            def mem_maxima(t, b, layer):
                dve.wait_ge(ms_done, T * layer + t + 1)
                link(dve.tensor_reduce(smx[:, 6, 4 * t:4 * t + MHEADS], heads(two(b), MHEADS), AX.X, ALU.max))
                dve.tensor_scalar(smx[:, t, 0:MHEADS], smx[:, 6, 4 * t:4 * t + MHEADS], -MD ** -0.5, None, ALU.mult)\
                   .then_inc(ms_max, 1)

            def mem_probs(t, layer):
                dve.wait_ge(mp_raw, MHEADS * (T * layer + t + 1))
                link(dve.reciprocal(smx[:, 7, 4 * t:4 * t + MHEADS], smx[:, 2 + t, 0:MHEADS]))
                dve.tensor_tensor(heads(pm[t], MHEADS), heads(pm[t], MHEADS),
                                  smx[:, 7, 4 * t:4 * t + MHEADS].unsqueeze(2).to_broadcast([P, MHEADS, S]), ALU.mult)\
                   .then_inc(mp_ready, 1)

            def mem_turned(b, layer):
                dve.wait_ge(mp_turned, T * layer + 2)
                dve.tensor_copy(pmt.rearrange("p j (h s) -> p j h s", h=MHEADS)[:, :, :, P:2 * P],
                                ps[:, b:b + 2, :].rearrange("p j (h s) -> p j h s", h=MHEADS)).then_inc(mpt_ready, 1)

            def mem_lo(b, layer):
                for i in range(2):
                    dve.wait_ge(mo_hi, 2 * layer + i + 1)
                    dve.tensor_tensor(ml[:, 2 * i:2 * i + 2, :], heads(ps[:, b + i, :], 2),
                                      mh[:, 2 * i:2 * i + 2, :].bitcast(F32), ALU.subtract).then_inc(mo_lo, 1)

            def gla():
                used(dve, ("ga", 0))
                dve.tensor_copy(glr, ps[0:RANK, 4, 0:S]).then_inc(glr_ready, 1)
                dve.wait_ge(z_done, 1)
                z, nab, cum = kst, sc[:, 1, :], am
                for h in range(GH):
                    link(dve.tensor_scalar(z[:, h * S:(h + 1) * S], ps[:, h // 2, (h % 2) * S:(h % 2 + 1) * S],
                                           bg[:, h:h + 1], None, ALU.add))
                dve.scalar_tensor_tensor(out=nab, in0=z, scalar=-1.0, in1=z, op0=ALU.mult, op1=ALU.min)\
                   .then_inc(zb_ready, 1)
                for e in range(2):
                    dve.memset(qe[e], 0.0)
                dve.wait_ge(ln_ready, 1)
                link(dve.scalar_tensor_tensor(out=z, in0=z, scalar=0.0, in1=nab, op0=ALU.min, op1=ALU.subtract))
                link(dve.tensor_tensor_scan(cum, cmask, z, 0.0, ALU.mult, ALU.add))
                cv = cum.rearrange("p (c j) -> p c j", j=CHUNK)
                total = cv[:, :, CHUNK - 1:CHUNK].to_broadcast([P, GH * 4, CHUNK])
                dve.scalar_tensor_tensor(out=qdn.rearrange("p (c j) -> p c j", j=CHUNK), in0=total, scalar=0.5,
                                         in1=cv, op0=ALU.mult, op1=ALU.subtract).then_inc(cum_ready, 1)
                dve.tensor_tensor(kst.rearrange("p (c j) -> p c j", j=CHUNK), total, cv, ALU.subtract)\
                   .then_inc(cum_ready, 1)
                dve.wait_ge(decay_ready, 3)
                used(dve, ("ka", 1))
                dve.tensor_tensor(kdn, two(2), qdn, ALU.mult)
                dve.tensor_tensor(kup, two(2), qup, ALU.mult)
                link(dve.tensor_tensor(kst, two(2), kst, ALU.mult))
                dve.engine_nop().then_inc(k_taken, 1)
                dve.wait_ge(decay_ready, 5)
                used(dve, ("qa", 1))
                for e in range(2):
                    at = np.s_[:, :, e * CHUNK:(e + 1) * CHUNK]
                    link(dve.scalar_tensor_tensor(out=qe[e].rearrange("p (x j) -> p x j", j=P)[at],
                                                  in0=two(6).rearrange("p (x j) -> p x j", j=P)[at], scalar=DK ** -0.5,
                                                  in1=cum.rearrange("p (x j) -> p x j", j=P)[at],
                                                  op0=ALU.mult, op1=ALU.mult))
                dve.scalar_tensor_tensor(out=qdn, in0=two(6), scalar=DK ** -0.5, in1=qdn, op0=ALU.mult, op1=ALU.mult)
                link(dve.memset(am, 0.0))
                dve.scalar_tensor_tensor(out=qup, in0=two(6), scalar=DK ** -0.5, in1=qup, op0=ALU.mult, op1=ALU.mult)\
                   .then_inc(q_taken, 1)

                def take_scores(t):
                    dve.wait_ge(a_done, t + 1)
                    dst = heads(am[:, t * GH * P:(t + 1) * GH * P], GH)
                    for b, mask in ((6, past), (7, fut)):
                        link(dve.copy_predicated(dst, mask[:].bitcast(I32).unsqueeze(1).to_broadcast([P, GH, P]),
                                                 heads(ps[:, b, :], GH)))
                    dve.engine_nop().then_inc(a_taken, 1)

                take_scores(0)
                take_scores(1)
                dve.wait_ge(kv_done, 1)
                dve.tensor_copy(state[1], two(4)).then_inc(s_ready, 1)
                dve.wait_ge(s_ready, 1)

                def next_state(n, b):
                    dve.wait_ge(kv_done, n + 1)
                    for h in range(GH):
                        at = np.s_[:, h * DV:(h + 1) * DV]
                        last = dve.scalar_tensor_tensor(out=state[n + 1][at], in0=state[n][at],
                                                        scalar=dec[:, h, n:n + 1], in1=two(b)[at],
                                                        op0=ALU.mult, op1=ALU.add)
                        if h < GH - 1:
                            link(last)
                    last.then_inc(s_ready, 1)
                    dve.wait_ge(s_ready, n + 1)

                def gate_gain(i):
                    dve.wait_ge(silr_ready, i + 1)
                    for t in range(T):
                        link(dve.tensor_tensor(heads(gs[:, t, i * 512:(i + 1) * 512], 2),
                                               heads(gs[:, t, i * 512:(i + 1) * 512], 2),
                                               glag[:].unsqueeze(1).to_broadcast([P, 2, DV]), ALU.mult))

                def gate_output(t, b):
                    for h in range(GH):
                        at = np.s_[:, h * DV:(h + 1) * DV]
                        last = dve.scalar_tensor_tensor(out=gs[:, t, :][at], in0=two(b)[at],
                                                        scalar=rsg[:, t * GH + h:t * GH + h + 1], in1=gs[:, t, :][at],
                                                        op0=ALU.mult, op1=ALU.mult)
                        if h < GH - 1:
                            link(last)
                    last.then_inc(on_ready, 1)

                mem_maxima(0, 0, 0)
                gate_gain(0)
                mem_probs(0, 0)
                next_state(1, 6)
                next_state(2, 4)
                mem_maxima(1, 0, 0)
                gate_gain(1)
                mem_probs(1, 0)
                mem_turned(0, 0)
                dve.wait_ge(osq_ready, T * GH)
                rsqrt(rsg[:], ssg[:], T * GH, 1.0 / DV)
                mem_lo(2, 0)
                gate_output(0, 6)
                gate_output(1, 4)
                for t, b in ((0, 6), (1, 4)):
                    for j in range(2):
                        dve.wait_ge(oh_ready, 2 * t + j + 1)
                        at = np.s_[:, 4 * j:4 * j + 4, t * P:(t + 1) * P]
                        dve.tensor_tensor(xl[at], ps[:, b + j, :].rearrange("p (k s) -> p k s", k=4),
                                          xh[at].bitcast(F32), ALU.subtract).then_inc(ol_ready, 1)

            def window_kv():
                used(dve, ("kv", 0))
                for t in range(T):
                    src = ps[:, 7, t * S:(t + 1) * S]
                    link(dve.tensor_scalar(kw[:, t * 2 * HD:(t + 1) * 2 * HD], src[:, 0:2 * HD], rr[:, RX, t:t + 1],
                                           None, ALU.mult))
                    for twice in range(2):
                        dve.tensor_scalar(vs[:, t, :, twice, :],
                                          src[:, 2 * HD:4 * HD].rearrange("p (g d) -> p g d", g=2),
                                          rr[:, RX, t:t + 1], None, ALU.mult).then_inc(vs_ready, 1)

            def rotate_keys():
                dve.wait_ge(sin_ready, 2)
                link(dve.tensor_scalar(sinw[:, :, 0, :], sinw[:, :, 1, :], -1.0, None, ALU.mult))
                v = "p (h a j) -> p h a j"
                for t in range(T):
                    rotated = kw[:, 256 + t * 2 * HD:256 + (t + 1) * 2 * HD]
                    link(rotate(rotated.rearrange(v, h=2, a=2),
                                kw[:, t * 2 * HD:(t + 1) * 2 * HD].rearrange(v, h=2, a=2), t, 2,
                                kw[:, 512 + t * 2 * HD:512 + (t + 1) * 2 * HD].rearrange(v, h=2, a=2)))
                    for twice in range(2):
                        link(dve.tensor_copy(gs[:, 0, t * 2 * P:(t + 1) * 2 * P]
                                             .rearrange("p (h w d) -> p h w d", h=2, w=2)[:, :, twice, :],
                                             rotated.rearrange("p (h d) -> p h d", h=2)))
                dve.engine_nop().then_inc(kr_ready, 1)
                dve.wait_ge(vs_ready, 4)
                dve.tensor_copy(vsh, vs[64:128, 0]).then_inc(vs_ready, 1)

            def window():
                dve.wait_ge(sin_ready, 2)

                def rotate_q(i):
                    half, t = i // 2, i % 2
                    used(dve, (f"qb{half}", 1))
                    v = "p (h a j) -> p h a j"
                    rotate(gs[:, t, half * 512:(half + 1) * 512].rearrange(v, h=8, a=2),
                           ps[:, 6 * half + t, :].rearrange(v, h=8, a=2), t, 8,
                           sc[:, t * 6, 0:512].rearrange(v, h=8, a=2)).then_inc(qr_ready, 1)

                def take_scores(s):
                    g, r, t = GROUPS[s]
                    n, m = KEYS[t], wsm[:, s % 4]
                    dve.wait_ge(sw_done, s + 1)
                    if s >= 4:
                        dve.wait_ge(wp_turned, s - 3)
                    dst = wsc[s % 4].rearrange("p (h k) -> p h k", h=HG)
                    mask = (band0, band1)[t]
                    if t == 0:
                        link(dve.scalar_tensor_tensor(out=dst, in0=heads(ps[:, 0, :], HG), scalar=HD ** -0.5,
                                                      in1=mask[:].unsqueeze(1).to_broadcast([P, HG, n]),
                                                      op0=ALU.mult, op1=ALU.add))
                    else:
                        for j in range(2):
                            link(dve.scalar_tensor_tensor(out=dst[:, 2 * j:2 * j + 2, :],
                                                          in0=heads(ps[:, 1 + j, 0:2 * n], 2), scalar=HD ** -0.5,
                                                          in1=mask[:].unsqueeze(1).to_broadcast([P, 2, n]),
                                                          op0=ALU.mult, op1=ALU.add))
                    dve.engine_nop().then_inc(sw_taken, 1)
                    own, negated = (v[:].rearrange("p (g i r) -> p g i r", g=2, r=2)[:, g, :, r] for v in (sink, nsink))
                    link(dve.tensor_reduce(m[:, 0, :], dst, AX.X, ALU.max))
                    link(dve.scalar_tensor_tensor(out=m[:, 1, :], in0=m[:, 0, :], scalar=-1.0,
                                                  in1=negated, op0=ALU.mult, op1=ALU.min))
                    dve.tensor_tensor(m[:, 3, :], own, m[:, 1, :], ALU.add).then_inc(sw_max, 1)

                def reciprocals(s):
                    m = wsm[:, s % 4]
                    dve.wait_ge(wp_raw, (HG + 1) * (s + 1))
                    link(dve.tensor_tensor(m[:, 4, :], m[:, 2, :], m[:, 3, :], ALU.add))
                    dve.reciprocal(m[:, 5, :], m[:, 4, :]).then_inc(wr_ready, 1)

                def output_lo(s):
                    g, r, t = GROUPS[s]
                    at = np.s_[r * HD:(r + 1) * HD, 4 * g:4 * g + 4, t * P:(t + 1) * P]
                    dve.wait_ge(oh_ready, 4 + s + 1)
                    dve.tensor_tensor(xl[at], heads(ps[r * HD:(r + 1) * HD, 6 + t, :], HG), xh[at].bitcast(F32),
                                      ALU.subtract).then_inc(ol_ready, 1)

                link(dve.tensor_scalar(nsink[:], sink[:], -1.0, None, ALU.mult))
                mem_maxima(0, 4, 1)
                mem_maxima(1, 2, 1)
                rotate_q(0)
                rotate_q(1)
                mem_probs(0, 1)
                mem_probs(1, 1)
                rotate_q(2)
                mem_turned(2, 1)
                take_scores(0)
                rotate_q(3)
                dve.wait_ge(qr_ready, 4)
                take_scores(1)
                reciprocals(0)
                mem_lo(4, 1)
                n = len(GROUPS)
                for s in range(2, n + 3):
                    if s < n:
                        take_scores(s)
                    if s <= n:
                        reciprocals(s - 1)
                    if s >= 4:
                        output_lo(s - 4)
                output_lo(n - 1)

            def angles():
                dve.wait_ge(small_in, 16 * 5)
                dve.wait_ge(const_ready, 2)
                link(dve.tensor_copy(posf[:], posi[:]))
                flat = [ang[:, i].rearrange("p t j -> p (t j)") for i in range(4)]
                a, k, kh, kl = flat
                for t in range(T):
                    link(dve.tensor_scalar(ang[:, 0, t, :], invf[:], posf[:, t:t + 1], None, ALU.mult))
                link(dve.tensor_scalar(k, a, 1.0 / TWO_PI, None, ALU.mult))
                big = 1.5 * 2.0 ** 23
                link(dve.tensor_scalar(k, k, big, None, ALU.add))
                link(dve.tensor_scalar(k, k, -big, None, ALU.add))
                link(dve.tensor_scalar(kh, k, big * 4096.0, None, ALU.add))
                link(dve.tensor_scalar(kh, kh, -big * 4096.0, None, ALU.add))
                link(dve.tensor_tensor(kl, k, kh, ALU.subtract))
                for part in parts_of(TWO_PI, 12, 4):
                    for n in (kh, kl):
                        link(dve.scalar_tensor_tensor(out=a, in0=n, scalar=-part, in1=a, op0=ALU.mult, op1=ALU.add))
                link(dve.tensor_scalar(a, a, PI_BELOW, -PI_BELOW, ALU.min, ALU.max))
                link(dve.scalar_tensor_tensor(out=k, in0=a, scalar=-1.0, in1=a, op0=ALU.mult, op1=ALU.min))
                dve.tensor_scalar(k, k, float(np.pi / 2), None, ALU.add).then_inc(ang_ready, 1)

            dve.wait_ge(res_in[0], 16)
            pre("x0", 0, 0)
            turned_lo("x0", xh, xl, PIECES[:1])
            lo(0, ffn_base[0][0])
            dve.wait_ge(res_in[1], 16)
            for t, j in PIECES[1:]:
                pre("x0", t, j)
            turned_lo("x0", xh, xl, PIECES[1:])
            factor()

            def first_memory():
                root(RM, n=T)
                mem_normed(0)
                turned_lo("mem0", mh, ml)

            ffn(0, between=first_memory)
            into_mixer(0, "pre1")
            turned_lo("x1", xh, xl)
            angles()
            gla()
            mem_normed(1)
            turned_lo("mem1", mh, ml)
            into_ffn(1, 1, 1.0)
            ffn(1)
            into_ffn(2, 2, 0.5)
            for t, j in PIECES:
                dve.wait_ge(turned, piece("x3", t, j))
                pre("kv", t, j)

            def kv():
                turned_lo("kv", mh, ml)
                for _ in PIECES:
                    dve.engine_nop().then_inc(xg_ready, 1)
                window_kv()

            ffn(2, kv, lambda: turned_lo("mem1 again", mh, ml))
            rotate_keys()
            into_mixer(3, "pre4")
            turned_lo("x4", xh, xl)
            window()
            into_ffn(3, 4, 1.0)
            ffn(3)
            for t in range(T):
                root(RY, t)
                for j in range(2):
                    update(5, 0.5, t, j)


_INS = ["x", "mem", "positions", "norm_g", "w_ffn_in", "w_ffn_out", "mem_norm_g", "w_mem_kv", "w_in_a",
        "w_gate_up", "b_gate", "gla_norm_g", "w_out_a", "kv_norm_g", "w_kv", "w_in_b", "sinks", "w_out_b"]


def kernel(**inputs):
    import numpy as _np
    import concourse.bacc as _bacc
    from concourse import mybir as _mybir
    from concourse.bass_utils import run_bass_kernel_spmd as _run

    nc = _bacc.Bacc("TRN2", target_bir_lowering=False, num_devices=1)
    arrays, args = {}, []
    for name in _INS:
        a = _np.ascontiguousarray(inputs[name])
        arrays[f"in_{name}"] = a
        args.append(nc.dram_tensor(f"in_{name}", a.shape, _mybir.dt.from_np(a.dtype), kind="ExternalInput").ap())
    args.append(nc.dram_tensor("out_0", inputs["x"].shape, F32, kind="ExternalOutput").ap())
    hybrid_kernel(nc, *args)
    r = _run(nc, [arrays], core_ids=[0])
    return r.results[0]["out_0"]
```
